# Optimizing a Trainium2 kernel written in Bass

```python
import math
import jax
import jax.numpy as jnp
from jax import lax
import numpy as np
import jax, jax.numpy as jnp

D_MODEL = 1024
BATCH = 1
SEQ = 256
DEPTH = 2

CHUNK = 64
Q_BLOCK = 128
ROPE_THETA = 500000.0
HEAD_DIM = 64

MLA_HEADS = 8
DIFF_HEADS = 4
FOX_HEADS = 4
D_MIX = (MLA_HEADS + DIFF_HEADS + FOX_HEADS) * HEAD_DIM

MLA_Q_RANK = 384
MLA_KV_RANK = 256
MLA_NOPE = 64
MLA_ROPE = 32
MLA_V = HEAD_DIM

DIFF_QK = HEAD_DIM // 2
DIFF_V = HEAD_DIM
DIFF_ROT = DIFF_QK // 4
DIFF_W = DIFF_HEADS * HEAD_DIM

FOX_W = FOX_HEADS * HEAD_DIM

IN_SPLITS = (MLA_Q_RANK, MLA_KV_RANK, MLA_ROPE,
             DIFF_W, DIFF_W, DIFF_W,
             FOX_W, FOX_W, FOX_W, FOX_HEADS)
IN_COLS = MLA_Q_RANK + MLA_KV_RANK + MLA_ROPE + 3 * DIFF_W + 3 * FOX_W + FOX_HEADS

N_EXPERTS = 16
N_GROUPS = 4
GROUP_SIZE = N_EXPERTS // N_GROUPS
TOP_K = 2
D_EXPERT = 512

DEEPNORM_ALPHA = (2 * DEPTH) ** 0.25
DEEPNORM_BETA = (8 * DEPTH) ** -0.25

LN_EPS = 1e-5
RMS_EPS = 1e-6
NEG_INF = -1e30
F32 = jnp.float32


def layer_norm(x, g, b):
    xf = x.astype(F32)
    mu = jnp.mean(xf, axis=-1, keepdims=True)
    var = jnp.mean(jnp.square(xf - mu), axis=-1, keepdims=True)
    return ((xf - mu) * lax.rsqrt(var + LN_EPS) * g.astype(F32) + b.astype(F32)).astype(x.dtype)

def rms_norm(x, g):
    xf = x.astype(F32)
    return (xf * lax.rsqrt(jnp.mean(xf * xf, axis=-1, keepdims=True) + RMS_EPS) * g.astype(F32)).astype(x.dtype)

def rope_tables(positions, rot_dim):
    inv_freq = ROPE_THETA ** (-jnp.arange(0, rot_dim, 2, dtype=F32) / rot_dim)
    ang = positions.astype(F32)[..., None] * inv_freq
    return jnp.cos(ang), jnp.sin(ang)

def apply_rope(x, cos, sin):
    xf = x.astype(F32)
    x1, x2 = jnp.split(xf, 2, axis=-1)
    c = cos[:, :, None, :]
    s = sin[:, :, None, :]
    return jnp.concatenate([x1 * c - x2 * s, x2 * c + x1 * s], axis=-1).astype(x.dtype)

def partial_rope(x, cos, sin, rot_dim):
    return jnp.concatenate([apply_rope(x[..., :rot_dim], cos, sin), x[..., rot_dim:]], axis=-1)

def q_block(a, i, axis=1):
    return lax.dynamic_slice_in_dim(a, i * Q_BLOCK, Q_BLOCK, axis)

def chunk_causal_mask(i, seq):
    q_idx = i * Q_BLOCK + jnp.arange(Q_BLOCK)
    k_idx = jnp.arange(seq)
    return (k_idx[None, :] // CHUNK) <= (q_idx[:, None] // CHUNK)

def frame_causal_mask(i, seq):
    q_idx = i * Q_BLOCK + jnp.arange(Q_BLOCK)
    k_idx = jnp.arange(seq)
    return k_idx[None, :] <= q_idx[:, None]

def sweep_query_blocks(block_fn, seq):
    out = lax.map(block_fn, jnp.arange(seq // Q_BLOCK))
    out = jnp.moveaxis(out, 0, 1)
    return out.reshape(out.shape[0], seq, out.shape[3], out.shape[4])

def mla_attention(c_q, c_kv, k_rope_raw, q_norm_g, kv_norm_g, w_uq, w_ukv, cos, sin):
    b, seq, _ = c_q.shape
    q = (rms_norm(c_q, q_norm_g) @ w_uq).reshape(b, seq, MLA_HEADS, MLA_NOPE + MLA_ROPE)
    q_nope = q[..., :MLA_NOPE]
    q_rope = apply_rope(q[..., MLA_NOPE:], cos, sin)
    kv = (rms_norm(c_kv, kv_norm_g) @ w_ukv).reshape(b, seq, MLA_HEADS, MLA_NOPE + MLA_V)
    k_nope = kv[..., :MLA_NOPE]
    v = kv[..., MLA_NOPE:]
    k_rope = apply_rope(k_rope_raw[:, :, None, :], cos, sin)[:, :, 0, :]
    scale = (MLA_NOPE + MLA_ROPE) ** -0.5

    def block(i):
        sc = (jnp.einsum('bqhd,bkhd->bhqk', q_block(q_nope, i), k_nope, preferred_element_type=F32)
              + jnp.einsum('bqhr,bkr->bhqk', q_block(q_rope, i), k_rope, preferred_element_type=F32)) * scale
        sc = jnp.where(chunk_causal_mask(i, seq), sc, NEG_INF)
        p = jax.nn.softmax(sc, axis=-1).astype(v.dtype)
        return jnp.einsum('bhqk,bkhd->bqhd', p, v)

    return sweep_query_blocks(block, seq)

def diff_attention(q, k, v, lam_q1, lam_k1, lam_q2, lam_k2, subln_g, lam_init, cos, sin):
    b, seq, _ = q.shape
    q = partial_rope(q.reshape(b, seq, 2 * DIFF_HEADS, DIFF_QK), cos, sin, DIFF_ROT)
    k = partial_rope(k.reshape(b, seq, 2 * DIFF_HEADS, DIFF_QK), cos, sin, DIFF_ROT)
    q1, q2 = q[:, :, 0::2], q[:, :, 1::2]
    k1, k2 = k[:, :, 0::2], k[:, :, 1::2]
    v = v.reshape(b, seq, DIFF_HEADS, DIFF_V)
    lam = (jnp.exp(jnp.sum(lam_q1.astype(F32) * lam_k1.astype(F32)))
           - jnp.exp(jnp.sum(lam_q2.astype(F32) * lam_k2.astype(F32))) + lam_init)
    scale = DIFF_QK ** -0.5

    def block(i):
        mask = chunk_causal_mask(i, seq)
        s1 = jnp.einsum('bqhd,bkhd->bhqk', q_block(q1, i), k1, preferred_element_type=F32) * scale
        s2 = jnp.einsum('bqhd,bkhd->bhqk', q_block(q2, i), k2, preferred_element_type=F32) * scale
        p = (jax.nn.softmax(jnp.where(mask, s1, NEG_INF), axis=-1)
             - lam * jax.nn.softmax(jnp.where(mask, s2, NEG_INF), axis=-1)).astype(v.dtype)
        return jnp.einsum('bhqk,bkhd->bqhd', p, v)

    o = sweep_query_blocks(block, seq)
    return rms_norm(o, subln_g) * (1.0 - lam_init)

def forgetting_attention(q, k, v, f_logit, f_bias):
    b, seq, _ = q.shape
    q = q.reshape(b, seq, FOX_HEADS, HEAD_DIM)
    k = k.reshape(b, seq, FOX_HEADS, HEAD_DIM)
    v = v.reshape(b, seq, FOX_HEADS, HEAD_DIM)
    log_f = jax.nn.log_sigmoid(f_logit.astype(F32) + f_bias.astype(F32))
    cum = jnp.cumsum(log_f, axis=1).transpose(0, 2, 1)
    scale = HEAD_DIM ** -0.5

    def block(i):
        sc = jnp.einsum('bqhd,bkhd->bhqk', q_block(q, i), k, preferred_element_type=F32) * scale
        sc = sc + q_block(cum, i, axis=2)[..., :, None] - cum[..., None, :]
        sc = jnp.where(frame_causal_mask(i, seq), sc, NEG_INF)
        p = jax.nn.softmax(sc, axis=-1).astype(v.dtype)
        return jnp.einsum('bhqk,bkhd->bqhd', p, v)

    return sweep_query_blocks(block, seq)

def mixer_sublayer(h, cos_m, sin_m, cos_d, sin_d, w_in, mla_q_norm_g, mla_kv_norm_g, mla_w_uq, mla_w_ukv,
                   diff_lam_q1, diff_lam_k1, diff_lam_q2, diff_lam_k2, diff_subln_g, lam_init, fox_f_bias, w_out):
    b, seq, _ = h.shape
    proj = h @ w_in
    parts = []
    start = 0
    for width in IN_SPLITS:
        parts.append(proj[..., start:start + width])
        start += width
    c_q, c_kv, k_rope, dq, dk, dv, fq, fk, fv, ff = parts
    o_mla = mla_attention(c_q, c_kv, k_rope, mla_q_norm_g, mla_kv_norm_g, mla_w_uq, mla_w_ukv, cos_m, sin_m)
    o_diff = diff_attention(dq, dk, dv, diff_lam_q1, diff_lam_k1, diff_lam_q2, diff_lam_k2,
                            diff_subln_g, lam_init, cos_d, sin_d)
    o_fox = forgetting_attention(fq, fk, fv, ff, fox_f_bias)
    o = jnp.concatenate([o_mla.reshape(b, seq, -1), o_diff.reshape(b, seq, -1),
                         o_fox.reshape(b, seq, -1)], axis=-1)
    return o @ w_out

def grouped_moe(h, router_w, router_bias, w_gate, w_up, w_down):
    n = h.shape[0]
    scores = jax.nn.sigmoid(jnp.einsum('nd,de->ne', h, router_w, preferred_element_type=F32))
    biased = (scores + router_bias.astype(F32)).reshape(n, N_GROUPS, GROUP_SIZE)
    group_score = jnp.sum(lax.top_k(biased, TOP_K)[0], axis=-1)
    group_sel = jnp.argmax(group_score, axis=-1)
    in_group = group_sel[:, None] == jnp.arange(N_GROUPS)[None, :]
    cand = jnp.where(in_group[:, :, None], biased, NEG_INF).reshape(n, N_EXPERTS)
    _, idx = lax.top_k(cand, TOP_K)
    sel = jnp.take_along_axis(scores, idx, axis=-1)
    gates = sel / jnp.sum(sel, axis=-1, keepdims=True)
    dense_gates = jnp.einsum('nk,nke->ne', gates, jax.nn.one_hot(idx, N_EXPERTS, dtype=F32)).astype(h.dtype)
    y = jnp.zeros_like(h)
    for e in range(N_EXPERTS):
        a = jax.nn.silu(h @ w_gate[e]) * (h @ w_up[e])
        y = y + dense_gates[:, e:e + 1] * (a @ w_down[e])
    return y

def first_inputs(seed: int = 0) -> dict:
    key = jax.random.key(seed)
    ks = jax.random.split(key, 24)

    def nrm(k, shape, scale):
        return jax.random.normal(k, shape, F32) * scale

    def gain(k, shape):
        return 1.0 + nrm(k, shape, 0.02)

    x = nrm(ks[0], (BATCH, SEQ, D_MODEL), 1.0)
    offsets = jax.random.randint(ks[1], (BATCH, 1), 0, 64, dtype=jnp.int32) * CHUNK
    positions = offsets + jnp.arange(SEQ, dtype=jnp.int32)[None, :]
    return {
        "x": x,
        "positions": positions,
        "ln_in_g": gain(ks[2], (D_MODEL,)),
        "ln_in_b": nrm(ks[3], (D_MODEL,), 0.02),
        "w_in": nrm(ks[4], (DEPTH, D_MODEL, IN_COLS), D_MODEL ** -0.5),
        "mla_q_norm_g": gain(ks[5], (DEPTH, MLA_Q_RANK)),
        "mla_kv_norm_g": gain(ks[6], (DEPTH, MLA_KV_RANK)),
        "mla_w_uq": nrm(ks[7], (DEPTH, MLA_Q_RANK, MLA_HEADS * (MLA_NOPE + MLA_ROPE)), MLA_Q_RANK ** -0.5),
        "mla_w_ukv": nrm(ks[8], (DEPTH, MLA_KV_RANK, MLA_HEADS * (MLA_NOPE + MLA_V)), MLA_KV_RANK ** -0.5),
        "diff_lam_q1": nrm(ks[9], (DEPTH, DIFF_QK), 0.1),
        "diff_lam_k1": nrm(ks[10], (DEPTH, DIFF_QK), 0.1),
        "diff_lam_q2": nrm(ks[11], (DEPTH, DIFF_QK), 0.1),
        "diff_lam_k2": nrm(ks[12], (DEPTH, DIFF_QK), 0.1),
        "diff_subln_g": gain(ks[13], (DEPTH, DIFF_V)),
        "fox_f_bias": jax.random.uniform(ks[14], (DEPTH, FOX_HEADS), F32, 1.0, 4.0),
        "w_out": nrm(ks[15], (DEPTH, D_MIX, D_MODEL), D_MIX ** -0.5 * DEEPNORM_BETA),
        "ln1_g": gain(ks[16], (DEPTH, D_MODEL)),
        "ln1_b": nrm(ks[17], (DEPTH, D_MODEL), 0.02),
        "router_w": nrm(ks[18], (D_MODEL, N_EXPERTS), D_MODEL ** -0.5),
        "router_bias": nrm(ks[19], (N_EXPERTS,), 0.01),
        "exp_w_gate": nrm(ks[20], (DEPTH, N_EXPERTS, D_MODEL, D_EXPERT), D_MODEL ** -0.5),
        "exp_w_up": nrm(ks[21], (DEPTH, N_EXPERTS, D_MODEL, D_EXPERT), D_MODEL ** -0.5),
        "exp_w_down": nrm(ks[22], (DEPTH, N_EXPERTS, D_EXPERT, D_MODEL), D_EXPERT ** -0.5 * DEEPNORM_BETA),
        "ln2_g": gain(ks[23], (DEPTH, D_MODEL)),
        "ln2_b": nrm(jax.random.fold_in(ks[23], 1), (DEPTH, D_MODEL), 0.02),
    }

def first_block(x, positions, ln_in_g, ln_in_b, w_in, mla_q_norm_g, mla_kv_norm_g, mla_w_uq, mla_w_ukv,
              diff_lam_q1, diff_lam_k1, diff_lam_q2, diff_lam_k2, diff_subln_g, fox_f_bias, w_out,
              ln1_g, ln1_b, router_w, router_bias, exp_w_gate, exp_w_up, exp_w_down, ln2_g, ln2_b):
    b, seq, d = x.shape
    cos_m, sin_m = rope_tables(positions, MLA_ROPE)
    cos_d, sin_d = rope_tables(positions, DIFF_ROT)
    h = layer_norm(x, ln_in_g, ln_in_b)
    for l in range(DEPTH):
        lam_init = 0.8 - 0.6 * math.exp(-0.3 * l)
        mix = mixer_sublayer(h, cos_m, sin_m, cos_d, sin_d, w_in[l], mla_q_norm_g[l], mla_kv_norm_g[l],
                             mla_w_uq[l], mla_w_ukv[l], diff_lam_q1[l], diff_lam_k1[l], diff_lam_q2[l],
                             diff_lam_k2[l], diff_subln_g[l], lam_init, fox_f_bias[l], w_out[l])
        h = layer_norm(DEEPNORM_ALPHA * h + mix, ln1_g[l], ln1_b[l])
        ffn = grouped_moe(h.reshape(b * seq, d), router_w, router_bias,
                          exp_w_gate[l], exp_w_up[l], exp_w_down[l]).reshape(b, seq, d)
        h = layer_norm(DEEPNORM_ALPHA * h + ffn, ln2_g[l], ln2_b[l])
    return h


D_FF = 2816
FFN_RESIDUAL = 0.5
SSD_HEADS = 16
SSD_HEAD_DIM = 64
D_SSM = SSD_HEADS * SSD_HEAD_DIM
SSD_GROUPS = 2
D_STATE = 128
CONV_WIDTH = 4
CHUNK_2 = 128
CONV_CH = D_SSM + 2 * SSD_GROUPS * D_STATE
POOL_WINDOWS = (2, 4, 8, 16)
POOL_GROUP = 256
D_POOL = POOL_GROUP * len(POOL_WINDOWS)
IN_PROJ = D_SSM + CONV_CH + SSD_HEADS + D_POOL
D_MIX_EVEN = D_SSM + D_POOL
ATTN_HEADS = 16
ATTN_KV_HEADS = 4
ATTN_GROUP = ATTN_HEADS // ATTN_KV_HEADS
ATTN_HEAD_DIM = 64
WINDOW = 128
BLOCK = 128
QKV_DIM = (ATTN_HEADS + 2 * ATTN_KV_HEADS) * ATTN_HEAD_DIM
MEM_LEN = 256
MEM_HEADS = 4
MEM_HEAD_DIM = D_MODEL // MEM_HEADS
EPS = 1e-6
N_EVEN = (DEPTH + 1) // 2
N_ODD = DEPTH // 2


def rms_norm_2(x, gain):
    xf = x.astype(jnp.float32)
    y = xf * lax.rsqrt(jnp.mean(xf * xf, axis=-1, keepdims=True) + EPS)
    return (y * gain.astype(jnp.float32)).astype(x.dtype)

def swiglu(h, wi, wo):
    gate, up = jnp.split(h @ wi, 2, axis=-1)
    return (jax.nn.silu(gate) * up) @ wo

def alibi_slopes(n):
    return jnp.asarray(2.0 ** (-8.0 * (np.arange(n) + 1) / n), dtype=jnp.float32)

def causal_depthwise_conv(u, w, b):
    ch = u.shape[-1]
    y = lax.conv_general_dilated(u, w[:, None, :].astype(u.dtype), window_strides=(1,),
                                 padding=((CONV_WIDTH - 1, 0),),
                                 dimension_numbers=('NWC', 'WIO', 'NWC'),
                                 feature_group_count=ch)
    return y + b

def ssd_chunked(x, dt, a, b_in, c_in):
    bsz, T = x.shape[0], x.shape[1]
    nc = T // CHUNK_2
    J = SSD_HEADS // SSD_GROUPS
    xr = (x * dt[..., None]).reshape(bsz, nc, CHUNK_2, SSD_GROUPS, J, SSD_HEAD_DIM)
    adt = (dt * a).reshape(bsz, nc, CHUNK_2, SSD_GROUPS, J).transpose(0, 1, 3, 4, 2)
    acs = jnp.cumsum(adt, axis=-1)
    br = b_in.reshape(bsz, nc, CHUNK_2, SSD_GROUPS, D_STATE)
    cr = c_in.reshape(bsz, nc, CHUNK_2, SSD_GROUPS, D_STATE)
    causal = np.tril(np.ones((CHUNK_2, CHUNK_2), dtype=bool))
    seg = jnp.exp(jnp.where(causal, acs[..., :, None] - acs[..., None, :], -jnp.inf))
    cb = jnp.einsum('bclgn,bcsgn->bcgls', cr, br)
    y_diag = jnp.einsum('bcgjls,bcsgjp->bclgjp', cb[:, :, :, None] * seg, xr)
    decay_to_end = jnp.exp(acs[..., -1:] - acs).transpose(0, 1, 4, 2, 3)
    states = jnp.einsum('bclgn,bclgjp->bcgjpn', br, xr * decay_to_end[..., None])
    chunk_decay = jnp.exp(acs[..., -1])

    def carry_state(h, inp):
        st, dec = inp
        return h * dec[..., None, None] + st, h

    _, states_in = lax.scan(carry_state, jnp.zeros_like(states[:, 0]),
                            (jnp.moveaxis(states, 1, 0), jnp.moveaxis(chunk_decay, 1, 0)))
    states_in = jnp.moveaxis(states_in, 0, 1)
    decay_from_start = jnp.exp(acs).transpose(0, 1, 4, 2, 3)
    y_off = jnp.einsum('bclgn,bcgjpn->bclgjp', cr, states_in) * decay_from_start[..., None]
    return (y_diag + y_off).reshape(bsz, T, SSD_HEADS, SSD_HEAD_DIM)

def multiscale_causal_pool(u, pool_w, pool_scale):
    T = u.shape[1]
    t = jnp.arange(T)
    outs = []
    for k, w in enumerate(POOL_WINDOWS):
        ug = u[..., k * POOL_GROUP:(k + 1) * POOL_GROUP].astype(jnp.float32)
        csum = jnp.cumsum(ug, axis=1)
        csum_shift = jnp.pad(csum, ((0, 0), (w, 0), (0, 0)))[:, :T]
        count = jnp.minimum(t + 1, w).astype(jnp.float32)[None, :, None]
        pooled = ((csum - csum_shift) / count - ug).astype(u.dtype)
        outs.append(pooled @ pool_w[k])
    return jnp.concatenate(outs, axis=-1) * pool_scale

def ssd_pool_mixer(h, in_proj, conv_w, conv_b, dt_bias, a_log, d_skip, ssd_norm,
                   pool_w, pool_scale, out_proj):
    bsz, T, _ = h.shape
    proj = h @ in_proj
    z, xbc, dt_raw, u_pool = jnp.split(
        proj, [D_SSM, D_SSM + CONV_CH, D_SSM + CONV_CH + SSD_HEADS], axis=-1)
    xbc = jax.nn.silu(causal_depthwise_conv(xbc, conv_w, conv_b))
    xs, b_in, c_in = jnp.split(xbc, [D_SSM, D_SSM + SSD_GROUPS * D_STATE], axis=-1)
    dt = jax.nn.softplus(dt_raw.astype(jnp.float32) + dt_bias.astype(jnp.float32))
    a = -jnp.exp(a_log.astype(jnp.float32))
    xs_h = xs.reshape(bsz, T, SSD_HEADS, SSD_HEAD_DIM).astype(jnp.float32)
    y = ssd_chunked(xs_h, dt, a,
                    b_in.reshape(bsz, T, SSD_GROUPS, D_STATE).astype(jnp.float32),
                    c_in.reshape(bsz, T, SSD_GROUPS, D_STATE).astype(jnp.float32))
    y = y + d_skip.astype(jnp.float32)[:, None] * xs_h
    y = y.reshape(bsz, T, D_SSM) * jax.nn.silu(z.astype(jnp.float32))
    y = rms_norm_2(y.reshape(bsz, T, SSD_GROUPS, D_SSM // SSD_GROUPS),
                 ssd_norm.reshape(SSD_GROUPS, D_SSM // SSD_GROUPS))
    y_ssd = y.reshape(bsz, T, D_SSM).astype(h.dtype)
    y_pool = multiscale_causal_pool(u_pool, pool_w, pool_scale)
    return jnp.concatenate([y_ssd, y_pool], axis=-1) @ out_proj

def swa_sink_attention(h, wqkv, bqkv, qnorm, knorm, sinks, wo, bo):
    bsz, T, _ = h.shape
    nb = T // BLOCK
    HD, KVH, G = ATTN_HEAD_DIM, ATTN_KV_HEADS, ATTN_GROUP
    qkv = h @ wqkv + bqkv
    q, k, v = jnp.split(qkv, [ATTN_HEADS * HD, (ATTN_HEADS + KVH) * HD], axis=-1)
    q = rms_norm_2(q.reshape(bsz, T, KVH, G, HD), qnorm)
    k = rms_norm_2(k.reshape(bsz, T, KVH, HD), knorm)
    v = v.reshape(bsz, T, KVH, HD)
    qb = q.reshape(bsz, nb, BLOCK, KVH, G, HD)

    def band(t):
        tb = t.reshape(bsz, nb, BLOCK, KVH, HD)
        prev = jnp.pad(tb, ((0, 0), (1, 0), (0, 0), (0, 0), (0, 0)))[:, :nb]
        return jnp.concatenate([prev, tb], axis=2)

    kk, vv = band(k), band(v)
    s = jnp.einsum('bnqhgd,bnkhd->bnhgqk', qb, kk).astype(jnp.float32) * (HD ** -0.5)
    dist = np.arange(BLOCK)[:, None] + BLOCK - np.arange(2 * BLOCK)[None, :]
    in_window = (dist >= 0) & (dist < WINDOW)
    has_prev = (jnp.arange(nb)[:, None, None] > 0) | (np.arange(2 * BLOCK) >= BLOCK)[None, None, :]
    mask = in_window[None] & has_prev
    slopes = alibi_slopes(ATTN_HEADS).reshape(KVH, G)
    s = s - slopes[:, :, None, None] * jnp.asarray(dist, dtype=jnp.float32)
    s = jnp.where(mask[None, :, None, None], s, -jnp.inf)
    sink = jnp.broadcast_to(sinks.astype(jnp.float32).reshape(KVH, G, 1, 1), s.shape[:-1] + (1,))
    p = jax.nn.softmax(jnp.concatenate([s, sink], axis=-1), axis=-1)[..., :-1]
    o = jnp.einsum('bnhgqk,bnkhd->bnqhgd', p.astype(h.dtype), vv)
    return o.reshape(bsz, T, ATTN_HEADS * HD) @ wo + bo

def memory_cross_attention(h, mem_k, mem_v, wq, qnorm, wo):
    bsz, T, _ = h.shape
    q = rms_norm_2((h @ wq).reshape(bsz, T, MEM_HEADS, MEM_HEAD_DIM), qnorm)
    s = jnp.einsum('bthd,bmhd->bhtm', q, mem_k).astype(jnp.float32) * (MEM_HEAD_DIM ** -0.5)
    p = jax.nn.softmax(s, axis=-1).astype(h.dtype)
    o = jnp.einsum('bhtm,bmhd->bthd', p, mem_v)
    return o.reshape(bsz, T, D_MODEL) @ wo

def second_inputs(seed: int = 0) -> dict:
    key = jax.random.key(seed)
    ks = iter(jax.random.split(key, 48))
    f32 = jnp.float32

    def nrm(shape, scale):
        return jax.random.normal(next(ks), shape, f32) * scale

    def gain(shape):
        return 1.0 + nrm(shape, 0.05)

    L = DEPTH
    dt0 = jnp.exp(jax.random.uniform(next(ks), (N_EVEN, SSD_HEADS), f32,
                                     np.log(1e-3), np.log(1e-1)))
    dt_bias = dt0 + jnp.log(-jnp.expm1(-dt0))
    a_log = jnp.log(jax.random.uniform(next(ks), (N_EVEN, SSD_HEADS), f32, 1.0, 16.0))
    return {
        "x": nrm((BATCH, SEQ, D_MODEL), 1.0),
        "mem": nrm((BATCH, MEM_LEN, D_MODEL), 1.0),
        "mem_norm": gain((D_MODEL,)),
        "mem_wkv": nrm((D_MODEL, 2 * D_MODEL), D_MODEL ** -0.5),
        "mem_knorm": gain((MEM_HEAD_DIM,)),
        "ffn1_norm": gain((L, D_MODEL)),
        "ffn1_wi": nrm((L, D_MODEL, 2 * D_FF), D_MODEL ** -0.5),
        "ffn1_wo": nrm((L, D_FF, D_MODEL), D_FF ** -0.5),
        "mix_norm": gain((L, D_MODEL)),
        "ssd_in_proj": nrm((N_EVEN, D_MODEL, IN_PROJ), D_MODEL ** -0.5),
        "ssd_conv_w": nrm((N_EVEN, CONV_WIDTH, CONV_CH), CONV_WIDTH ** -0.5),
        "ssd_conv_b": nrm((N_EVEN, CONV_CH), 0.02),
        "ssd_dt_bias": dt_bias,
        "ssd_a_log": a_log,
        "ssd_d": 1.0 + nrm((N_EVEN, SSD_HEADS), 0.1),
        "ssd_norm": gain((N_EVEN, D_SSM)),
        "pool_w": nrm((N_EVEN, len(POOL_WINDOWS), POOL_GROUP, POOL_GROUP), POOL_GROUP ** -0.5),
        "pool_scale": gain((N_EVEN, D_POOL)),
        "even_out_proj": nrm((N_EVEN, D_MIX_EVEN, D_MODEL), D_MIX_EVEN ** -0.5),
        "attn_wqkv": nrm((N_ODD, D_MODEL, QKV_DIM), D_MODEL ** -0.5),
        "attn_bqkv": nrm((N_ODD, QKV_DIM), 0.02),
        "attn_qnorm": gain((N_ODD, ATTN_HEAD_DIM)),
        "attn_knorm": gain((N_ODD, ATTN_HEAD_DIM)),
        "attn_sinks": nrm((N_ODD, ATTN_HEADS), 0.5),
        "attn_wo": nrm((N_ODD, ATTN_HEADS * ATTN_HEAD_DIM, D_MODEL), (ATTN_HEADS * ATTN_HEAD_DIM) ** -0.5),
        "attn_bo": nrm((N_ODD, D_MODEL), 0.02),
        "xattn_norm": gain((L, D_MODEL)),
        "xattn_wq": nrm((L, D_MODEL, D_MODEL), D_MODEL ** -0.5),
        "xattn_qnorm": gain((L, MEM_HEAD_DIM)),
        "xattn_wo": nrm((L, D_MODEL, D_MODEL), D_MODEL ** -0.5),
        "ffn2_norm": gain((L, D_MODEL)),
        "ffn2_wi": nrm((L, D_MODEL, 2 * D_FF), D_MODEL ** -0.5),
        "ffn2_wo": nrm((L, D_FF, D_MODEL), D_FF ** -0.5),
    }

def second_block(x, mem, mem_norm, mem_wkv, mem_knorm, ffn1_norm, ffn1_wi, ffn1_wo, mix_norm,
              ssd_in_proj, ssd_conv_w, ssd_conv_b, ssd_dt_bias, ssd_a_log, ssd_d, ssd_norm,
              pool_w, pool_scale, even_out_proj, attn_wqkv, attn_bqkv, attn_qnorm, attn_knorm,
              attn_sinks, attn_wo, attn_bo, xattn_norm, xattn_wq, xattn_qnorm, xattn_wo,
              ffn2_norm, ffn2_wi, ffn2_wo):
    bsz = mem.shape[0]
    mem_kv = rms_norm_2(mem, mem_norm) @ mem_wkv
    mem_k, mem_v = jnp.split(mem_kv, 2, axis=-1)
    mem_k = rms_norm_2(mem_k.reshape(bsz, MEM_LEN, MEM_HEADS, MEM_HEAD_DIM), mem_knorm)
    mem_v = mem_v.reshape(bsz, MEM_LEN, MEM_HEADS, MEM_HEAD_DIM)
    for i in range(DEPTH):
        x = x + FFN_RESIDUAL * swiglu(rms_norm_2(x, ffn1_norm[i]), ffn1_wi[i], ffn1_wo[i])
        h = rms_norm_2(x, mix_norm[i])
        if i % 2 == 0:
            e = i // 2
            x = x + ssd_pool_mixer(h, ssd_in_proj[e], ssd_conv_w[e], ssd_conv_b[e], ssd_dt_bias[e],
                                   ssd_a_log[e], ssd_d[e], ssd_norm[e], pool_w[e], pool_scale[e],
                                   even_out_proj[e])
        else:
            o = i // 2
            x = x + swa_sink_attention(h, attn_wqkv[o], attn_bqkv[o], attn_qnorm[o], attn_knorm[o],
                                       attn_sinks[o], attn_wo[o], attn_bo[o])
        x = x + memory_cross_attention(rms_norm_2(x, xattn_norm[i]), mem_k, mem_v,
                                       xattn_wq[i], xattn_qnorm[i], xattn_wo[i])
        x = x + FFN_RESIDUAL * swiglu(rms_norm_2(x, ffn2_norm[i]), ffn2_wi[i], ffn2_wo[i])
    return x


def setup_inputs(seed=0):
    out = dict(first_inputs(seed))
    for name, value in second_inputs(seed + 1).items():
        if name != "x":
            out[name + "_2"] = value
    return out


def reference(
    x, positions, ln_in_g, ln_in_b, w_in, mla_q_norm_g, mla_kv_norm_g, mla_w_uq, mla_w_ukv,
    diff_lam_q1, diff_lam_k1, diff_lam_q2, diff_lam_k2, diff_subln_g, fox_f_bias, w_out, ln1_g,
    ln1_b, router_w, router_bias, exp_w_gate, exp_w_up, exp_w_down, ln2_g, ln2_b, mem_2,
    mem_norm_2, mem_wkv_2, mem_knorm_2, ffn1_norm_2, ffn1_wi_2, ffn1_wo_2, mix_norm_2,
    ssd_in_proj_2, ssd_conv_w_2, ssd_conv_b_2, ssd_dt_bias_2, ssd_a_log_2, ssd_d_2, ssd_norm_2,
    pool_w_2, pool_scale_2, even_out_proj_2, attn_wqkv_2, attn_bqkv_2, attn_qnorm_2,
    attn_knorm_2, attn_sinks_2, attn_wo_2, attn_bo_2, xattn_norm_2, xattn_wq_2, xattn_qnorm_2,
    xattn_wo_2, ffn2_norm_2, ffn2_wi_2, ffn2_wo_2,
):
    x = first_block(
        x, positions, ln_in_g, ln_in_b, w_in, mla_q_norm_g, mla_kv_norm_g, mla_w_uq, mla_w_ukv,
        diff_lam_q1, diff_lam_k1, diff_lam_q2, diff_lam_k2, diff_subln_g, fox_f_bias, w_out,
        ln1_g, ln1_b, router_w, router_bias, exp_w_gate, exp_w_up, exp_w_down, ln2_g, ln2_b,
    )
    return second_block(
        x, mem_2, mem_norm_2, mem_wkv_2, mem_knorm_2, ffn1_norm_2, ffn1_wi_2, ffn1_wo_2,
        mix_norm_2, ssd_in_proj_2, ssd_conv_w_2, ssd_conv_b_2, ssd_dt_bias_2, ssd_a_log_2,
        ssd_d_2, ssd_norm_2, pool_w_2, pool_scale_2, even_out_proj_2, attn_wqkv_2, attn_bqkv_2,
        attn_qnorm_2, attn_knorm_2, attn_sinks_2, attn_wo_2, attn_bo_2, xattn_norm_2,
        xattn_wq_2, xattn_qnorm_2, xattn_wo_2, ffn2_norm_2, ffn2_wi_2, ffn2_wo_2,
    )


_drawn_inputs = setup_inputs


def setup_inputs(seed=0):
    import zlib

    import numpy as np

    out = dict(_drawn_inputs(seed))
    spreads = {}
    factors = {'mla_q_norm_g': 8.0,
     'mla_kv_norm_g': 3.213,
     'diff_lam_k1': 3.323,
     'diff_subln_g': 2.715,
     'mem_norm_2': 7.332,
     'mem_knorm_2': 8.0,
     'ssd_conv_b_2': 3.858,
     'attn_bqkv_2': 4.569,
     'attn_qnorm_2': 7.84,
     'attn_knorm_2': 8.0,
     'attn_sinks_2': 18.825,
     'attn_bo_2': 4.142,
     'xattn_norm_2': 8.0,
     'xattn_qnorm_2': 8.0}
    for name, (base, spread) in spreads.items():
        noise = np.random.default_rng([zlib.crc32(name.encode()), seed]).standard_normal(out[name].shape)
        drawn = base * np.exp(spread * noise) if base else spread * noise
        out[name] = jnp.asarray(drawn.astype(out[name].dtype))
    for name, factor in factors.items():
        out[name] = (out[name] * factor).astype(out[name].dtype)
    return out
```

```python
from contextlib import ExitStack
import math

import numpy as np
import concourse.bass as bass
from concourse import mybir

F32 = mybir.dt.float32
F32R = mybir.dt.float32r
I32 = mybir.dt.int32
ACT = mybir.ActivationFunctionType
ALU = mybir.AluOpType
AXX = mybir.AxisListType.X

D, T, DEPTH, HD = 1024, 256, 2, 64
F, NE, FE = 2816, 16, 512
CW = 2048
NS, NR = 3, 2
ALPHA = (2 * DEPTH) ** 0.25
NEG = -1e30
MAGIC = 12582912.0
SPLITS = (384, 256, 32, 256, 256, 256, 256, 256, 256, 4)
IN_COLS = sum(SPLITS)
OFF = [sum(SPLITS[:i]) for i in range(len(SPLITS))]



def constants():
    p = np.arange(128)
    out = {}
    out["ident"] = np.eye(128)
    out["zto"] = np.concatenate([np.zeros((128, 128)), (p[:, None] <= p[None, :]) * 1.0, np.ones((128, 128))], axis=1)
    k = np.arange(256)
    q1 = 128 + p
    out["mchunk"] = np.where(k[None, :] // 64 <= q1[:, None] // 64, 0.0, NEG)
    out["mframe"] = np.where(k[None, :] <= q1[:, None], 0.0, NEG)
    out["mseg"] = np.where(p[:, None] <= p[None, :], 0.0, NEG)
    fm = [500000.0 ** (-i / 32) for i in range(0, 32, 2)]
    fd = [500000.0 ** (-i / 8) for i in range(0, 8, 2)]
    out["invf"] = np.tile(np.array(fm + fd), (128, 1))
    out["c4"] = np.tile(np.arange(4, 0, -1), (128, 1))
    out["c16"] = np.tile(np.arange(16, 0, -1), (128, 1))
    out["half"] = np.full((128, 8), -0.5)
    return out


def late_constants():
    p = np.arange(128)
    k = np.arange(256)
    t = np.arange(256)
    bands = np.zeros((128, 2, 4, 256))
    for w in range(4):
        n = 2 << w
        for s in range(2):
            si = s * 128 + p
            d = t[None, :] - si[:, None]
            cnt = np.minimum(t + 1, n)
            bands[:, s, w, :] = ((d >= 0) & (d < n)) / cnt[None, :] - (d == 0)
    dist = (128 + p)[:, None] - k[None, :]
    slopes = 2.0 ** (-8.0 * (np.arange(16) + 1) / 16)
    ali = np.where((dist >= 0) & (dist < 128), 0.0, NEG)[:, None, :] - slopes[None, :, None] * dist[:, None, :]
    e = np.zeros((128, 16, 128))
    for i in range(16):
        e[i, i, :] = 1.0
    return {"esel": e.reshape(128, -1)[:16], "bands": bands.reshape(128, -1), "alibi": ali.reshape(128, -1)}


def layout(parts):
    at, out = 0, {}
    for name, a in parts.items():
        out[name] = (at, a.shape[1])
        at += a.shape[1]
    return out, at


CONST, NCONST = layout(constants())

VECS = [("mem_norm", 8), ("ffn1_norm0", 8), ("ffn1_norm1", 8), ("mix_norm0", 8), ("mix_norm1", 8),
        ("xattn_norm0", 8), ("xattn_norm1", 8), ("ffn2_norm0", 8), ("ffn2_norm1", 8), ("ssd_norm", 8),
        ("pool_scale", 8), ("conv_b", 12), ("conv_w", 48)]
VAT, NV = {}, 0
for _n, _c in VECS:
    VAT[_n] = NV
    NV += _c

ROWS = {
    "mla": [("qg", 384), ("kvg", 256), ("subln", 64), ("fb", 4), ("lq1", 32), ("lq2", 32), ("lk1", 32), ("lk2", 32)],
    "moe": [("rb", 16)],
    "ssd": [("dtb", 16), ("alog", 16), ("dskip", 16)],
    "swa": [("bqkv", 1536), ("qn", 64), ("kn", 64), ("sink", 16), ("bo", 1024)],
    "mem": [("kn", 256)],
    "xat": [("qn", 256)],
}


def row_at(stage, name):
    at = 0
    for n, c in ROWS[stage]:
        if n == name:
            return at, at + c
        at += c
    raise KeyError(name)


def row_len(stage):
    return sum(c for _, c in ROWS[stage])




def plan_moving(K, N):
    out = []
    for n0 in range(0, N, 512):
        w = min(512, N - n0)
        per = CW // w
        kt = K // 128
        for k0 in range(0, kt, per):
            out.append((n0, w, k0, min(per, kt - k0)))
    return out


def pack_moving(W):
    K, N = W.shape
    return [W[k0 * 128:(k0 + n) * 128, n0:n0 + w].reshape(n, 128, w).transpose(1, 0, 2).reshape(-1)
            for n0, w, k0, n in plan_moving(K, N)]


def pack_pair(G, U, f):
    g = G[:, f * 128:(f + 1) * 128].reshape(-1, 128, 128).transpose(1, 0, 2)
    u = U[:, f * 128:(f + 1) * 128].reshape(-1, 128, 128).transpose(1, 0, 2)
    return np.stack([g, u], axis=1).reshape(-1)


def pack_down(W, f):
    return W[f * 128:(f + 2) * 128].reshape(2, 128, -1).transpose(1, 0, 2).reshape(-1)


def plan_gated(nf):
    out = []
    for f in range(0, nf, 2):
        out += [("gu", f), ("gu", f + 1)]
        if f >= 2:
            out.append(("d", f - 2))
    return out + [("d", nf - 2)]


def pack_gated(G, U, W):
    return [pack_pair(G, U, f) if kind == "gu" else pack_down(W, f) for kind, f in plan_gated(G.shape[1] // 128)]


def plan_experts():
    return plan_gated(NE * FE // 128)


def pack_experts(G, U, W):
    nf = FE // 128
    return [pack_pair(G[f // nf], U[f // nf], f % nf) if kind == "gu" else pack_down(W[f // nf], f % nf)
            for kind, f in plan_experts()]


def sizes_moving(K, N):
    return [w * n for _, w, _, n in plan_moving(K, N)]


STREAM = []
for _l in range(DEPTH):
    STREAM += [(f"w_in{_l}", sizes_moving(D, IN_COLS)), (f"uq{_l}", sizes_moving(384, 768)),
               (f"ukv{_l}", sizes_moving(256, 1024)), (f"w_out{_l}", sizes_moving(D, D)),
               (f"exp{_l}", [CW] * len(plan_experts()))]
STREAM += [("mem_wkv", sizes_moving(D, 2 * D)), ("ffn10", [CW] * len(plan_gated(F // 128))),
           ("pool_in", sizes_moving(D, D)), ("pool_w", [CW]), ("out_pool", sizes_moving(D, D)),
           ("ssd_xbc", [CW] * 6), ("ssd_z", sizes_moving(D, D + 16)), ("out_ssd", sizes_moving(D, D)),
           ("xwq0", sizes_moving(D, D)), ("xwo0", sizes_moving(D, D)), ("ffn20", [CW] * len(plan_gated(F // 128))),
           ("ffn11", [CW] * len(plan_gated(F // 128))), ("wqkv", sizes_moving(D, 1536)), ("wo", sizes_moving(D, D)),
           ("xwq1", sizes_moving(D, D)), ("xwo1", sizes_moving(D, D)), ("ffn21", [CW] * len(plan_gated(F // 128)))]


def pack_weights(i):
    out = {}
    for l in range(DEPTH):
        out[f"w_in{l}"] = pack_moving(i["w_in"][l])
        out[f"uq{l}"] = pack_moving(i["mla_w_uq"][l])
        out[f"ukv{l}"] = pack_moving(i["mla_w_ukv"][l])
        out[f"w_out{l}"] = pack_moving(i["w_out"][l])
        out[f"exp{l}"] = pack_experts(i["exp_w_gate"][l], i["exp_w_up"][l], i["exp_w_down"][l])
        for n in ("ffn1", "ffn2"):
            wi = i[n + "_wi_2"][l]
            out[f"{n}{l}"] = pack_gated(wi[:, :F], wi[:, F:], i[n + "_wo_2"][l])
        out[f"xwq{l}"] = pack_moving(i["xattn_wq_2"][l])
        out[f"xwo{l}"] = pack_moving(i["xattn_wo_2"][l])
    out["mem_wkv"] = pack_moving(i["mem_wkv_2"])
    w = i["ssd_in_proj_2"][0]
    out["ssd_z"] = pack_moving(np.concatenate([w[:, :1024], w[:, 2560:2576]], axis=1))
    out["pool_in"] = pack_moving(w[:, 2576:3600])
    x = w[:, 1024:2560].reshape(D, 12, 128)
    even, odd = x[:, 0::2].reshape(D, 768), x[:, 1::2].reshape(D, 768)
    out["ssd_xbc"] = [pack_pair(even, odd, f) for f in range(6)]
    pw = i["pool_w_2"][0].reshape(4, 2, 128, 2, 128)
    out["pool_w"] = [pw.transpose(2, 0, 3, 1, 4).reshape(-1)]
    out["out_ssd"] = pack_moving(i["even_out_proj_2"][0][:1024])
    out["out_pool"] = pack_moving(i["even_out_proj_2"][0][1024:])
    out["wqkv"] = pack_moving(i["attn_wqkv_2"][0])
    out["wo"] = pack_moving(i["attn_wo_2"][0])
    return {n: np.concatenate(out[n]) for n, _ in STREAM}


def pack_small(i):
    f = np.float32
    out = {"const": np.concatenate(list(constants().values()), axis=1).astype(f)}
    for n, a in late_constants().items():
        out[n] = a.astype(f)
    v = {"mem_norm": i["mem_norm_2"], "ssd_norm": i["ssd_norm_2"][0], "pool_scale": i["pool_scale_2"][0],
         "conv_b": i["ssd_conv_b_2"][0], "conv_w": i["ssd_conv_w_2"][0].reshape(-1)}
    for l in range(DEPTH):
        for n in ("ffn1_norm", "mix_norm", "xattn_norm", "ffn2_norm"):
            v[f"{n}{l}"] = i[n + "_2"][l]
    out["vecs"] = np.ascontiguousarray(np.concatenate([v[n].reshape(-1, 128) for n, _ in VECS], axis=0).T)
    for l in range(DEPTH):
        out[f"row_mla{l}"] = np.concatenate([i["mla_q_norm_g"][l], i["mla_kv_norm_g"][l], i["diff_subln_g"][l],
                                             i["fox_f_bias"][l], i["diff_lam_q1"][l], i["diff_lam_q2"][l],
                                             i["diff_lam_k1"][l], i["diff_lam_k2"][l]])
        out[f"row_ln1{l}"] = np.concatenate([i["ln1_g"][l], i["ln1_b"][l]])
        out[f"row_ln2{l}"] = np.concatenate([i["ln2_g"][l], i["ln2_b"][l]])
        out[f"row_xat{l}"] = i["xattn_qnorm_2"][l]
    out["row_moe"] = i["router_bias"]
    out["row_lnin"] = np.concatenate([i["ln_in_g"], i["ln_in_b"]])
    out["row_ssd"] = np.concatenate([i["ssd_dt_bias_2"][0], i["ssd_a_log_2"][0], i["ssd_d_2"][0]])
    out["row_swa"] = np.concatenate([i["attn_bqkv_2"][0], i["attn_qnorm_2"][0], i["attn_knorm_2"][0],
                                     i["attn_sinks_2"][0], i["attn_bo_2"][0]])
    out["row_mem"] = i["mem_knorm_2"]
    out["x"] = i["x"][0]
    out["mem"] = i["mem_2"][0]
    out["pos"] = np.ascontiguousarray(i["positions"].reshape(2, 128).T)
    out["router"] = np.ascontiguousarray(i["router_w"].reshape(8, 128, 16).transpose(1, 0, 2).reshape(128, 128))
    return out



class Program:

    ENGINES = ("sync", "tensor", "vector", "scalar", "gpsimd")

    def __init__(self, nc, ctx):
        self.nc, self.ctx = nc, ctx
        self.todo = {e: [] for e in self.ENGINES}
        self.done = {e: 0 for e in self.ENGINES}
        self.sems = {e: ctx.enter_context(nc.semaphore("s_" + e)) for e in self.ENGINES}
        self.gate = {e: [] for e in self.ENGINES}

    def sem(self, name):
        self.sems[name] = self.ctx.enter_context(self.nc.semaphore(name))
        self.done[name] = 0
        return name

    def op(self, engine, fn, *after):
        waits = list(after) + self.gate[engine]
        self.gate[engine] = []
        self.done[engine] += 1
        self.todo[engine].append((waits, fn, engine, 1))
        return (engine, self.done[engine])

    def dma(self, sem, fn, *after, engine="sync"):
        self.done[sem] += 16
        self.todo[engine].append((list(after), fn, sem, 16))
        return (sem, self.done[sem])

    def own(self, engine):
        return (engine, self.done[engine])

    def meet(self):
        now = [self.own(e) for e in ("tensor", "vector", "scalar", "gpsimd")]
        for e in ("tensor", "vector", "scalar", "gpsimd"):
            self.gate[e] = list(now)
        return now

    def emit(self, block, last):
        def flat(x):
            for t in x:
                if isinstance(t, list):
                    yield from flat(t)
                elif t is not None:
                    yield t

        def run(engine):
            def body(eng):
                seen = {}
                for waits, fn, sem, n in self.todo[engine]:
                    for s, v in flat(waits):
                        if v > seen.get(s, 0):
                            eng.wait_ge(self.sems[s], v)
                            seen[s] = v
                    fn(eng).then_inc(self.sems[sem], n)
                if engine == "sync":
                    eng.wait_ge(self.sems[last[0]], last[1])
            return body

        block.sync(run("sync"))
        block.tensor(run("tensor"))
        block.vector(run("vector"))
        block.scalar(run("scalar"))
        block.gpsimd(run("gpsimd"))


class Bank:

    def __init__(self, tensor):
        self.t = tensor
        self.free = None


class Scratch:

    def __init__(self, tensor, size):
        self.t, self.size, self.at = tensor, size, 0

    def cut(self, n):
        a = self.at
        self.at += n
        assert self.at <= self.size, self.at
        return self.t[:, a:a + n]


def bc(ap, axis, n):
    ap = ap.unsqueeze(axis)
    shape = list(ap.shape)
    shape[axis] = n
    return ap.broadcast_to(shape)


def r3(ap, b):
    return ap.rearrange("p (a b) -> p a b", b=b)


class Kernel:

    def __init__(self, nc, ctx, d):
        self.nc, self.d = nc, d
        self.P = Program(nc, ctx)

        def sb(name, n, dt=F32, p=128):
            return ctx.enter_context(nc.sbuf_tensor(name, [p, n], dt))

        self.stage = [sb(f"stage{i}", CW) for i in range(NS)]
        self.hi = [sb(f"hi{i}", CW, F32R) for i in range(NR)]
        self.lo = [sb(f"lo{i}", CW, F32R) for i in range(NR)]
        self.thi = sb("thi", 8 * T, F32R)
        self.tlo = sb("tlo", 8 * T, F32R)
        self.ahi = sb("ahi", 4 * T, F32R)
        self.alo = sb("alo", 4 * T, F32R)
        self.X = sb("X", 2 * D)
        self.gb_ = sb("gb_", 2 * D)
        self.rows = sb("rows", max(row_len(s) for s in ROWS))
        self.const = sb("const_sb", NCONST)
        self.vecs = sb("vecs_sb", NV)
        self.st = sb("st", 256)
        n = 24200
        self.scr = Scratch(sb("scr", n), n)
        self.bank = [Bank(ctx.enter_context(nc.psum_tensor(f"bank{i}", [128, 512], F32))) for i in range(8)]
        self.d_stage = [self.P.sem(f"d_stage{i}") for i in range(NS)]
        self.d_const = self.P.sem("d_const")
        self.d_x = self.P.sem("d_x")
        self.d_row = self.P.sem("d_row")
        self.d_ln = self.P.sem("d_ln")
        self.d_late = self.P.sem("d_late")
        self.d_out = self.P.sem("d_out")
        self.ident = self.c("ident")
        self.zto = self.c("zto")
        self.tri, self.ones = self.zto[:, 128:256], self.zto[:, 256:384]
        self.chunks = []
        for name, sizes in STREAM:
            at = 0
            for n in sizes:
                self.chunks.append((name, at, n))
                at += 128 * n
        self.at = 0
        self.loaded, self.rounded, self.parted, self.used = {}, {}, {}, {}
        for i in range(NS):
            self.load(i)
        for i in range(NR):
            self.split(i)
            self.load(i + NS)

    def c(self, name):
        a, n = CONST[name]
        return self.const[:, a:a + n]

    def vec(self, name, k):
        a = VAT[name] + k
        return self.vecs[:, a:a + 1]

    def row(self, stage, name):
        a, b = row_at(stage, name)
        return self.rows[:, a:b]

    def v(self, fn, *after):
        return self.P.op("vector", fn, self.P.own("vector"), *after)

    def a(self, fn, *after):
        return self.P.op("scalar", fn, self.P.own("scalar"), *after)

    def g(self, fn, *after):
        return self.P.op("gpsimd", fn, self.P.own("gpsimd"), *after)

    def pe(self, fn, *after):
        return self.P.op("tensor", fn, *after)

    def load(self, i):
        if i >= len(self.chunks):
            return
        name, at, n = self.chunks[i]
        src = self.d[name][at:at + 128 * n].rearrange("(p c) -> p c", p=128)
        dst = self.stage[i % NS][:, :n]
        before = [self.rounded[i - NS], self.parted[i - NS]] if i >= NS else []
        self.loaded[i] = self.P.dma(self.d_stage[i % NS], lambda e: e.dma_start(dst, src), *before)

    def split(self, i):
        if i >= len(self.chunks):
            return
        n = self.chunks[i][2]
        src = self.stage[i % NS][:, :n]
        hi, lo = self.hi[i % NR][:, :n], self.lo[i % NR][:, :n]
        last = self.used.get(i - NR)
        old = self.parted.get(i - NR)
        self.rounded[i] = self.P.op("scalar", lambda e: e.activation(hi, src, ACT.Copy), self.loaded[i], last, old)
        self.parted[i] = self.P.op("vector", lambda e: e.tensor_tensor(lo, src, hi.bitcast(F32), ALU.subtract),
                                   self.loaded[i], self.rounded[i], last)

    def chunk(self, name, fn, *after):
        i = self.at
        assert self.chunks[i][0] == name, (self.chunks[i], name)
        self.at += 1
        hi, lo = self.hi[i % NR], self.lo[i % NR]
        tok = self.P.op("tensor", lambda e: fn(e, hi, lo), self.rounded[i], self.parted[i], *after)
        self.used[i] = tok
        self.split(i + NR)
        self.load(i + NR + NS)
        return tok

    def moving(self, name, K, N, banks, evac, ready):
        plan = plan_moving(K, N)
        kt = K // 128
        turn = 0
        for n0, w, k0, n in plan:
            pair = banks[turn % len(banks)]

            def fn(e, hi, lo, n0=n0, w=w, k0=k0, n=n, pair=pair):
                for j in range(n):
                    for tt in range(2):
                        xs = slice((k0 + j) * T + tt * 128, (k0 + j) * T + tt * 128 + 128)
                        ws = slice(j * w, (j + 1) * w)
                        out = pair[tt].t[:, :w]
                        e.matmul(out, self.thi[:, xs], hi[:, ws], start=(k0 + j == 0), stop=False)
                        e.matmul(out, self.thi[:, xs], lo[:, ws], start=False, stop=False)
                        m = e.matmul(out, self.tlo[:, xs], hi[:, ws], start=False, stop=(k0 + j == kt - 1))
                return m
            tok = self.chunk(name, fn, ready, pair[0].free, pair[1].free)
            if k0 + n == kt:
                for tt in range(2):
                    pair[tt].free = evac(tt, n0, w, pair[tt].t[:, :w], tok)
                turn += 1

    def pair_product(self, name, bank, ready):
        def fn(e, hi, lo):
            for s in range(2):
                out = bank.t[:, s * T:(s + 1) * T]
                for k in range(8):
                    ws = slice((s * 8 + k) * 128, (s * 8 + k + 1) * 128)
                    xs = slice(k * T, (k + 1) * T)
                    e.matmul(out, hi[:, ws], self.thi[:, xs], start=(k == 0), stop=False)
                    e.matmul(out, hi[:, ws], self.tlo[:, xs], start=False, stop=False)
                    m = e.matmul(out, lo[:, ws], self.thi[:, xs], start=False, stop=(k == 7))
            return m
        return self.chunk(name, fn, ready, bank.free)

    def gated(self, name, plan, ready, gate=None):
        nf = max(f for k, f in plan if k == "gu") + 1
        act, used = {}, {}
        ys = self.bank[0:4]
        sil = [self.scr.cut(T) for _ in range(4)]
        val = [self.scr.cut(T) for _ in range(4)]
        last = None
        vfree, parts = {}, {}
        for kind, f in plan:
            if kind == "gu":
                bank = self.bank[4 + f % 4]
                tok = self.pair_product(name, bank, ready)
                s, o = sil[f % 4], val[f % 4]
                g_ps, u_ps = bank.t[:, :T], bank.t[:, T:]
                sl = slice((f % 4) * T, (f % 4 + 1) * T)
                hi, lo = self.ahi[:, sl], self.alo[:, sl]
                t = self.a(lambda e, s=s, x=g_ps: e.activation(s, x, ACT.Silu), tok, parts.get(f - 4), vfree.get(f - 4))
                if gate is not None:
                    gt = gate(f)
                    t = self.g(lambda e, s=s, gt=gt: e.tensor_tensor(s, s, gt, ALU.mult), t)
                t = self.v(lambda e, s=s, o=o, x=u_ps: e.tensor_tensor(o, s, x, ALU.mult), t, act.get(f - 4))
                bank.free = t
                vfree[f] = t
                down = used.get((f - 4) - (f - 4) % 2) if f >= 4 else None
                h = self.a(lambda e, o=o, hi=hi: e.activation(hi, o, ACT.Copy), t, down, parts.get(f - 4))
                p = self.v(lambda e, o=o, hi=hi, lo=lo: e.tensor_tensor(lo, o, hi.bitcast(F32), ALU.subtract), h, down)
                act[f], parts[f] = h, p
            else:
                def fn(e, hi, lo, f=f):
                    for j in range(2):
                        for tt in range(2):
                            at = ((f + j) % 4) * T + tt * 128
                            xs = slice(at, at + 128)
                            for half in range(2):
                                ws = slice(j * D + half * 512, j * D + half * 512 + 512)
                                out = ys[tt * 2 + half].t[:, :]
                                e.matmul(out, self.ahi[:, xs], hi[:, ws], start=(f + j == 0), stop=False)
                                e.matmul(out, self.ahi[:, xs], lo[:, ws], start=False, stop=False)
                                m = e.matmul(out, self.alo[:, xs], hi[:, ws], start=False, stop=(f + j == nf - 1))
                    return m
                first = [b.free for b in ys] if f == 0 else []
                last = self.chunk(name, fn, first, act[f], parts[f], act[f + 1], parts[f + 1])
                used[f] = last
        return last

    def turn(self, src, kts, ready, scale=None, free=None, hi=None, lo=None):
        hi = hi or self.thi
        lo = lo or self.tlo
        toks = []
        for n, k0 in enumerate(range(0, kts, 2)):
            bank = self.bank[4 + n % 4]
            kk = min(2, kts - k0)

            def fn(e, k0=k0, kk=kk, bank=bank):
                for j in range(kk):
                    for tt in range(2):
                        m = e.transpose(bank.t[:, j * T + tt * 128:j * T + tt * 128 + 128],
                                        src(tt)[:, (k0 + j) * 128:(k0 + j + 1) * 128], self.ident)
                return m
            tok = self.pe(fn, ready, bank.free)
            if scale is None:
                h_, l_ = hi[:, k0 * T:(k0 + kk) * T], lo[:, k0 * T:(k0 + kk) * T]
                ps = bank.t[:, :kk * T]
                t = self.a(lambda e, h_=h_, ps=ps: e.activation(h_, ps, ACT.Copy), tok, free)
                t = self.v(lambda e, h_=h_, l_=l_, ps=ps: e.tensor_tensor(l_, ps, h_.bitcast(F32), ALU.subtract), t, free)
            else:
                t = tok
                for j in range(kk):
                    sl = slice((k0 + j) * T, (k0 + j + 1) * T)
                    h_, l_, ps = hi[:, sl], lo[:, sl], bank.t[:, j * T:(j + 1) * T]
                    sc = scale(k0 + j)
                    t = self.a(lambda e, h_=h_, ps=ps, sc=sc: e.activation(h_, ps, ACT.Copy, scale=sc), t, free)
                for j in range(kk):
                    sl = slice((k0 + j) * T, (k0 + j + 1) * T)
                    h_, l_, ps = hi[:, sl], lo[:, sl], bank.t[:, j * T:(j + 1) * T]
                    sc = scale(k0 + j)
                    t = self.v(lambda e, h_=h_, l_=l_, ps=ps, sc=sc: e.scalar_tensor_tensor(
                        l_, ps, sc, h_.bitcast(F32), ALU.mult, ALU.subtract), t, free)
            bank.free = t
            toks += [t]
        return toks

    def power(self, out, x, n, after):
        return self.g(lambda e: e.tensor_tensor(out, x, self.c("half")[:, :1].broadcast_to([128, n]), ALU.pow), after)

    def x(self, tt):
        return self.X[:, tt * D:(tt + 1) * D]

    def layer_norm(self, src, ready, ln):
        def one(tt):
            s, st = src(tt), self.st[:, tt * 32:(tt + 1) * 32]
            for c in range(2):
                self.v(lambda e, c=c: e.bn_stats(st[:, c * 6:(c + 1) * 6], s[:, c * 512:(c + 1) * 512]), ready)
            self.v(lambda e: e.bn_aggr(st[:, 12:14], st[:, 0:12]))
            t = self.v(lambda e: e.tensor_scalar(st[:, 14:15], st[:, 13:14], 1e-5, None, ALU.add))
            t = self.power(st[:, 15:16], st[:, 14:15], 1, t)
            t = self.v(lambda e: e.tensor_scalar(s, s, st[:, 12:13], st[:, 15:16], ALU.subtract, ALU.mult), t)
            t = self.v(lambda e: e.tensor_tensor(s, s, self.gb_[:, :D], ALU.mult), ln)
            return self.g(lambda e: e.tensor_tensor(self.x(tt), s, self.gb_[:, D:], ALU.add), t)

        return [one(tt) for tt in range(2)]

    def rms_rows(self, src, groups, width, eps, ready, col=64):
        junk = self.junk[:, :width]
        ss, r = self.st[:, col:col + groups], self.st[:, col + groups:col + 2 * groups]
        for i in range(groups):
            t = self.a(lambda e, i=i: e.activation(junk, src[:, i * width:(i + 1) * width], ACT.Square,
                                                   accum_out=ss[:, i:i + 1]), ready)
        t = self.v(lambda e: e.tensor_scalar(ss, ss, 1.0 / width, eps, ALU.mult, ALU.add), t)
        return r, self.power(r, ss, groups, t)

    def rms_turn(self, gain, ready):
        xn = [self.scr.cut(D) for _ in range(2)]
        self.junk = self.scr.cut(D)
        done = []
        for tt in range(2):
            r, t = self.rms_rows(self.x(tt), 1, D, 1e-6, ready, col=64 + 8 * tt)
            done.append(self.v(lambda e, tt=tt, r=r: e.tensor_scalar(xn[tt], self.x(tt), r, None, ALU.mult), t))
        return self.turn(lambda tt: xn[tt], 8, done, scale=lambda k: self.vec(gain, k))

    def rows_load(self, stage, name, after):
        n = row_len(stage)
        src = self.d[name].partition_broadcast(128)
        return self.P.dma(self.d_row, lambda e: e.dma_start(self.rows[:, :n], src), after)

    def ln_load(self, name, after):
        src = self.d[name].partition_broadcast(128)
        return self.P.dma(self.d_ln, lambda e: e.dma_start(self.gb_[:, :], src), after)

    def begin(self):
        self.scr.at = 0
        return self.P.meet()

    def heads_turned(self, src, n, width, dst, ready, banks):
        todo = [(i, tt) for i in range(n) for tt in range(2)]
        toks = []
        for m, at in enumerate(range(0, len(todo), 4)):
            part = todo[at:at + 4]
            bank = banks[m % len(banks)]

            def fn(e, part=part, bank=bank):
                for j, (i, tt) in enumerate(part):
                    ins = e.transpose(bank.t[0:width, j * 128:(j + 1) * 128], src(tt, i), self.ident)
                return ins
            tok = self.pe(fn, ready, bank.free)
            i0 = part[0][0] * T
            out, ps = dst[0:width, i0:i0 + len(part) * 128], bank.t[0:width, :len(part) * 128]
            if m % 2 == 0:
                bank.free = self.a(lambda e, out=out, ps=ps: e.activation(out, ps, ACT.Copy), tok)
            else:
                bank.free = self.v(lambda e, out=out, ps=ps: e.tensor_copy(out, ps), tok)
            toks.append(bank.free)
        return toks

    def attention(self, units, ready):
        sc = [self.scr.cut(1024) for _ in range(2)]
        pt = [self.scr.cut(1024) for _ in range(2)]
        stok, ptok, otok = {}, {}, {}

        def scores(u):
            unit = units[u]
            banks = self.bank[0:2] if u % 2 == 0 else self.bank[2:4]
            H, nk = len(unit["heads"]), unit["nk"]
            per = 512 // nk

            def fn(e):
                for j in range(H):
                    out = banks[j // per].t[:, (j % per) * nk:(j % per + 1) * nk]
                    m = unit["scores"](e, out, unit["heads"][j])
                return m
            stok[u] = self.pe(fn, ready, banks[0].free, banks[1].free)

        def one(u, unit):
            H, nk, tt = len(unit["heads"]), unit["nk"], unit["tt"]
            per = 512 // nk
            banks = self.bank[0:2] if u % 2 == 0 else self.bank[2:4]
            S = sc[u % 2][:, :H * nk]
            S3 = r3(S, nk)
            free = ptok.get(u - 2)
            for b in range((H + per - 1) // per):
                hb = min(per, H - b * per)
                out = S3[:, b * per:b * per + hb, :]
                ps = r3(banks[b].t[:, :hb * nk], nk)
                mask = unit["mask"](b * per, hb)
                t = self.v(lambda e, out=out, ps=ps, mask=mask: (
                    e.tensor_scalar(out, ps, unit["scale"], None, ALU.mult) if mask is None else
                    e.scalar_tensor_tensor(out, ps, unit["scale"], mask, ALU.mult, ALU.add)), stok[u], free)
                banks[b].free = t
            if "shift" in unit:
                t = self.v(lambda e: e.tensor_tensor(S3, S3, bc(unit["shift"], 2, nk), ALU.add), t)
            c0 = 96 + 64 * (u % 2)
            m = self.st[:, c0:c0 + H]
            s = self.st[:, c0 + 16:c0 + 16 + H]
            x = self.st[:, c0 + 32:c0 + 32 + H]
            t = self.v(lambda e: e.tensor_reduce(m, S3, AXX, ALU.max), otok.get(u - 2))
            if "sink" in unit:
                t = self.v(lambda e: e.tensor_tensor(m, m, unit["sink"], ALU.max))
                t = self.v(lambda e: e.tensor_tensor(x, unit["sink"], m, ALU.subtract))
            t = self.v(lambda e: e.tensor_tensor(S3, S3, bc(m, 2, nk), ALU.subtract), t)
            t = self.a(lambda e: e.activation(S, S, ACT.Exp), t)
            if "sink" in unit:
                t = self.a(lambda e: e.activation(x, x, ACT.Exp), t)
            t = self.v(lambda e: e.tensor_reduce(s, S3, AXX, ALU.add), t)
            if "sink" in unit:
                t = self.v(lambda e: e.tensor_tensor(s, s, x, ALU.add), t)
            t = self.v(lambda e: e.reciprocal(s, s), t)
            src, G = S3, H
            if "lam" in unit:
                t = self.v(lambda e: e.tensor_scalar(s[:, 1:H:2], s[:, 1:H:2], unit["lam"], None, ALU.mult))
                t = self.v(lambda e: e.tensor_tensor(S3, S3, bc(s, 2, nk), ALU.mult))
                t = self.v(lambda e: e.tensor_tensor(S3[:, 0:H:2, :], S3[:, 0:H:2, :], S3[:, 1:H:2, :], ALU.subtract))
                src, G = S3[:, 0:H:2, :], H // 2
            nt = nk // 128
            PT = pt[u % 2]
            blocks = [(j, k) for j in range(G) for k in range(nt)]
            pts = []
            for n, at in enumerate(range(0, len(blocks), 4)):
                part = blocks[at:at + 4]
                bank = self.bank[4 + n]

                def fn(e, part=part, bank=bank):
                    for q, (j, k) in enumerate(part):
                        ins = e.transpose(bank.t[:, q * 128:(q + 1) * 128], src[:, j, k * 128:(k + 1) * 128], self.ident)
                    return ins
                tok = self.pe(fn, t, bank.free)
                out, ps = PT[:, at * 128:(at + len(part)) * 128], bank.t[:, :len(part) * 128]
                bank.free = self.a(lambda e, out=out, ps=ps: e.activation(out, ps, ACT.Copy), tok, otok.get(u - 2))
                pts.append(bank.free)
            ptok[u] = tok
            dv = unit["dv"]
            hp = 512 // dv
            for b in range((G + hp - 1) // hp):
                hb = min(hp, G - b * hp)
                bank = self.bank[6 + (u + b) % 2]

                def fn(e, b=b, hb=hb, bank=bank):
                    for j in range(b * hp, b * hp + hb):
                        for k in range(nt):
                            ins = e.matmul(bank.t[:, (j - b * hp) * dv:(j - b * hp + 1) * dv],
                                           PT[:, (j * nt + k) * 128:(j * nt + k + 1) * 128],
                                           unit["v"](j, k), start=(k == 0), stop=(k == nt - 1))
                    return ins
                otok[u] = self.pe(fn, pts, bank.free)
                out = r3(unit["out"], dv)[:, b * hp:b * hp + hb, :]
                ps = r3(bank.t[:, :hb * dv], dv)
                if "lam" in unit:
                    bank.free = self.v(lambda e, out=out, ps=ps: e.tensor_copy(out, ps), otok[u])
                else:
                    rr = bc(s[:, b * hp:b * hp + hb], 2, dv)
                    bank.free = self.v(lambda e, out=out, ps=ps, rr=rr: e.tensor_tensor(out, ps, rr, ALU.mult), otok[u])
            otok[u] = [otok[u], bank.free]
        scores(0)
        for u, unit in enumerate(units):
            if u + 1 < len(units):
                scores(u + 1)
            one(u, unit)
        return self.P.own("vector")

    def rope(self, x, H, half, cos, sin, after):
        n = H * 2 * half
        t1, t2 = self.rt[0][:, :n], self.rt[1][:, :n]
        v4 = lambda a: a.rearrange("p (h s f) -> p h s f", s=2, f=half)
        c = bc(bc(cos, 1, 2), 1, H)
        s = bc(bc(sin, 1, 2), 1, H)
        x4 = x.rearrange("p h (s f) -> p h s f", s=2)
        self.v(lambda e: e.tensor_tensor(v4(t1), x4, c, ALU.mult), after)
        self.v(lambda e: e.tensor_tensor(v4(t2), x4, s, ALU.mult))
        self.v(lambda e: e.tensor_tensor(x4[:, :, 0, :], v4(t1)[:, :, 0, :], v4(t2)[:, :, 1, :], ALU.subtract))
        return self.v(lambda e: e.tensor_tensor(x4[:, :, 1, :], v4(t1)[:, :, 1, :], v4(t2)[:, :, 0, :], ALU.add))

    def rotations(self):
        P = self.P
        n = 40
        pos, ang, k, r, b = (self.keep(2, I32), self.scr.cut(n), self.scr.cut(n), self.scr.cut(n), self.scr.cut(n))
        self.cos, self.sin = self.keep(n), self.keep(n)
        posf = self.keep(2)
        t = P.dma(self.d_late, lambda e: e.dma_start(pos, self.d["pos"]))
        t = self.v(lambda e: e.tensor_copy(posf, pos), t)
        for tt in range(2):
            t = self.v(lambda e, tt=tt: e.tensor_scalar(ang[:, tt * 20:(tt + 1) * 20], self.c("invf"), posf[:, tt:tt + 1],
                                                        None, ALU.mult), t, self.const_ready)
        self.v(lambda e: e.tensor_scalar(k, ang, 1.0 / (2 * math.pi), None, ALU.mult))
        self.v(lambda e: e.tensor_scalar(k, k, MAGIC, None, ALU.add))
        self.v(lambda e: e.tensor_scalar(k, k, -MAGIC, None, ALU.add))
        c1 = 6.28125
        c2 = float(np.float32(2 * math.pi - c1))
        c3 = 2 * math.pi - c1 - c2
        for c in (c1, c2, c3):
            self.v(lambda e, c=c: e.scalar_tensor_tensor(ang, k, -c, ang, ALU.mult, ALU.add))
        pi = float(np.nextafter(np.float32(math.pi), np.float32(0)))
        t = self.v(lambda e: e.tensor_scalar(r, ang, pi, -pi, ALU.min, ALU.max))
        self.a(lambda e: e.activation(self.sin, r, ACT.Sin), t)
        self.v(lambda e: e.tensor_scalar(ang, ang, math.pi / 2, None, ALU.add))
        self.v(lambda e: e.tensor_scalar(b, ang, math.pi, -2 * math.pi, ALU.is_gt, ALU.mult))
        self.v(lambda e: e.tensor_tensor(ang, ang, b, ALU.add))
        t = self.v(lambda e: e.tensor_scalar(ang, ang, pi, -pi, ALU.min, ALU.max))
        return self.a(lambda e: e.activation(self.cos, ang, ACT.Sin), t)

    def keep(self, n, dt=F32):
        a = self.kept_at
        self.kept_at += n
        ap = self.small[:, a:a + n]
        return ap.bitcast(dt) if dt != F32 else ap

    def begin_program(self):
        P = self.P
        self.kept_at = 0
        t = [P.dma(self.d_const, lambda e: e.dma_start(self.const[:, :], self.d["const"])),
             P.dma(self.d_const, lambda e: e.dma_start(self.vecs[:, :], self.d["vecs"]))]
        self.const_ready = t[-1]
        ln = self.ln_load("row_lnin", None)
        xs = [self.scr.cut(D) for _ in range(2)]
        t = None
        for tt in range(2):
            t = P.dma(self.d_x, lambda e, tt=tt: e.dma_start(xs[tt], self.d["x"][tt * 128:(tt + 1) * 128, :]))
        self.layer_norm(lambda tt: xs[tt], [t, self.const_ready], ln)
        self.rotations()

    def mixer(self, l):
        P, cut = self.P, self.scr.cut
        now = self.begin()
        rows = self.rows_load("mla", f"row_mla{l}", now)
        ln = self.ln_load(f"row_ln1{l}", now)
        R = lambda n: self.row("mla", n)
        proj = [cut(IN_COLS) for _ in range(2)]
        B = self.bank
        lam_init = 0.8 - 0.6 * math.exp(-0.3 * l)
        ready = self.turn(self.x, 8, None)
        col = lambda tt, i, j=None: proj[tt][:, OFF[i]:OFF[(j or i) + 1] if (j or i) + 1 < 10 else IN_COLS]

        def to_proj(tt, n0, w, ps, tok):
            out = proj[tt][:, n0:n0 + w]
            if tt == 0:
                return self.a(lambda e: e.activation(out, ps, ACT.Copy), tok)
            return self.v(lambda e: e.tensor_copy(out, ps), tok)
        self.moving(f"w_in{l}", D, IN_COLS, [(B[0], B[1]), (B[2], B[3])], to_proj, ready)
        used = P.own("tensor")
        done = [P.own("scalar"), P.own("vector")]
        lam = self.keep(8) if l == 0 else self.lam
        self.lam = lam
        prod = cut(64)
        a, b = row_at("mla", "lq1")[0], row_at("mla", "lk1")[0]
        self.v(lambda e: e.tensor_tensor(prod, self.rows[:, a:a + 64], self.rows[:, b:b + 64], ALU.mult), rows)
        t = self.v(lambda e: e.tensor_reduce(lam[:, 0:2], r3(prod, 32), AXX, ALU.add))
        t = self.a(lambda e: e.activation(lam[:, 0:2], lam[:, 0:2], ACT.Exp), t)
        t = self.v(lambda e: e.tensor_tensor(lam[:, 2:3], lam[:, 0:1], lam[:, 1:2], ALU.subtract), t)
        t = self.v(lambda e: e.tensor_scalar(lam[:, 2:3], lam[:, 2:3], lam_init, None, ALU.add))
        mark = self.scr.at
        self.junk = cut(384)
        for tt in range(2):
            for i, g, w, c in ((0, "qg", 384, 64), (1, "kvg", 256, 72)):
                def one(tt=tt, i=i, g=g, w=w, c=c):
                    x = col(tt, i)
                    r, t = self.rms_rows(x, 1, w, 1e-6, [done, rows], col=c + 16 * tt)
                    self.v(lambda e: e.scalar_tensor_tensor(x, x, r, R(g), ALU.mult, ALU.mult), t)
                one()
        done = P.own("vector")
        ready = self.turn(lambda tt: col(tt, 0), 3, done, free=used)
        q = [cut(768) for _ in range(2)]

        def to_q(tt, n0, w, ps, tok):
            out = q[tt][:, n0:n0 + w]
            if tt == 0:
                return self.a(lambda e: e.activation(out, ps, ACT.Copy), tok)
            return self.v(lambda e: e.tensor_copy(out, ps), tok)
        self.moving(f"uq{l}", 384, 768, [(B[0], B[1]), (B[2], B[3])], to_q, ready)
        used = P.own("tensor")
        ready = self.turn(lambda tt: col(tt, 1), 2, done, free=used)
        kf = [cut(768) for _ in range(2)]
        vv = [cut(512) for _ in range(2)]

        def to_kv(tt, n0, w, ps, tok):
            h0 = n0 // 128
            p4 = r3(ps, 128)
            out_k = r3(kf[tt], 96)[:, h0:h0 + 4, 0:64]
            out_v = r3(vv[tt], 64)[:, h0:h0 + 4, :]
            t = self.a(lambda e: e.activation(out_k, p4[:, :, 0:64], ACT.Copy), tok)
            return self.v(lambda e: e.tensor_copy(out_v, p4[:, :, 64:128]), t)
        self.moving(f"ukv{l}", 256, 1024, [(B[0], B[1]), (B[2], B[3])], to_kv, ready)
        self.rt = [cut(512), cut(512)]
        for tt in range(2):
            cm, sm = self.cos[:, tt * 20:tt * 20 + 16], self.sin[:, tt * 20:tt * 20 + 16]
            cd, sd = self.cos[:, tt * 20 + 16:tt * 20 + 20], self.sin[:, tt * 20 + 16:tt * 20 + 20]
            self.rope(r3(q[tt], 96)[:, :, 64:96], 8, 16, cm, sm, P.own("scalar"))
            self.rope(col(tt, 2).unsqueeze(1), 1, 16, cm, sm, None)
            self.v(lambda e, tt=tt: e.tensor_copy(r3(kf[tt], 96)[:, :, 64:96], bc(col(tt, 2), 1, 8)))
            self.rope(r3(col(tt, 3), 32)[:, :, 0:8], 8, 4, cd, sd, None)
            self.rope(r3(col(tt, 4), 32)[:, :, 0:8], 8, 4, cd, sd, None)
        roped = P.own("vector")
        now = self.P.meet()
        qT, kT = cut(8 * T), cut(8 * T)
        o = [cut(D) for _ in range(2)]
        mark = self.scr.at
        self.heads_turned(lambda tt, i: q[tt][:, i * 96:(i + 1) * 96], 8, 96, qT, roped, B[0:4])
        self.heads_turned(lambda tt, i: kf[tt][:, i * 96:(i + 1) * 96], 8, 96, kT, roped, B[0:4])
        ready = [P.own("scalar"), P.own("vector")]

        def unit(tt, heads, off, **kw):
            nk = 128 * (tt + 1)
            m = self.c(kw.pop("m"))[:, 256 - nk:]
            G = len(heads)
            ng = G // (2 if "lam" in kw else 1)
            h0 = heads[0] // (2 if "lam" in kw else 1)
            return dict(tt=tt, heads=heads, nk=nk, dv=64, mask=lambda b, n: bc(m, 1, n),
                        out=o[tt][:, off + h0 * 64:off + (h0 + ng) * 64], **kw)

        def mla_scores(tt):
            def f(e, out, h):
                nk = 128 * (tt + 1)
                return e.matmul(out, qT[0:96, h * T + tt * 128:h * T + tt * 128 + 128], kT[0:96, h * T:h * T + nk],
                                start=True, stop=True)
            return f

        def vals(src, h0):
            return lambda j, k: src(k)[:, (h0 + j) * 64:(h0 + j + 1) * 64]
        units = []
        for tt, hs in ((0, range(8)), (1, range(4)), (1, range(4, 8))):
            units.append(unit(tt, list(hs), 0, m="mchunk", scale=96 ** -0.5, scores=mla_scores(tt),
                              v=vals(lambda k: vv[k], hs[0])))
        self.attention(units, ready)
        self.P.meet()
        self.scr.at = mark
        self.heads_turned(lambda tt, i: col(tt, 3)[:, i * 32:(i + 1) * 32], 8, 32, qT, None, B[0:4])
        self.heads_turned(lambda tt, i: col(tt, 4)[:, i * 32:(i + 1) * 32], 8, 32, kT, None, B[0:4])
        ready = [P.own("scalar"), P.own("vector")]

        def diff_scores(tt):
            def f(e, out, h):
                nk = 128 * (tt + 1)
                return e.matmul(out, qT[0:32, h * T + tt * 128:h * T + tt * 128 + 128], kT[0:32, h * T:h * T + nk],
                                start=True, stop=True)
            return f
        units = []
        for tt, hs in ((0, range(8)), (1, range(4)), (1, range(4, 8))):
            units.append(unit(tt, list(hs), 512, m="mchunk", scale=32 ** -0.5, scores=diff_scores(tt),
                              v=vals(lambda k: col(k, 5), hs[0] // 2), lam=lam[:, 2:3]))
        self.attention(units, ready)
        self.P.meet()
        self.scr.at = mark
        lf = [self.st[:, 0:4], self.st[:, 4:8]]
        cum = [self.st[:, 8:12], self.st[:, 12:16]]
        tmp = self.st[:, 16:24]
        lb = [cut(512) for _ in range(2)]
        self.heads_turned(lambda tt, i: col(tt, 6)[:, i * 64:(i + 1) * 64], 4, 64, qT, None, B[0:4])
        self.heads_turned(lambda tt, i: col(tt, 7)[:, i * 64:(i + 1) * 64], 4, 64, kT, None, B[0:4])
        ready = [P.own("scalar"), P.own("vector")]
        for tt in range(2):
            self.v(lambda e, tt=tt: e.tensor_tensor(lf[tt], col(tt, 9), R("fb"), ALU.add))
        both = self.st[:, 0:8]
        t = self.v(lambda e: e.tensor_scalar(tmp, both, 0.0, None, ALU.min))
        t = self.a(lambda e: e.activation(both, both, ACT.Abs), t)
        t = self.a(lambda e: e.activation(both, both, ACT.Exp, scale=-1.0))
        t = self.a(lambda e: e.activation(both, both, ACT.Ln, bias=1.0))
        t = self.v(lambda e: e.tensor_tensor(both, tmp, both, ALU.subtract), t)
        for tt in range(2):
            t = self.v(lambda e, tt=tt: e.tensor_scalar(r3(lb[tt], 128), bc(lf[tt], 2, 128), -8.0, None, ALU.mult))
        bank = B[6]

        def cums(e):
            e.matmul(bank.t[:, 0:4], self.tri, lf[0], start=True, stop=True)
            e.matmul(bank.t[:, 4:8], self.ones, lf[0], start=True, stop=False)
            return e.matmul(bank.t[:, 4:8], self.tri, lf[1], start=False, stop=True)
        t = self.pe(cums, t, bank.free)
        t = self.v(lambda e: e.tensor_copy(self.st[:, 8:16], bank.t[:, 0:8]), t)
        bank.free = t
        ready = [ready, t]

        def fox_scores(tt):
            def f(e, out, h):
                nk = 128 * (tt + 1)
                e.matmul(out, qT[0:64, h * T + tt * 128:h * T + tt * 128 + 128], kT[0:64, h * T:h * T + nk],
                         start=True, stop=False)
                m = e.matmul(out, lb[0][:, h * 128:(h + 1) * 128], self.zto[:, 128:128 + nk], start=False, stop=(tt == 0))
                if tt:
                    m = e.matmul(out, lb[1][:, h * 128:(h + 1) * 128], self.zto[:, 0:256], start=False, stop=True)
                return m
            return f
        units = []
        for tt, hs in ((0, range(4)), (1, range(4))):
            units.append(unit(tt, list(hs), 768, m="mframe", scale=0.125, scores=fox_scores(tt),
                              v=vals(lambda k: col(k, 8), 0), shift=cum[tt]))
        done = self.attention(units, ready)
        self.junk = cut(64)
        for tt in range(2):
            def one(tt=tt):
                x = o[tt][:, 512:768]
                r, t = self.rms_rows(x, 4, 64, 1e-6, done, col=64 + 8 * tt)
                t = self.v(lambda e: e.tensor_tensor(r3(x, 64), r3(x, 64), bc(r, 2, 64), ALU.mult), t)
                return self.v(lambda e: e.scalar_tensor_tensor(r3(x, 64), r3(x, 64), 1.0 - lam_init,
                                                               bc(R("subln"), 1, 4), ALU.mult, ALU.mult))
            one()
        self.P.meet()
        ready = self.turn(lambda tt: o[tt], 8, None)
        y = [kT[:, 0:D], kT[:, D:2 * D]]

        def to_y(tt, n0, w, ps, tok):
            return self.v(lambda e: e.scalar_tensor_tensor(y[tt][:, n0:n0 + w], self.x(tt)[:, n0:n0 + w], ALPHA, ps,
                                                           ALU.mult, ALU.add), tok)
        self.moving(f"w_out{l}", D, D, [(B[0], B[1]), (B[2], B[3])], to_y, ready)
        self.layer_norm(lambda tt: y[tt], P.own("vector"), ln)

    def moe(self, l):
        P, cut = self.P, self.scr.cut
        now = self.begin()
        rows = self.rows_load("moe", "row_moe", now)
        ln = self.ln_load(f"row_ln2{l}", now)
        B = self.bank
        rw = cut(128)
        rt = P.dma(self.d_x, lambda e: e.dma_start(rw, self.d["router"]), now)
        es = cut(16 * 128)
        late = P.dma(self.d_late, lambda e: e.dma_start(es[0:16, :], self.d["esel"]), now)
        xT = cut(8 * T)
        gb = cut(NE * T)
        toks = []
        for n in range(4):
            bank = B[4 + n]

            def fn(e, n=n, bank=bank):
                for j in range(2):
                    for tt in range(2):
                        m = e.transpose(bank.t[:, j * T + tt * 128:j * T + tt * 128 + 128],
                                        self.x(tt)[:, (2 * n + j) * 128:(2 * n + j + 1) * 128], self.ident)
                return m
            t = self.pe(fn, bank.free)
            sl = slice(n * 512, (n + 1) * 512)
            t = self.v(lambda e, sl=sl, bank=bank: e.tensor_copy(xT[:, sl], bank.t[:, :]), t)
            bank.free = t
            h = self.a(lambda e, sl=sl: e.activation(self.thi[:, sl], xT[:, sl], ACT.Copy), t)
            toks.append(self.v(lambda e, sl=sl: e.tensor_tensor(self.tlo[:, sl], xT[:, sl],
                                                                self.thi[:, sl].bitcast(F32), ALU.subtract), h))
        bank = B[0]

        def route(e):
            for tt in range(2):
                for k in range(8):
                    m = e.matmul(bank.t[:, tt * 16:tt * 16 + 16], xT[:, k * T + tt * 128:k * T + tt * 128 + 128],
                                 rw[:, k * 16:(k + 1) * 16], start=(k == 0), stop=(k == 7))
            return m
        t = self.pe(route, toks, rt, bank.free)
        sc, bi, t1, t2, t3 = (cut(32) for _ in range(5))
        g1, g2, g3, g4 = (cut(16) for _ in range(4))
        oh = cut(32)
        t = self.a(lambda e: e.activation(sc, bank.t[:, 0:32], ACT.Sigmoid), t)
        bank.free = t
        V = self.v
        TT = lambda o_, a_, b_, op: V(lambda e: e.tensor_tensor(o_, a_, b_, op))
        V(lambda e: e.tensor_tensor(r3(bi, 16), r3(sc, 16), bc(self.row("moe", "rb"), 1, 2), ALU.add), t, rows)
        b4 = r3(bi, 2)
        TT(g1, b4[:, :, 0], b4[:, :, 1], ALU.max)
        TT(g2, b4[:, :, 0], b4[:, :, 1], ALU.min)
        h1, h2 = r3(g1, 2), r3(g2, 2)
        top, a1, a2 = g3[:, 0:8], g3[:, 8:16], g4[:, 0:8]
        TT(top, h1[:, :, 0], h1[:, :, 1], ALU.max)
        TT(a1, h1[:, :, 0], h1[:, :, 1], ALU.min)
        TT(a2, h2[:, :, 0], h2[:, :, 1], ALU.max)
        TT(a1, a1, a2, ALU.max)
        TT(top, top, a1, ALU.add)
        mx = g4[:, 8:10]

        def first_max(out, x, c, n):
            V(lambda e: e.tensor_reduce(mx, r3(x, n), AXX, ALU.max))
            V(lambda e: e.tensor_tensor(r3(out, n), r3(x, n), bc(mx, 2, n), ALU.is_equal))
            V(lambda e: e.tensor_tensor(r3(out, n), r3(out, n), bc(c, 1, 2), ALU.mult))
            V(lambda e: e.tensor_reduce(mx, r3(out, n), AXX, ALU.max))
            V(lambda e: e.tensor_tensor(r3(out, n), r3(out, n), bc(mx, 2, n), ALU.is_equal))
        grp = g1[:, 0:8]
        first_max(grp, top, self.c("c4"), 4)
        t38 = g2[:, 0:8]
        V(lambda e: e.tensor_scalar(t38, grp, -NEG, NEG, ALU.mult, ALU.add))
        V(lambda e: e.tensor_tensor(r3(t1, 4), r3(bi, 4), bc(grp, 2, 4), ALU.mult))
        V(lambda e: e.tensor_tensor(r3(t1, 4), r3(t1, 4), bc(t38, 2, 4), ALU.add))
        first_max(t2, t1, self.c("c16"), 16)
        V(lambda e: e.scalar_tensor_tensor(t1, t2, 3 * NEG, t1, ALU.mult, ALU.add))
        first_max(t3, t1, self.c("c16"), 16)
        TT(t2, t2, t3, ALU.add)
        TT(t2, t2, sc, ALU.mult)
        V(lambda e: e.tensor_reduce(mx, r3(t2, 16), AXX, ALU.add))
        V(lambda e: e.reciprocal(mx, mx))
        t = V(lambda e: e.tensor_tensor(r3(oh, 16), r3(t2, 16), bc(mx, 2, 16), ALU.mult))
        gt = cut(T)

        def tg(e):
            for tt in range(2):
                m = e.transpose(bank.t[0:16, tt * 128:(tt + 1) * 128], oh[:, tt * 16:(tt + 1) * 16], self.ident)
            return m
        t = self.pe(tg, t, bank.free)
        t = V(lambda e: e.tensor_copy(gt[0:16, :], bank.t[0:16, 0:T]), t)
        bank.free = t
        gate_tok = {}
        for n in range(8):
            bk = B[n % 4]

            def fn(e, n=n, bk=bk):
                for j in range(2):
                    i = 2 * n + j
                    m = e.matmul(bk.t[:, j * T:(j + 1) * T], es[0:16, i * 128:(i + 1) * 128], gt[0:16, :],
                                 start=True, stop=True)
                return m
            t2_ = self.pe(fn, t, late, bk.free)
            out = gb[:, n * 512:(n + 1) * 512]
            bk.free = V(lambda e, out=out, bk=bk: e.tensor_copy(out, bk.t[:, :]), t2_)
            gate_tok[n] = bk.free
        last = self.gated(f"exp{l}", plan_experts(), toks + [P.own("vector")],
                          gate=lambda f: gb[:, (f // 4) * T:(f // 4 + 1) * T])
        y = [xT[:, 0:D], xT[:, D:2 * D]]
        for tt in range(2):
            for half in range(2):
                bk = B[tt * 2 + half]
                sl = slice(half * 512, half * 512 + 512)
                bk.free = V(lambda e, tt=tt, sl=sl, bk=bk: e.scalar_tensor_tensor(
                    y[tt][:, sl], self.x(tt)[:, sl], ALPHA, bk.t[:, :], ALU.mult, ALU.add), last)
        self.layer_norm(lambda tt: y[tt], P.own("vector"), ln)

    def ffn(self, name, gain):
        self.begin()
        ready = self.rms_turn(gain, None)
        last = self.gated(name, plan_gated(F // 128), ready)
        for tt in range(2):
            for half in range(2):
                bk = self.bank[tt * 2 + half]
                x = self.x(tt)[:, half * 512:half * 512 + 512]
                bk.free = self.v(lambda e, x=x, bk=bk: e.scalar_tensor_tensor(x, bk.t[:, :], 0.5, x, ALU.mult, ALU.add),
                                 last)

    def add_moving(self, name, ready, bias=None):
        B = self.bank

        def evac(tt, n0, w, ps, tok):
            x = self.x(tt)[:, n0:n0 + w]
            t = self.v(lambda e: e.tensor_tensor(x, x, ps, ALU.add), tok)
            if bias is not None:
                t = self.v(lambda e: e.tensor_tensor(x, x, bias[:, n0:n0 + w], ALU.add))
            return t
        return self.moving(name, D, D, [(B[0], B[1]), (B[2], B[3])], evac, ready)

    def memory(self):
        P, cut = self.P, self.scr.cut
        now = self.begin()
        rows = self.rows_load("mem", "row_mem", now)
        mm = [cut(D) for _ in range(2)]
        t = None
        for tt in range(2):
            t = P.dma(self.d_x, lambda e, tt=tt: e.dma_start(mm[tt], self.d["mem"][tt * 128:(tt + 1) * 128, :]), now)
        self.junk = cut(D)
        done = []
        for tt in range(2):
            def one(tt=tt):
                r, t2 = self.rms_rows(mm[tt], 1, D, 1e-6, t, col=64 + 8 * tt)
                return self.v(lambda e: e.tensor_scalar(mm[tt], mm[tt], r, None, ALU.mult), t2)
            done.append(one())
        ready = self.turn(lambda tt: mm[tt], 8, done, scale=lambda k: self.vec("mem_norm", k))
        mk = [cut(D) for _ in range(2)]
        B = self.bank

        def evac(tt, n0, w, ps, tok):
            if n0 < D:
                return self.a(lambda e: e.activation(mk[tt][:, n0:n0 + w], ps, ACT.Copy), tok)
            return self.v(lambda e: e.tensor_copy(self.memv[tt][:, n0 - D:n0 - D + w], ps), tok)
        self.moving("mem_wkv", D, 2 * D, [(B[0], B[1]), (B[2], B[3])], evac, ready)
        done = [P.own("scalar"), P.own("vector")]
        self.head_norm(mk, 4, 256, self.row("mem", "kn"), [done, rows])
        self.heads_turned(lambda tt, i: mk[tt][:, i * 128:(i + 1) * 128], 8, 128, self.memk, P.own("vector"), B[4:8])

    def head_norm(self, x, H, w, gain, ready, base=96):
        for tt in range(2):
            def one(tt=tt):
                a = x[tt]
                r, t = self.rms_rows(a, H, w, 1e-6, ready, col=base + 32 * tt)
                self.v(lambda e: e.tensor_tensor(r3(a, w), r3(a, w), bc(r, 2, w), ALU.mult), t)
                return self.v(lambda e: e.tensor_tensor(r3(a, w), r3(a, w), bc(gain, 1, H), ALU.mult))
            one()

    def cross(self, l):
        P, cut = self.P, self.scr.cut
        now = self.begin()
        rows = self.rows_load("xat", f"row_xat{l}", now)
        ready = self.rms_turn(f"xattn_norm{l}", None)
        B = self.bank
        q = [cut(D) for _ in range(2)]

        def evac(tt, n0, w, ps, tok):
            return self.a(lambda e: e.activation(q[tt][:, n0:n0 + w], ps, ACT.Copy), tok)
        self.moving(f"xwq{l}", D, D, [(B[0], B[1]), (B[2], B[3])], evac, ready)
        self.head_norm(q, 4, 256, self.row("xat", "qn"), [P.own("scalar"), rows])
        qT = cut(8 * T)
        self.heads_turned(lambda tt, i: q[tt][:, i * 128:(i + 1) * 128], 8, 128, qT, P.own("vector"), B[4:8])
        ready = [P.own("scalar"), P.own("vector")]

        def scores(tt):
            def f(e, out, h):
                for c in range(2):
                    i = 2 * h + c
                    m = e.matmul(out, qT[:, i * T + tt * 128:i * T + tt * 128 + 128], self.memk[:, i * T:(i + 1) * T],
                                 start=(c == 0), stop=(c == 1))
                return m
            return f
        o = [cut(D) for _ in range(2)]
        units = [dict(tt=tt, heads=[0, 1, 2, 3], nk=256, dv=256, mask=lambda b, n: None, scale=1 / 16.0,
                      scores=scores(tt), out=o[tt], v=lambda j, k: self.memv[k][:, j * 256:(j + 1) * 256])
                 for tt in range(2)]
        done = self.attention(units, ready)
        ready = self.turn(lambda tt: o[tt], 8, done)
        self.add_moving(f"xwo{l}", ready)

    def swa(self):
        P, cut = self.P, self.scr.cut
        now = self.begin()
        rows = self.rows_load("swa", "row_swa", now)
        ali = cut(16 * T)
        late = P.dma(self.d_late, lambda e: e.dma_start(ali, self.d["alibi"]), now)
        R = lambda n: self.row("swa", n)
        mark = self.scr.at
        ready = self.rms_turn("mix_norm1", None)
        self.P.meet()
        self.scr.at = mark
        self.junk = cut(64)
        B = self.bank
        qkv = [cut(1536) for _ in range(2)]

        def evac(tt, n0, w, ps, tok):
            return self.v(lambda e: e.tensor_tensor(qkv[tt][:, n0:n0 + w], ps, R("bqkv")[:, n0:n0 + w], ALU.add), tok, rows)
        self.moving("wqkv", D, 1536, [(B[0], B[1]), (B[2], B[3])], evac, ready)
        done = P.own("vector")
        self.head_norm([x[:, 0:1024] for x in qkv], 16, 64, R("qn"), [done], base=96)
        self.head_norm([x[:, 1024:1280] for x in qkv], 4, 64, R("kn"), [done], base=160)
        qT, kT = cut(16 * T), cut(4 * T)
        t = P.own("vector")
        self.heads_turned(lambda tt, i: qkv[tt][:, i * 64:(i + 1) * 64], 16, 64, qT, t, B[4:8])
        self.heads_turned(lambda tt, i: qkv[tt][:, 1024 + i * 64:1024 + (i + 1) * 64], 4, 64, kT, t, B[4:8])
        ready = [P.own("scalar"), P.own("vector"), late]
        o = [cut(D) for _ in range(2)]

        def scores(tt):
            def f(e, out, h):
                nk = 128 * (tt + 1)
                return e.matmul(out, qT[0:64, h * T + tt * 128:h * T + tt * 128 + 128],
                                kT[0:64, (h // 4) * T:(h // 4) * T + nk], start=True, stop=True)
            return f
        ali3 = r3(ali, T)
        units = []
        for tt, n in ((0, 8), (1, 4)):
            for h0 in range(0, 16, n):
                units.append(dict(
                    tt=tt, heads=list(range(h0, h0 + n)), nk=128 * (tt + 1), dv=64, scale=0.125, scores=scores(tt),
                    mask=lambda b, c, h0=h0, tt=tt: ali3[:, h0 + b:h0 + b + c, 128 * (1 - tt):],
                    sink=R("sink")[:, h0:h0 + n], out=o[tt][:, h0 * 64:(h0 + n) * 64],
                    v=lambda j, k, h0=h0: qkv[k][:, 1280 + (h0 + j) // 4 * 64:1280 + (h0 + j) // 4 * 64 + 64]))
        done = self.attention(units, ready)
        ready = self.turn(lambda tt: o[tt], 8, done)
        self.add_moving("wo", ready, bias=R("bo"))

    def ssd(self):
        P, cut = self.P, self.scr.cut
        now = self.begin()
        rows = self.rows_load("ssd", "row_ssd", now)
        R = lambda n: self.row("ssd", n)
        B = self.bank
        V, A, G = self.v, self.a, self.g
        h32 = cut(8 * T)
        mark = self.scr.at
        xn = [cut(D) for _ in range(2)]
        self.junk = cut(D)
        done = []
        for tt in range(2):
            r, t = self.rms_rows(self.x(tt), 1, D, 1e-6, None, col=64 + 8 * tt)
            done.append(V(lambda e, tt=tt, r=r: e.tensor_scalar(xn[tt], self.x(tt), r, None, ALU.mult), t))
        for n in range(4):
            bank = B[4 + n]

            def fn(e, n=n, bank=bank):
                for j in range(2):
                    for tt in range(2):
                        m = e.transpose(bank.t[:, j * T + tt * 128:j * T + tt * 128 + 128],
                                        xn[tt][:, (2 * n + j) * 128:(2 * n + j + 1) * 128], self.ident)
                return m
            t = self.pe(fn, done, bank.free)
            for j in range(2):
                k = 2 * n + j
                t = V(lambda e, k=k, j=j, bank=bank: e.tensor_scalar(
                    h32[:, k * T:(k + 1) * T], bank.t[:, j * T:(j + 1) * T], self.vec("mix_norm0", k), None, ALU.mult), t)
            bank.free = t

        def parts(after):
            t = A(lambda e: e.activation(self.thi[:, :], h32, ACT.Copy), after)
            return V(lambda e: e.tensor_tensor(self.tlo[:, :], h32, self.thi[:, :].bitcast(F32), ALU.subtract), t, after)
        ready = parts(P.own("vector"))
        self.P.meet()
        self.scr.at = mark
        u = [cut(D) for _ in range(2)]
        bands = cut(8 * T)
        late = P.dma(self.d_late, lambda e: e.dma_start(bands, self.d["bands"]), now, P.own("vector"), P.own("scalar"))

        def to_u(tt, n0, w, ps, tok):
            if tt == 0:
                return A(lambda e: e.activation(u[tt][:, n0:n0 + w], ps, ACT.Copy), tok)
            return V(lambda e: e.tensor_copy(u[tt][:, n0:n0 + w], ps), tok)
        self.moving("pool_in", D, D, [(B[0], B[1]), (B[2], B[3])], to_u, ready)
        used = P.own("tensor")
        done = [P.own("scalar"), P.own("vector"), late]
        bnd = bands.rearrange("p (s w t) -> p s w t", s=2, w=4)
        toks = []
        for w in range(4):
            bank = B[4 + w]

            def fn(e, w=w, bank=bank):
                for c in range(2):
                    for s in range(2):
                        m = e.matmul(bank.t[:, c * T:(c + 1) * T], u[s][:, w * 256 + c * 128:w * 256 + (c + 1) * 128],
                                     bnd[:, s, w, :], start=(s == 0), stop=(s == 1))
                return m
            t = self.pe(fn, done, bank.free)
            sl = slice(w * 512, (w + 1) * 512)
            t = A(lambda e, sl=sl, bank=bank: e.activation(self.thi[:, sl], bank.t[:, :], ACT.Copy), t, used)
            t = V(lambda e, sl=sl, bank=bank: e.tensor_tensor(self.tlo[:, sl], bank.t[:, :],
                                                              self.thi[:, sl].bitcast(F32), ALU.subtract), t)
            bank.free = t
            toks.append(t)

        def pools(e, hi, lo):
            for w in range(4):
                for o_ in range(2):
                    out = B[w].t[:, o_ * T:(o_ + 1) * T]
                    for k in range(2):
                        ws = slice(((w * 2 + o_) * 2 + k) * 128, ((w * 2 + o_) * 2 + k + 1) * 128)
                        xs = slice((w * 2 + k) * T, (w * 2 + k + 1) * T)
                        e.matmul(out, hi[:, ws], self.thi[:, xs], start=(k == 0), stop=False)
                        e.matmul(out, hi[:, ws], self.tlo[:, xs], start=False, stop=False)
                        m = e.matmul(out, lo[:, ws], self.thi[:, xs], start=False, stop=(k == 1))
            return m
        tok = self.chunk("pool_w", pools, toks, [b.free for b in B[0:4]])
        done = []
        for w in range(4):
            for o_ in range(2):
                k = 2 * w + o_
                ps, sl = B[w].t[:, o_ * T:(o_ + 1) * T], slice(k * T, (k + 1) * T)
                sc = self.vec("pool_scale", k)
                t = A(lambda e, ps=ps, sl=sl, sc=sc: e.activation(self.thi[:, sl], ps, ACT.Copy, scale=sc), tok)
            for o_ in range(2):
                k = 2 * w + o_
                ps, sl = B[w].t[:, o_ * T:(o_ + 1) * T], slice(k * T, (k + 1) * T)
                sc = self.vec("pool_scale", k)
                t = V(lambda e, ps=ps, sl=sl, sc=sc: e.scalar_tensor_tensor(
                    self.tlo[:, sl], ps, sc, self.thi[:, sl].bitcast(F32), ALU.mult, ALU.subtract), t)
            B[w].free = t
            done.append(t)
        self.add_moving("out_pool", done)
        ready = parts([P.own("tensor")])
        self.P.meet()
        self.scr.at = mark
        U = cut(12 * 260).rearrange("p (c t) -> p c t", t=260)
        cv = cut(12 * T)
        z0 = V(lambda e: e.memset(U[:, :, 0:4], 0.0))
        conv = {}
        for f in range(6):
            bank = B[f % 4]
            tok = self.pair_product("ssd_xbc", bank, ready)
            t = A(lambda e, f=f, bank=bank: e.activation(U[:, 2 * f:2 * f + 2, 4:260], r3(bank.t[:, :], T), ACT.Copy), tok)
            bank.free = t
            for c in (2 * f, 2 * f + 1):
                out = cv[:, c * T:(c + 1) * T]
                V(lambda e, c=c, out=out: e.tensor_scalar(out, U[:, c, 4:260], self.vec("conv_w", 36 + c), None, ALU.mult),
                  t, z0)
                for k in (2, 1, 0):
                    t2 = V(lambda e, c=c, out=out, k=k: e.scalar_tensor_tensor(
                        out, U[:, c, 1 + k:257 + k], self.vec("conv_w", 12 * k + c), out, ALU.mult, ALU.add))
                conv[c] = A(lambda e, c=c, out=out: e.activation(out, out, ACT.Silu, bias=self.vec("conv_b", c)), t2)
        z = [h32[:, 0:D], h32[:, D:2 * D]]
        dtr = [self.st[:, 0:16], self.st[:, 16:32]]

        def to_z(tt, n0, w, ps, tok):
            if n0 < D:
                return A(lambda e: e.activation(z[tt][:, n0:n0 + w], ps, ACT.Silu), tok)
            return V(lambda e: e.tensor_copy(dtr[tt], ps), tok)
        self.moving("ssd_z", D, D + 16, [(B[0], B[1]), (B[2], B[3])], to_z, ready)
        self.P.meet()
        self.scr.at = mark
        xs = [cut(D) for _ in range(2)]
        cut(12 * 260 - 2 * D)
        cut(12 * T)
        both, tmp, ea = self.st[:, 0:32], self.st[:, 32:64], self.st[:, 64:80]
        dt = dtr
        V(lambda e: e.tensor_tensor(r3(both, 16), r3(both, 16), bc(R("dtb"), 1, 2), ALU.add), rows)
        t = V(lambda e: e.tensor_scalar(tmp, both, 0.0, None, ALU.max))
        A(lambda e: e.activation(both, both, ACT.Abs), t)
        A(lambda e: e.activation(both, both, ACT.Exp, scale=-1.0))
        A(lambda e: e.activation(both, both, ACT.Ln, bias=1.0))
        t = A(lambda e: e.activation(ea, R("alog"), ACT.Exp))
        V(lambda e: e.tensor_tensor(both, both, tmp, ALU.add), t)
        V(lambda e: e.tensor_scalar(ea, ea, -1.0, None, ALU.mult))
        adt = self.st[:, 80:112]
        t = V(lambda e: e.tensor_tensor(r3(adt, 16), r3(both, 16), bc(ea, 1, 2), ALU.mult))
        bank = B[4]
        acs, dfs, dte = self.st[:, 112:144], self.st[:, 144:160], self.st[:, 160:176]

        def cums(e):
            e.matmul(bank.t[:, 0:16], self.tri, adt[:, 0:16], start=True, stop=True)
            e.matmul(bank.t[:, 16:32], self.tri, adt[:, 16:32], start=True, stop=True)
            return e.matmul(bank.t[:, 32:48], self.ones, adt[:, 0:16], start=True, stop=True)
        t = self.pe(cums, t, bank.free)
        V(lambda e: e.tensor_copy(acs, bank.t[:, 0:32]), t)
        bank.free = V(lambda e: e.tensor_tensor(dte, bank.t[:, 32:48], acs[:, 0:16], ALU.subtract))
        t = P.own("vector")
        A(lambda e: e.activation(dte, dte, ACT.Exp), t)
        t_exp = A(lambda e: e.activation(dfs, acs[:, 16:32], ACT.Exp))
        Bt = cut(256)
        for n in range(4):
            bk = B[5 + n % 3]
            tt, half = n // 2, n % 2

            def fn(e, tt=tt, half=half, bk=bk):
                for j in range(4):
                    c = half * 4 + j
                    m = e.transpose(bk.t[:, j * 128:(j + 1) * 128], cv[:, c * T + tt * 128:c * T + tt * 128 + 128],
                                    self.ident)
                return m
            t = self.pe(fn, bk.free)
            bk.free = A(lambda e, tt=tt, half=half, bk=bk: e.activation(
                xs[tt][:, half * 512:half * 512 + 512], bk.t[:, :], ACT.Copy), t)
        bk = B[5]

        def fn(e):
            for g in range(2):
                m = e.transpose(bk.t[:, g * 128:(g + 1) * 128], cv[:, (8 + g) * T:(8 + g) * T + 128], self.ident)
            return m
        t = self.pe(fn, bk.free)
        bk.free = A(lambda e: e.activation(Bt, bk.t[:, 0:256], ACT.Copy), t)
        t = P.own("scalar")
        xr = [cut(D) for _ in range(2)]
        xd = cut(D)
        for tt in range(2):
            V(lambda e, tt=tt: e.tensor_tensor(r3(xr[tt], 64), r3(xs[tt], 64), bc(dt[tt], 2, 64), ALU.mult), t)
        xready = V(lambda e: e.tensor_tensor(r3(xd, 64), r3(xr[0], 64), bc(dte, 2, 64), ALU.mult), t_exp)
        sts = cut(D)
        for g in range(2):
            bk = B[6 + g]
            t = self.pe(lambda e, g=g, bk=bk: e.matmul(bk.t[:, :], Bt[:, g * 128:(g + 1) * 128],
                                                      xd[:, g * 512:(g + 1) * 512], start=True, stop=True),
                        xready, P.own("scalar"), bk.free)
            bk.free = A(lambda e, g=g, bk=bk: e.activation(sts[:, g * 512:(g + 1) * 512], bk.t[:, :], ACT.Copy), t)
        st_ready = P.own("scalar")
        cb = cut(512)
        bk5 = B[5]

        def fcb(e):
            for tt in range(2):
                for g in range(2):
                    m = e.matmul(bk5.t[:, (2 * tt + g) * 128:(2 * tt + g + 1) * 128],
                                 cv[:, (8 + g) * T + tt * 128:(8 + g) * T + tt * 128 + 128],
                                 cv[:, (10 + g) * T + tt * 128:(10 + g) * T + tt * 128 + 128], start=True, stop=True)
            return m
        t = self.pe(fcb, bk5.free)
        bk5.free = A(lambda e: e.activation(cb, bk5.t[:, :], ACT.Copy), t)
        cbt = P.own("scalar")
        ab = cut(8 * 128)
        M = cut(16 * 128)
        y = [cut(D) for _ in range(2)]
        mseg = self.c("mseg")
        for tt in range(2):
            mt = []
            for hb in range(4):
                def quarter(tt=tt, hb=hb):
                    a = ab[:, (hb % 2) * 512:(hb % 2 + 1) * 512]
                    t = V(lambda e: e.tensor_copy(r3(a, 128), bc(adt[:, tt * 16 + hb * 4:tt * 16 + hb * 4 + 4], 2, 128)),
                          self.abused.get(hb % 2))
                    bk = B[hb % 2]

                    def fn(e):
                        for j in range(4):
                            m = e.matmul(bk.t[:, j * 128:(j + 1) * 128], a[:, j * 128:(j + 1) * 128], self.tri,
                                         start=True, stop=True)
                        return m
                    t = self.pe(fn, t, bk.free)
                    self.abused[hb % 2] = t
                    m4 = M[:, hb * 512:(hb + 1) * 512]
                    m3 = r3(m4, 128)
                    t = V(lambda e: e.tensor_tensor(m3, r3(bk.t[:, :], 128),
                                                    bc(acs[:, tt * 16 + hb * 4:tt * 16 + hb * 4 + 4], 2, 128),
                                                    ALU.subtract), t, self.mused)
                    bk.free = t
                    t = G(lambda e: e.tensor_tensor(m3, m3, bc(mseg, 1, 4), ALU.add), t)
                    t = A(lambda e: e.activation(m4, m4, ACT.Exp), t)
                    g = hb // 2
                    return V(lambda e: e.tensor_tensor(
                        m3, m3, bc(cb[:, (2 * tt + g) * 128:(2 * tt + g + 1) * 128], 1, 4), ALU.mult), t, cbt)
                mt.append(quarter())
            for g in range(2):
                def half(tt=tt, g=g):
                    bk = B[2 + g]

                    def fn(e):
                        for j in range(8):
                            h = g * 8 + j
                            m = e.matmul(bk.t[:, j * 64:(j + 1) * 64], M[:, h * 128:(h + 1) * 128],
                                         xr[tt][:, h * 64:(h + 1) * 64], start=True, stop=True)
                        return m
                    t = self.pe(fn, mt, xready, bk.free)
                    self.mused = t
                    yy = y[tt][:, g * 512:(g + 1) * 512]
                    x_ = xs[tt][:, g * 512:(g + 1) * 512]
                    V(lambda e: e.tensor_tensor(r3(yy, 64), r3(x_, 64), bc(R("dskip")[:, g * 8:g * 8 + 8], 2, 64), ALU.mult))
                    bk.free = V(lambda e: e.tensor_tensor(yy, yy, bk.t[:, :], ALU.add), t)
                    if tt == 1:
                        b2 = B[6 + g]
                        t = self.pe(lambda e: e.matmul(b2.t[:, :], cv[:, (10 + g) * T + 128:(10 + g) * T + 256],
                                                       sts[:, g * 512:(g + 1) * 512], start=True, stop=True),
                                    st_ready, b2.free)
                        t = V(lambda e: e.tensor_tensor(r3(x_, 64), r3(b2.t[:, :], 64),
                                                        bc(dfs[:, g * 8:g * 8 + 8], 2, 64), ALU.mult), t)
                        b2.free = t
                        V(lambda e: e.tensor_tensor(yy, yy, x_, ALU.add))
                    return V(lambda e: e.tensor_tensor(yy, yy, z[tt][:, g * 512:(g + 1) * 512], ALU.mult))
                half()
        self.junk = M[:, 0:512]
        t = [P.own("vector"), P.own("tensor")]
        done = []
        for tt in range(2):
            def one(tt=tt):
                r, t2 = self.rms_rows(y[tt], 2, 512, 1e-6, t, col=176 + 8 * tt)
                return V(lambda e: e.tensor_tensor(r3(y[tt], 512), r3(y[tt], 512), bc(r, 2, 512), ALU.mult), t2)
            done.append(one())
        ready = self.turn(lambda tt: y[tt], 8, done, scale=lambda k: self.vec("ssd_norm", k))
        self.add_moving("out_ssd", ready)


def program(nc, d, out, upto=99):
    with ExitStack() as ctx:
        K = Kernel(nc, ctx, d)
        P = K.P
        K.small = ctx.enter_context(nc.sbuf_tensor("small", [128, 100], F32))
        K.abused, K.mused = {}, None
        K.begin_program()
        steps = []
        for l in range(DEPTH):
            steps += [lambda l=l: K.mixer(l), lambda l=l: K.moe(l)]

        def late():
            K.memk = K.scr.t[:, K.scr.size - 2048:K.scr.size]
            K.memv = [K.scr.t[:, K.scr.size - 4096:K.scr.size - 3072], K.scr.t[:, K.scr.size - 3072:K.scr.size - 2048]]
            K.scr.size -= 4096
            K.memory()
        steps += [late, lambda: K.ffn("ffn10", "ffn1_norm0"), K.ssd, lambda: K.cross(0),
                  lambda: K.ffn("ffn20", "ffn2_norm0"), lambda: K.ffn("ffn11", "ffn1_norm1"), K.swa,
                  lambda: K.cross(1), lambda: K.ffn("ffn21", "ffn2_norm1")]
        for step in steps[:upto]:
            step()
        now = P.meet()
        for tt in range(2):
            last = P.dma(K.d_out, lambda e, tt=tt: e.dma_start(out[tt * 128:(tt + 1) * 128, :], K.x(tt)), now)
        P.gate["sync"] = []
        with nc.Block() as block:
            P.emit(block, last)




def kernel(**inputs):
    from concourse import bacc
    from concourse.bass_utils import run_bass_kernel_spmd

    i = {k: np.asarray(v) for k, v in inputs.items()}
    arrays = {**pack_weights(i), **pack_small(i)}
    nc = bacc.Bacc("TRN2", target_bir_lowering=False, num_devices=1)
    d = {n: nc.dram_tensor("in_" + n, a.shape, mybir.dt.from_np(a.dtype), kind="ExternalInput").ap()
         for n, a in arrays.items()}
    out = nc.dram_tensor("out_x", (T, D), F32, kind="ExternalOutput").ap()
    program(nc, d, out)
    r = run_bass_kernel_spmd(nc, [{"in_" + n: a for n, a in arrays.items()}], core_ids=[0])
    return r.results[0]["out_x"].reshape(1, T, D)
```

```python
from contextlib import ExitStack
import math

import numpy as np
import concourse.bass as bass
from concourse import mybir

F32 = mybir.dt.float32
F32R = mybir.dt.float32r
I32 = mybir.dt.int32
ACT = mybir.ActivationFunctionType
ALU = mybir.AluOpType
AXX = mybir.AxisListType.X

D, T, DEPTH, HD = 1024, 256, 2, 64
F, NE, FE = 2816, 16, 512
CW = 2048
NS, NR = 3, 3
ALPHA = (2 * DEPTH) ** 0.25
NEG = -1e30
MAGIC = 12582912.0
SPLITS = (384, 256, 32, 256, 256, 256, 256, 256, 256, 4)
IN_COLS = sum(SPLITS)
OFF = [sum(SPLITS[:i]) for i in range(len(SPLITS))]



def constants():
    p = np.arange(128)
    out = {}
    out["ident"] = np.eye(128)
    out["zto"] = np.concatenate([np.zeros((128, 128)), (p[:, None] <= p[None, :]) * 1.0, np.ones((128, 128))], axis=1)
    k = np.arange(256)
    q1 = 128 + p
    out["mchunk"] = np.where(k[None, :] // 64 <= q1[:, None] // 64, 0.0, NEG)
    out["mframe"] = np.where(k[None, :] <= q1[:, None], 0.0, NEG)
    out["mseg"] = np.where(p[:, None] <= p[None, :], 0.0, NEG)
    fm = [500000.0 ** (-i / 32) for i in range(0, 32, 2)]
    fd = [500000.0 ** (-i / 8) for i in range(0, 8, 2)]
    out["invf"] = np.tile(np.array(fm + fd), (128, 1))
    out["iota"] = np.tile(np.arange(128), (128, 1))
    out["c4"] = np.tile(np.arange(4, 0, -1), (128, 1))
    out["c16"] = np.tile(np.arange(16, 0, -1), (128, 1))
    out["half"] = np.full((128, 8), -0.5)
    return out


def mask_constants():
    c = constants()
    return np.concatenate([c["ident"], c["mchunk"], c["mframe"]], axis=1)


def late_constants():
    p = np.arange(128)
    k = np.arange(256)
    t = np.arange(256)
    bands = np.zeros((128, 2, 4, 256))
    for w in range(4):
        n = 2 << w
        for s in range(2):
            si = s * 128 + p
            d = t[None, :] - si[:, None]
            cnt = np.minimum(t + 1, n)
            bands[:, s, w, :] = ((d >= 0) & (d < n)) / cnt[None, :] - (d == 0)
    dist = (128 + p)[:, None] - k[None, :]
    slopes = 2.0 ** (-8.0 * (np.arange(16) + 1) / 16)
    ali = np.where((dist >= 0) & (dist < 128), 0.0, NEG)[:, None, :] - slopes[None, :, None] * dist[:, None, :]
    ali = np.where(ali > 0.5 * NEG, 8.0 * ali, NEG)
    e = np.zeros((128, 16, 128))
    for i in range(16):
        e[i, i, :] = 1.0
    return {"esel": e.reshape(128, -1)[:16], "bands": bands.reshape(128, -1), "alibi": ali.reshape(128, -1)}


def layout(parts):
    at, out = 0, {}
    for name, a in parts.items():
        out[name] = (at, a.shape[1])
        at += a.shape[1]
    return out, at


CONST, NCONST = layout(constants())

VECS = [("mem_norm", 8), ("ffn1_norm0", 8), ("ffn1_norm1", 8), ("mix_norm0", 8), ("mix_norm1", 8),
        ("xattn_norm0", 8), ("xattn_norm1", 8), ("ffn2_norm0", 8), ("ffn2_norm1", 8), ("ssd_norm", 8),
        ("pool_scale", 8), ("conv_b", 12), ("conv_w", 48)]
VAT, NV = {}, 0
for _n, _c in VECS:
    VAT[_n] = NV
    NV += _c

ROWS = {
    "mla": [("qg", 384), ("kvg", 256), ("subln", 64), ("fb", 4), ("lq1", 32), ("lq2", 32), ("lk1", 32), ("lk2", 32)],
    "moe": [("rb", 16)],
    "ssd": [("dtb", 16), ("alog", 16), ("dskip", 16)],
    "swa": [("bqkv", 1536), ("qn", 64), ("kn", 64), ("sink", 16), ("bo", 1024)],
    "mem": [("kn", 256)],
    "xat": [("qn", 256)],
}


def row_at(stage, name):
    at = 0
    for n, c in ROWS[stage]:
        if n == name:
            return at, at + c
        at += c
    raise KeyError(name)


def row_len(stage):
    return sum(c for _, c in ROWS[stage])




def plan_moving(K, N):
    out = []
    for n0 in range(0, N, 512):
        w = min(512, N - n0)
        per = CW // w
        kt = K // 128
        for k0 in range(0, kt, per):
            out.append((n0, w, k0, min(per, kt - k0)))
    return out


def pack_moving(W):
    K, N = W.shape
    return [W[k0 * 128:(k0 + n) * 128, n0:n0 + w].reshape(n, 128, w).transpose(1, 0, 2).reshape(-1)
            for n0, w, k0, n in plan_moving(K, N)]


def pack_pair(G, U, f):
    g = G[:, f * 128:(f + 1) * 128].reshape(-1, 128, 128).transpose(1, 0, 2)
    u = U[:, f * 128:(f + 1) * 128].reshape(-1, 128, 128).transpose(1, 0, 2)
    return np.stack([g, u], axis=1).reshape(-1)


def pack_down(W, f):
    return W[f * 128:(f + 2) * 128].reshape(2, 128, -1).transpose(1, 0, 2).reshape(-1)


def plan_gated(nf):
    out = []
    for f in range(0, nf, 2):
        out += [("gu", f), ("gu", f + 1)]
        if f >= 2:
            out.append(("d", f - 2))
    return out + [("d", nf - 2)]


def pack_gated(G, U, W):
    return [pack_pair(G, U, f) if kind == "gu" else pack_down(W, f) for kind, f in plan_gated(G.shape[1] // 128)]


def plan_experts():
    return plan_gated(NE * FE // 128)


def pack_experts(G, U, W):
    nf = FE // 128
    return [pack_pair(G[f // nf], U[f // nf], f % nf) if kind == "gu" else pack_down(W[f // nf], f % nf)
            for kind, f in plan_experts()]


def sizes_moving(K, N):
    return [w * n for _, w, _, n in plan_moving(K, N)]


STREAM = []
for _l in range(DEPTH):
    STREAM += [(f"w_in{_l}", sizes_moving(D, IN_COLS)), (f"uq{_l}", sizes_moving(384, 768)),
               (f"ukv{_l}", sizes_moving(256, 1024)), (f"w_out{_l}", sizes_moving(D, D)),
               (f"exp{_l}", [CW] * len(plan_experts()))]
STREAM += [("mem_wkv", sizes_moving(D, 2 * D)), ("ffn10", [CW] * len(plan_gated(F // 128))),
           ("pool_in", sizes_moving(D, D)), ("pool_w", [CW]), ("out_pool", sizes_moving(D, D)),
           ("ssd_xbc", [CW] * 6), ("ssd_z", sizes_moving(D, D + 16)), ("out_ssd", sizes_moving(D, D)),
           ("xwq0", sizes_moving(D, D)), ("xwo0", sizes_moving(D, D)), ("ffn20", [CW] * len(plan_gated(F // 128))),
           ("ffn11", [CW] * len(plan_gated(F // 128))), ("wqkv", sizes_moving(D, 1536)), ("wo", sizes_moving(D, D)),
           ("xwq1", sizes_moving(D, D)), ("xwo1", sizes_moving(D, D)), ("ffn21", [CW] * len(plan_gated(F // 128)))]


def pack_weights(i):
    out = {}
    for l in range(DEPTH):
        out[f"w_in{l}"] = pack_moving(i["w_in"][l])
        out[f"uq{l}"] = pack_moving(i["mla_w_uq"][l])
        out[f"ukv{l}"] = pack_moving(i["mla_w_ukv"][l])
        out[f"w_out{l}"] = pack_moving(i["w_out"][l])
        out[f"exp{l}"] = pack_experts(i["exp_w_gate"][l], i["exp_w_up"][l], i["exp_w_down"][l])
        for n in ("ffn1", "ffn2"):
            wi = i[n + "_wi_2"][l]
            out[f"{n}{l}"] = pack_gated(wi[:, :F], wi[:, F:], i[n + "_wo_2"][l])
        out[f"xwq{l}"] = pack_moving(i["xattn_wq_2"][l])
        out[f"xwo{l}"] = pack_moving(i["xattn_wo_2"][l])
    out["mem_wkv"] = pack_moving(i["mem_wkv_2"])
    w = i["ssd_in_proj_2"][0]
    out["ssd_z"] = pack_moving(np.concatenate([w[:, :1024], w[:, 2560:2576]], axis=1))
    out["pool_in"] = pack_moving(w[:, 2576:3600])
    x = w[:, 1024:2560].reshape(D, 12, 128)
    even, odd = x[:, 0::2].reshape(D, 768), x[:, 1::2].reshape(D, 768)
    out["ssd_xbc"] = [pack_pair(even, odd, f) for f in range(6)]
    pw = i["pool_w_2"][0].reshape(4, 2, 128, 2, 128)
    out["pool_w"] = [pw.transpose(2, 0, 3, 1, 4).reshape(-1)]
    out["out_ssd"] = pack_moving(i["even_out_proj_2"][0][:1024])
    out["out_pool"] = pack_moving(i["even_out_proj_2"][0][1024:])
    out["wqkv"] = pack_moving(i["attn_wqkv_2"][0])
    out["wo"] = pack_moving(i["attn_wo_2"][0])
    return {n: np.concatenate(out[n]) for n, _ in STREAM}


def pack_small(i):
    f = np.float32
    out = {"const": np.concatenate(list(constants().values()), axis=1).astype(f)}
    for n, a in late_constants().items():
        out[n] = a.astype(f)
    out["masks"] = mask_constants().astype(f)
    v = {"mem_norm": i["mem_norm_2"], "ssd_norm": i["ssd_norm_2"][0], "pool_scale": i["pool_scale_2"][0],
         "conv_b": i["ssd_conv_b_2"][0], "conv_w": i["ssd_conv_w_2"][0].reshape(-1)}
    for l in range(DEPTH):
        for n in ("ffn1_norm", "mix_norm", "xattn_norm", "ffn2_norm"):
            v[f"{n}{l}"] = i[n + "_2"][l]
    out["vecs"] = np.ascontiguousarray(np.concatenate([v[n].reshape(-1, 128) for n, _ in VECS], axis=0).T)
    for l in range(DEPTH):
        out[f"row_mla{l}"] = np.concatenate([i["mla_q_norm_g"][l], i["mla_kv_norm_g"][l], i["diff_subln_g"][l],
                                             i["fox_f_bias"][l], i["diff_lam_q1"][l], i["diff_lam_q2"][l],
                                             i["diff_lam_k1"][l], i["diff_lam_k2"][l]])
        out[f"row_ln1{l}"] = np.concatenate([i["ln1_g"][l], i["ln1_b"][l]])
        out[f"row_ln2{l}"] = np.concatenate([i["ln2_g"][l], i["ln2_b"][l]])
        out[f"row_xat{l}"] = i["xattn_qnorm_2"][l]
    out["row_moe"] = i["router_bias"]
    out["row_lnin"] = np.concatenate([i["ln_in_g"], i["ln_in_b"]])
    out["row_ssd"] = np.concatenate([i["ssd_dt_bias_2"][0], i["ssd_a_log_2"][0], i["ssd_d_2"][0]])
    out["row_swa"] = np.concatenate([i["attn_bqkv_2"][0], i["attn_qnorm_2"][0], i["attn_knorm_2"][0],
                                     i["attn_sinks_2"][0], i["attn_bo_2"][0]])
    out["row_mem"] = i["mem_knorm_2"]
    out["x"] = i["x"][0]
    out["mem"] = i["mem_2"][0]
    out["pos"] = np.ascontiguousarray(i["positions"].reshape(2, 128).T)
    out["router"] = np.ascontiguousarray(i["router_w"].reshape(8, 128, 16).transpose(1, 0, 2).reshape(128, 128))
    return out



class Program:

    ENGINES = ("sync", "tensor", "vector", "scalar", "gpsimd")

    def __init__(self, nc, ctx):
        self.nc, self.ctx = nc, ctx
        self.todo = {e: [] for e in self.ENGINES}
        self.done = {e: 0 for e in self.ENGINES}
        self.sems = {e: ctx.enter_context(nc.semaphore("s_" + e)) for e in self.ENGINES}
        self.gate = {e: [] for e in self.ENGINES}

    def sem(self, name):
        self.sems[name] = self.ctx.enter_context(self.nc.semaphore(name))
        self.done[name] = 0
        return name

    def op(self, engine, fn, *after):
        waits = list(after) + self.gate[engine]
        self.gate[engine] = []
        self.done[engine] += 1
        self.todo[engine].append((waits, fn, engine, 1))
        return (engine, self.done[engine])

    def dma(self, sem, fn, *after, engine="sync"):
        self.done[sem] += 16
        self.todo[engine].append((list(after), fn, sem, 16))
        return (sem, self.done[sem])

    def own(self, engine):
        return (engine, self.done[engine])

    def meet(self):
        now = [self.own(e) for e in ("tensor", "vector", "scalar", "gpsimd")]
        for e in ("tensor", "vector", "scalar", "gpsimd"):
            self.gate[e] = list(now)
        return now

    def branch(self, flag, known, yes, no, held, hold):
        outer, start, gates = self.todo, dict(self.done), {e: list(g) for e, g in self.gate.items()}
        kept = held()
        ways = []
        for way in (yes, no):
            self.todo = {e: [] for e in self.ENGINES}
            self.done = dict(start)
            self.gate = {e: list(g) for e, g in gates.items()}
            hold(kept)
            way()
            ways.append((self.todo, dict(self.done)))
        self.todo = outer
        self.done = {s: max(w[1][s] for w in ways) for s in start}
        for e in self.ENGINES:
            both = []
            for todo, done in ways:
                short = self.done[e] - done[e]
                pad = [([(e, done[e])], lambda eng: eng.nop(), e, short)] if short else []
                both.append(todo[e] + pad)
            if both[0] or both[1]:
                self.todo[e].append(("branch", (flag, known), *both))
        assert all(self.done[s] == w[1][s] for w in ways for s in start if s not in self.ENGINES)
        self.meet()

    def emit(self, block, last):
        def flat(x):
            for t in x:
                if isinstance(t, list):
                    yield from flat(t)
                elif t is not None:
                    yield t

        def play(eng, todo, seen):
            for waits, fn, sem, n in todo:
                if waits == "branch":
                    flag, known = fn
                    eng.wait_ge(self.sems[known[0]], known[1])
                    seen[known[0]] = max(seen.get(known[0], 0), known[1])
                    taken = eng.value_load(flag, min_val=0, max_val=1)
                    with eng.If(taken == 1):
                        play(eng, sem, dict(seen))
                    with eng.Else():
                        play(eng, n, dict(seen))
                    continue
                for s, v in flat(waits):
                    if v > seen.get(s, 0):
                        eng.wait_ge(self.sems[s], v)
                        seen[s] = v
                fn(eng).then_inc(self.sems[sem], n)

        def run(engine):
            def body(eng):
                play(eng, self.todo[engine], {})
                if engine == "sync":
                    eng.wait_ge(self.sems[last[0]], last[1])
            return body

        block.sync(run("sync"))
        block.tensor(run("tensor"))
        block.vector(run("vector"))
        block.scalar(run("scalar"))
        block.gpsimd(run("gpsimd"))


def interleave(steps, width):
    going, left = [], list(steps)
    while going or left:
        if len(going) < width and left:
            going.append(left.pop(0))
        for gen in list(going):
            try:
                next(gen)
            except StopIteration:
                going.remove(gen)


class Bank:

    def __init__(self, tensor):
        self.t = tensor
        self.free = None


class Scratch:

    def __init__(self, tensor, size):
        self.t, self.size, self.at = tensor, size, 0

    def cut(self, n):
        a = self.at
        self.at += n
        assert self.at <= self.size, self.at
        return self.t[:, a:a + n]


def bc(ap, axis, n):
    ap = ap.unsqueeze(axis)
    shape = list(ap.shape)
    shape[axis] = n
    return ap.broadcast_to(shape)


def r3(ap, b):
    return ap.rearrange("p (a b) -> p a b", b=b)


class Kernel:

    def __init__(self, nc, ctx, d):
        self.nc, self.d = nc, d
        self.P = Program(nc, ctx)

        def sb(name, n, dt=F32, p=128):
            return ctx.enter_context(nc.sbuf_tensor(name, [p, n], dt))

        self.stage = [sb(f"stage{i}", CW) for i in range(NS)]
        self.hi = [sb(f"hi{i}", CW, F32R) for i in range(NR)]
        self.lo = [sb(f"lo{i}", CW, F32R) for i in range(NR)]
        self.thi = sb("thi", 8 * T, F32R)
        self.tlo = sb("tlo", 8 * T, F32R)
        self.ahi = sb("ahi", 4 * T, F32R)
        self.alo = sb("alo", 4 * T, F32R)
        self.X = sb("X", 2 * D)
        self.gb_ = sb("gb_", 2 * D)
        self.rows = sb("rows", max(row_len(s) for s in ROWS))
        self.const = sb("const_sb", NCONST)
        self.vecs = sb("vecs_sb", NV)
        self.maskr = sb("maskr", 640, F32R)
        self.identr = self.maskr[:, 0:128]
        self.st = sb("st", 288)
        n = 19240
        self.scr = Scratch(sb("scr", n), n)
        self.bank = [Bank(ctx.enter_context(nc.psum_tensor(f"bank{i}", [128, 512], F32))) for i in range(8)]
        self.d_stage = [self.P.sem(f"d_stage{i}") for i in range(NS)]
        self.d_const = self.P.sem("d_const")
        self.d_x = self.P.sem("d_x")
        self.d_row = self.P.sem("d_row")
        self.d_ln = self.P.sem("d_ln")
        self.d_late = self.P.sem("d_late")
        self.d_out = self.P.sem("d_out")
        self.ident = self.c("ident")
        self.zto = self.c("zto")
        self.tri, self.ones = self.zto[:, 128:256], self.zto[:, 256:384]
        self.chunks = []
        for name, sizes in STREAM:
            at = 0
            for n in sizes:
                self.chunks.append((name, at, n))
                at += 128 * n
        self.at = 0
        self.loaded, self.rounded, self.parted, self.used = {}, {}, {}, {}

    def start(self):
        for i in range(NS):
            self.load(i)
        for i in range(NR - 1):
            self.split(i)
            self.load(i + NS)

    def c(self, name):
        a, n = CONST[name]
        return self.const[:, a:a + n]

    def vec(self, name, k):
        a = VAT[name] + k
        return self.vecs[:, a:a + 1]

    def row(self, stage, name):
        a, b = row_at(stage, name)
        return self.rows[:, a:b]

    def v(self, fn, *after):
        return self.P.op("vector", fn, self.P.own("vector"), *after)

    def a(self, fn, *after):
        return self.P.op("scalar", fn, self.P.own("scalar"), *after)

    def g(self, fn, *after):
        return self.P.op("gpsimd", fn, self.P.own("gpsimd"), *after)

    def pe(self, fn, *after):
        return self.P.op("tensor", fn, *after)

    def load(self, i):
        if i >= len(self.chunks):
            return
        name, at, n = self.chunks[i]
        src = self.d[name][at:at + 128 * n].rearrange("(p c) -> p c", p=128)
        dst = self.stage[i % NS][:, :n]
        before = [self.rounded[i - NS], self.parted[i - NS]] if i >= NS else []
        self.loaded[i] = self.P.dma(self.d_stage[i % NS], lambda e: e.dma_start(dst, src), *before)

    def split(self, i):
        if i >= len(self.chunks):
            return
        n = self.chunks[i][2]
        src = self.stage[i % NS][:, :n]
        hi, lo = self.hi[i % NR][:, :n], self.lo[i % NR][:, :n]
        last = self.used.get(i - NR)
        old = self.parted.get(i - NR)
        m = n // 2

        def part(a, b, *after):
            s_, h_, l_ = src[:, a:b], hi[:, a:b], lo[:, a:b]
            r = self.P.op("scalar", lambda e: e.activation(h_, s_, ACT.Copy), self.loaded[i], last, old)
            return r, (l_, s_, h_)
        both = [part(0, m), part(m, n)]
        for r, (l_, s_, h_) in both:
            self.parted[i] = self.P.op("vector", lambda e, l_=l_, s_=s_, h_=h_: e.tensor_tensor(
                l_, s_, h_.bitcast(F32), ALU.subtract), self.loaded[i], r, last)
        self.rounded[i] = both[1][0]

    def chunk(self, name, fn, *after, between=None):
        i = self.at
        assert self.chunks[i][0] == name, (self.chunks[i], name)
        self.at += 1
        hi, lo = self.hi[i % NR], self.lo[i % NR]
        tok = self.P.op("tensor", lambda e: fn(e, hi, lo), self.rounded[i], self.parted[i], *after)
        self.used[i] = tok
        self.split(i + NR - 1)
        self.load(i + NR - 1 + NS)
        if between is not None:
            between(tok)
        return tok

    def moving(self, name, K, N, banks, evac, ready, base=0):
        plan = plan_moving(K, N)
        kt = K // 128
        turn = 0
        for n0, w, k0, n in plan:
            pair = banks[turn % len(banks)]

            def fn(e, hi, lo, n0=n0, w=w, k0=k0, n=n, pair=pair):
                for j in range(n):
                    for tt in range(2):
                        xs = slice((base + k0 + j) * T + tt * 128, (base + k0 + j) * T + tt * 128 + 128)
                        ws = slice(j * w, (j + 1) * w)
                        out = pair[tt].t[:, :w]
                        e.matmul(out, self.thi[:, xs], hi[:, ws], start=(k0 + j == 0), stop=False)
                        e.matmul(out, self.thi[:, xs], lo[:, ws], start=False, stop=False)
                        m = e.matmul(out, self.tlo[:, xs], hi[:, ws], start=False, stop=(k0 + j == kt - 1))
                return m
            tok = self.chunk(name, fn, ready, pair[0].free, pair[1].free)
            if k0 + n == kt:
                for tt in range(2):
                    pair[tt].free = evac(tt, n0, w, pair[tt].t[:, :w], tok)
                turn += 1

    def pair_product(self, name, bank, ready):
        def fn(e, hi, lo):
            for s in range(2):
                out = bank.t[:, s * T:(s + 1) * T]
                for k in range(8):
                    ws = slice((s * 8 + k) * 128, (s * 8 + k + 1) * 128)
                    xs = slice(k * T, (k + 1) * T)
                    e.matmul(out, hi[:, ws], self.thi[:, xs], start=(k == 0), stop=False)
                    e.matmul(out, hi[:, ws], self.tlo[:, xs], start=False, stop=False)
                    m = e.matmul(out, lo[:, ws], self.thi[:, xs], start=False, stop=(k == 7))
            return m
        return self.chunk(name, fn, ready, bank.free)

    def gated(self, name, plan, ready, gate=None):
        nf = max(f for k, f in plan if k == "gu") + 1
        act, used = {}, {}
        ys = self.bank[0:4]
        sil = [self.scr.cut(T) for _ in range(4)]
        val = [self.scr.cut(T) for _ in range(4)]
        last = None
        vfree, parts = {}, {}
        for kind, f in plan:
            if kind == "gu":
                bank = self.bank[4 + f % 4]
                tok = self.pair_product(name, bank, ready)
                s, o = sil[f % 4], val[f % 4]
                g_ps, u_ps = bank.t[:, :T], bank.t[:, T:]
                sl = slice((f % 4) * T, (f % 4 + 1) * T)
                hi, lo = self.ahi[:, sl], self.alo[:, sl]
                t = self.a(lambda e, s=s, x=g_ps: e.activation(s, x, ACT.Silu), tok, parts.get(f - 4), vfree.get(f - 4))
                if gate is not None:
                    gt = gate(f)
                    t = self.g(lambda e, s=s, gt=gt: e.tensor_tensor(s, s, gt, ALU.mult), t)
                t = self.v(lambda e, s=s, o=o, x=u_ps: e.tensor_tensor(o, s, x, ALU.mult), t, act.get(f - 4))
                bank.free = t
                vfree[f] = t
                down = used.get((f - 4) - (f - 4) % 2) if f >= 4 else None
                h = self.a(lambda e, o=o, hi=hi: e.activation(hi, o, ACT.Copy), t, down, parts.get(f - 4))
                p = self.v(lambda e, o=o, hi=hi, lo=lo: e.tensor_tensor(lo, o, hi.bitcast(F32), ALU.subtract), h, down)
                act[f], parts[f] = h, p
            else:
                def fn(e, hi, lo, f=f):
                    for j in range(2):
                        for tt in range(2):
                            at = ((f + j) % 4) * T + tt * 128
                            xs = slice(at, at + 128)
                            for half in range(2):
                                ws = slice(j * D + half * 512, j * D + half * 512 + 512)
                                out = ys[tt * 2 + half].t[:, :]
                                e.matmul(out, self.ahi[:, xs], hi[:, ws], start=(f + j == 0), stop=False)
                                e.matmul(out, self.ahi[:, xs], lo[:, ws], start=False, stop=False)
                                m = e.matmul(out, self.alo[:, xs], hi[:, ws], start=False, stop=(f + j == nf - 1))
                    return m
                first = [b.free for b in ys] if f == 0 else []
                last = self.chunk(name, fn, first, act[f], parts[f], act[f + 1], parts[f + 1])
                used[f] = last
        return last

    def held(self):
        return (self.at, dict(self.loaded), dict(self.rounded), dict(self.parted), dict(self.used),
                self.scr.at, [b.free for b in self.bank])

    def hold(self, kept):
        self.at, self.scr.at = kept[0], kept[5]
        self.loaded, self.rounded, self.parted, self.used = (dict(x) for x in kept[1:5])
        for b, t in zip(self.bank, kept[6]):
            b.free = t

    def joined(self):
        for i in range(self.at - NS - NR, self.at + NS + NR):
            if i in self.rounded:
                self.rounded[i], self.parted[i] = self.P.own("scalar"), self.P.own("vector")
            if i in self.used:
                self.used[i] = self.P.own("tensor")
        for b in self.bank:
            b.free = [self.P.own(e) for e in ("tensor", "vector", "scalar")]

    def turn(self, src, kts, ready, scale=None, free=None, hi=None, lo=None):
        hi = hi or self.thi
        lo = lo or self.tlo
        toks = []
        for n, k0 in enumerate(range(0, kts, 2)):
            bank = self.bank[4 + n % 4]
            kk = min(2, kts - k0)

            def fn(e, k0=k0, kk=kk, bank=bank):
                for j in range(kk):
                    for tt in range(2):
                        m = e.transpose(bank.t[:, j * T + tt * 128:j * T + tt * 128 + 128],
                                        src(tt)[:, (k0 + j) * 128:(k0 + j + 1) * 128], self.ident)
                return m
            tok = self.pe(fn, ready, bank.free)
            if scale is None:
                h_, l_ = hi[:, k0 * T:(k0 + kk) * T], lo[:, k0 * T:(k0 + kk) * T]
                ps = bank.t[:, :kk * T]
                t = self.a(lambda e, h_=h_, ps=ps: e.activation(h_, ps, ACT.Copy), tok, free)
                t = self.v(lambda e, h_=h_, l_=l_, ps=ps: e.tensor_tensor(l_, ps, h_.bitcast(F32), ALU.subtract), t, free)
            else:
                t = tok
                for j in range(kk):
                    sl = slice((k0 + j) * T, (k0 + j + 1) * T)
                    h_, l_, ps = hi[:, sl], lo[:, sl], bank.t[:, j * T:(j + 1) * T]
                    sc = scale(k0 + j)
                    t = self.a(lambda e, h_=h_, ps=ps, sc=sc: e.activation(h_, ps, ACT.Copy, scale=sc), t, free)
                for j in range(kk):
                    sl = slice((k0 + j) * T, (k0 + j + 1) * T)
                    h_, l_, ps = hi[:, sl], lo[:, sl], bank.t[:, j * T:(j + 1) * T]
                    sc = scale(k0 + j)
                    t = self.v(lambda e, h_=h_, l_=l_, ps=ps, sc=sc: e.scalar_tensor_tensor(
                        l_, ps, sc, h_.bitcast(F32), ALU.mult, ALU.subtract), t, free)
            bank.free = t
            toks += [t]
        return toks

    def power(self, out, x, n, after):
        return self.g(lambda e: e.tensor_tensor(out, x, self.c("half")[:, :1].broadcast_to([128, n]), ALU.pow), after)

    def x(self, tt):
        return self.X[:, tt * D:(tt + 1) * D]

    def layer_norm(self, src, ready, ln):
        def one(tt):
            s, st = src(tt), self.st[:, tt * 32:(tt + 1) * 32]
            for c in range(2):
                self.v(lambda e, c=c: e.bn_stats(st[:, c * 6:(c + 1) * 6], s[:, c * 512:(c + 1) * 512]), ready)
            self.v(lambda e: e.bn_aggr(st[:, 12:14], st[:, 0:12]))
            t = self.v(lambda e: e.tensor_scalar(st[:, 14:15], st[:, 13:14], 1e-5, None, ALU.add))
            t = self.power(st[:, 15:16], st[:, 14:15], 1, t)
            t = self.v(lambda e: e.tensor_scalar(s, s, st[:, 12:13], st[:, 15:16], ALU.subtract, ALU.mult), t)
            t = self.v(lambda e: e.tensor_tensor(s, s, self.gb_[:, :D], ALU.mult), ln)
            return self.g(lambda e: e.tensor_tensor(self.x(tt), s, self.gb_[:, D:], ALU.add), t)

        return [one(tt) for tt in range(2)]

    def rms_rows(self, src, groups, width, eps, ready, col=64):
        junk = self.junk[:, :width]
        ss, r = self.st[:, col:col + groups], self.st[:, col + groups:col + 2 * groups]
        for i in range(groups):
            t = self.a(lambda e, i=i: e.activation(junk, src[:, i * width:(i + 1) * width], ACT.Square,
                                                   accum_out=ss[:, i:i + 1]), ready)
        t = self.v(lambda e: e.tensor_scalar(ss, ss, 1.0 / width, eps, ALU.mult, ALU.add), t)
        return r, self.power(r, ss, groups, t)

    def rms_turn(self, gain, ready):
        xn = [self.scr.cut(D) for _ in range(2)]
        self.junk = self.scr.cut(D)
        done = []
        for tt in range(2):
            r, t = self.rms_rows(self.x(tt), 1, D, 1e-6, ready, col=64 + 8 * tt)
            done.append(self.v(lambda e, tt=tt, r=r: e.tensor_scalar(xn[tt], self.x(tt), r, None, ALU.mult), t))
        return self.turn(lambda tt: xn[tt], 8, done, scale=lambda k: self.vec(gain, k))

    def rows_load(self, stage, name, after):
        n = row_len(stage)
        src = self.d[name].partition_broadcast(128)
        return self.P.dma(self.d_row, lambda e: e.dma_start(self.rows[:, :n], src), after)

    def ln_load(self, name, after):
        src = self.d[name].partition_broadcast(128)
        return self.P.dma(self.d_ln, lambda e: e.dma_start(self.gb_[:, :], src), after)

    def begin(self):
        self.scr.at = 0
        return self.P.meet()

    def heads_turned(self, src, n, width, dst, ready, banks, p0=0):
        todo = [(i, tt) for i in range(n) for tt in range(2)]
        toks = []
        for m, at in enumerate(range(0, len(todo), 4)):
            part = todo[at:at + 4]
            bank = banks[m % len(banks)]

            def fn(e, part=part, bank=bank):
                for j, (i, tt) in enumerate(part):
                    ins = e.transpose(bank.t[0:width, j * 128:(j + 1) * 128], src(tt, i), self.ident)
                return ins
            tok = self.pe(fn, ready, bank.free)
            i0 = part[0][0] * T
            out, ps = dst[p0:p0 + width, i0:i0 + len(part) * 128], bank.t[0:width, :len(part) * 128]
            if m % 2 == 0:
                bank.free = self.a(lambda e, out=out, ps=ps: e.activation(out, ps, ACT.Copy), tok)
            else:
                bank.free = self.v(lambda e, out=out, ps=ps: e.tensor_copy(out, ps), tok)
            toks.append(bank.free)
        return toks

    def attention(self, units, ready):
        sc = [self.att[:, i * 1024:(i + 1) * 1024] for i in range(2)]
        pt = [self.att[:, (2 + i) * 1024:(3 + i) * 1024] for i in range(2)]
        turned, summed = {}, {}

        def one(u):
            unit = units[u]
            H, nk = len(unit["heads"]), unit["nk"]
            per = 512 // nk
            banks = self.bank[0:2] if u % 2 == 0 else self.bank[2:4]
            S, PT = sc[u % 2], pt[u % 2]
            scale = unit["scale"]

            def fn(e):
                for j in range(H):
                    bank = banks[j // per].t
                    if "mask" in unit and j % per == 0:
                        hb = min(per, H - j)
                        e.matmul(bank[:, :hb * nk], self.identr, bc(unit["mask"], 1, hb), start=True, stop=False)
                    last = j % per == per - 1 or j == H - 1
                    m = unit["scores"](e, bank[:, (j % per) * nk:(j % per + 1) * nk], unit["heads"][j], last)
                return m
            tok = self.pe(fn, ready, banks[0].free, banks[1].free)
            yield
            c0 = 96 + 80 * (u % 2)
            m, s, x, b = (self.st[:, c0 + 16 * i:c0 + 16 * i + H] for i in range(4))
            for i in range((H + per - 1) // per):
                hb = min(per, H - i * per)
                t = self.v(lambda e, i=i, hb=hb: e.tensor_reduce(
                    m[:, i * per:i * per + hb], r3(banks[i].t[:, :hb * nk], nk), AXX, ALU.max), tok, summed.get(u - 2))
            if "shift" in unit:
                self.v(lambda e: e.scalar_tensor_tensor(m, m, scale, unit["shift"], ALU.mult, ALU.add))
                t = self.v(lambda e: e.tensor_tensor(b, unit["shift"], m, ALU.subtract))
            elif "sink" in unit:
                self.v(lambda e: e.scalar_tensor_tensor(m, m, scale, unit["sink"], ALU.mult, ALU.max))
                self.v(lambda e: e.tensor_tensor(x, unit["sink"], m, ALU.subtract))
                t = self.v(lambda e: e.tensor_scalar(b, m, -1.0, None, ALU.mult))
            else:
                t = self.v(lambda e: e.tensor_scalar(b, m, -scale, None, ALU.mult))
            yield
            for j in range(H):
                bank = banks[j // per]
                ps = bank.t[:, (j % per) * nk:(j % per + 1) * nk]
                t2 = self.P.op("scalar", lambda e, j=j, ps=ps: e.activation(
                    S[:, j * nk:(j + 1) * nk], ps, ACT.Exp, bias=b[:, j:j + 1], scale=scale, accum_out=s[:, j:j + 1]),
                    t, turned.get(u - 2))
                bank.free = t2
            if "sink" in unit:
                t2 = self.a(lambda e: e.activation(x, x, ACT.Exp), t)
            yield
            if "sink" in unit:
                self.v(lambda e: e.tensor_tensor(s, s, x, ALU.add), t2)
            self.v(lambda e: e.reciprocal(s, s), t2)
            if "lam" in unit:
                self.v(lambda e: e.tensor_scalar(s[:, 1:H:2], s[:, 1:H:2], unit["lam"], None, ALU.mult))
            nt = nk // 128
            nb = H * nt // 4
            toks = []
            for n in range(nb):
                bank = self.bank[4 + n]

                def fn(e, n=n, bank=bank):
                    for q in range(4):
                        at = (4 * n + q) * 128
                        ins = e.transpose(bank.t[:, q * 128:(q + 1) * 128], S[:, at:at + 128], self.ident)
                    return ins
                toks.append(self.pe(fn, t2, bank.free))
            turned[u] = toks[-1]
            pts = []
            for n in range(nb):
                bank = self.bank[4 + n]
                out, ps = PT[:, n * 512:(n + 1) * 512], bank.t[:, :]
                if n == 0:
                    bank.free = self.a(lambda e, out=out, ps=ps: e.activation(out, ps, ACT.Copy), toks[n], summed.get(u - 2))
                else:
                    bank.free = self.v(lambda e, out=out, ps=ps: e.tensor_copy(out, ps), toks[n], summed.get(u - 2))
                pts.append(bank.free)
            yield
            dv = unit["dv"]
            hp = 512 // dv
            vtok = []
            for i in range((H + hp - 1) // hp):
                hb = min(hp, H - i * hp)
                bank = self.bank[6 + (u + i) % 2]

                def fn(e, i=i, hb=hb, bank=bank):
                    for j in range(i * hp, i * hp + hb):
                        for k in range(nt):
                            ins = e.matmul(bank.t[:, (j - i * hp) * dv:(j - i * hp + 1) * dv],
                                           PT[:, (j * nt + k) * 128:(j * nt + k + 1) * 128],
                                           unit["v"](j, k), start=(k == 0), stop=(k == nt - 1))
                    return ins
                tok = self.pe(fn, pts, bank.free)
                vtok.append(tok)
                ps = r3(bank.t[:, :hb * dv], dv)
                rr = bc(s[:, i * hp:i * hp + hb], 2, dv)
                if "lam" in unit:
                    o8 = r3(self.st2[:, (u % 2) * 512:(u % 2) * 512 + hb * dv], dv)
                    out = r3(unit["out"], dv)
                    bank.free = self.v(lambda e, ps=ps, rr=rr, o8=o8: e.tensor_tensor(o8, ps, rr, ALU.mult), tok)
                    self.v(lambda e, o8=o8, out=out, hb=hb: e.tensor_tensor(
                        out, o8[:, 0:hb:2, :], o8[:, 1:hb:2, :], ALU.subtract))
                else:
                    out = r3(unit["out"], dv)[:, i * hp:i * hp + hb, :]
                    bank.free = self.v(lambda e, out=out, ps=ps, rr=rr: e.tensor_tensor(out, ps, rr, ALU.mult), tok)
            summed[u] = vtok + [self.P.own("vector")]

        interleave([one(u) for u in range(len(units))], 2)
        return self.P.own("vector")

    def rope(self, x, H, half, cos, sin, after):
        n = H * 2 * half
        t1, t2 = self.rt[0][:, :n], self.rt[1][:, :n]
        v4 = lambda a: a.rearrange("p (h s f) -> p h s f", s=2, f=half)
        c = bc(bc(cos, 1, 2), 1, H)
        s = bc(bc(sin, 1, 2), 1, H)
        x4 = x.rearrange("p h (s f) -> p h s f", s=2)
        self.v(lambda e: e.tensor_tensor(v4(t1), x4, c, ALU.mult), after)
        self.v(lambda e: e.tensor_tensor(v4(t2), x4, s, ALU.mult))
        self.v(lambda e: e.tensor_tensor(x4[:, :, 0, :], v4(t1)[:, :, 0, :], v4(t2)[:, :, 1, :], ALU.subtract))
        return self.v(lambda e: e.tensor_tensor(x4[:, :, 1, :], v4(t1)[:, :, 1, :], v4(t2)[:, :, 0, :], ALU.add))

    def rotations(self):
        P = self.P
        n = 40
        pos = self.keep(2, I32)
        ang, k, r, b = (self.att[:, 2048 + 64 * i:2048 + 64 * i + n] for i in range(4))
        self.cos, self.sin = self.keep(n), self.keep(n)
        posf = self.keep(2)
        t = P.dma(self.d_late, lambda e: e.dma_start(pos, self.d["pos"]))
        t = self.v(lambda e: e.tensor_copy(posf, pos), t)
        for tt in range(2):
            t = self.v(lambda e, tt=tt: e.tensor_scalar(ang[:, tt * 20:(tt + 1) * 20], self.c("invf"), posf[:, tt:tt + 1],
                                                        None, ALU.mult), t, self.const_ready)
        self.v(lambda e: e.tensor_scalar(k, ang, 1.0 / (2 * math.pi), None, ALU.mult))
        self.v(lambda e: e.tensor_scalar(k, k, MAGIC, None, ALU.add))
        self.v(lambda e: e.tensor_scalar(k, k, -MAGIC, None, ALU.add))
        c1 = 6.28125
        c2 = float(np.float32(2 * math.pi - c1))
        c3 = 2 * math.pi - c1 - c2
        for c in (c1, c2, c3):
            self.v(lambda e, c=c: e.scalar_tensor_tensor(ang, k, -c, ang, ALU.mult, ALU.add))
        pi = float(np.nextafter(np.float32(math.pi), np.float32(0)))
        t = self.v(lambda e: e.tensor_scalar(r, ang, pi, -pi, ALU.min, ALU.max))
        self.a(lambda e: e.activation(self.sin, r, ACT.Sin), t)
        self.v(lambda e: e.tensor_scalar(ang, ang, math.pi / 2, None, ALU.add))
        self.v(lambda e: e.tensor_scalar(b, ang, math.pi, -2 * math.pi, ALU.is_gt, ALU.mult))
        self.v(lambda e: e.tensor_tensor(ang, ang, b, ALU.add))
        t = self.v(lambda e: e.tensor_scalar(ang, ang, pi, -pi, ALU.min, ALU.max))
        return self.a(lambda e: e.activation(self.cos, ang, ACT.Sin), t)

    def keep(self, n, dt=F32):
        a = self.kept_at
        self.kept_at += n
        ap = self.small[:, a:a + n]
        return ap.bitcast(dt) if dt != F32 else ap

    def begin_program(self):
        P = self.P
        self.kept_at = 0
        xs = [self.scr.cut(D) for _ in range(2)]
        t = None
        for tt in range(2):
            t = P.dma(self.d_x, lambda e, tt=tt: e.dma_start(xs[tt], self.d["x"][tt * 128:(tt + 1) * 128, :]))
        P.dma(self.d_const, lambda e: e.dma_start(self.const[:, :], self.d["const"]))
        ln = self.ln_load("row_lnin", None)
        raw = self.scr.cut(640)
        P.dma(self.d_const, lambda e: e.dma_start(raw, self.d["masks"]))
        self.const_ready = P.dma(self.d_const, lambda e: e.dma_start(self.vecs[:, :], self.d["vecs"]))
        self.start()
        self.layer_norm(lambda tt: xs[tt], [t, self.const_ready], ln)
        self.a(lambda e: e.activation(self.maskr[:, :], raw, ACT.Copy), self.const_ready)

    def mixer(self, l):
        P, cut = self.P, self.scr.cut
        now = self.begin()
        rows = self.rows_load("mla", f"row_mla{l}", now)
        R = lambda n: self.row("mla", n)
        proj = [cut(IN_COLS) for _ in range(2)]
        B = self.bank
        lam_init = 0.8 - 0.6 * math.exp(-0.3 * l)
        ready = self.turn(self.x, 8, None)
        col = lambda tt, i, j=None: proj[tt][:, OFF[i]:OFF[(j or i) + 1] if (j or i) + 1 < 10 else IN_COLS]

        def to_proj(tt, n0, w, ps, tok):
            out = proj[tt][:, n0:n0 + w]
            if tt == 0:
                return self.a(lambda e: e.activation(out, ps, ACT.Copy), tok)
            return self.v(lambda e: e.tensor_copy(out, ps), tok)
        self.moving(f"w_in{l}", D, IN_COLS, [(B[0], B[1]), (B[2], B[3])], to_proj, ready)
        used = P.own("tensor")
        done = [P.own("scalar"), P.own("vector")]
        lam = self.keep(8) if l == 0 else self.lam
        self.lam = lam
        prod = self.gb_[:, 1024:1088]
        a, b = row_at("mla", "lq1")[0], row_at("mla", "lk1")[0]
        self.v(lambda e: e.tensor_tensor(prod, self.rows[:, a:a + 64], self.rows[:, b:b + 64], ALU.mult), rows)
        t = self.v(lambda e: e.tensor_reduce(lam[:, 0:2], r3(prod, 32), AXX, ALU.add))
        t = self.a(lambda e: e.activation(lam[:, 0:2], lam[:, 0:2], ACT.Exp), t)
        t = self.v(lambda e: e.tensor_tensor(lam[:, 2:3], lam[:, 0:1], lam[:, 1:2], ALU.subtract), t)
        t = self.v(lambda e: e.tensor_scalar(lam[:, 2:3], lam[:, 2:3], lam_init, None, ALU.add))
        q_at = self.scr.at
        q = [cut(768) for _ in range(2)]
        kf = [cut(768) for _ in range(2)]
        vv = [cut(512) for _ in range(2)]
        self.att = cut(4096)
        self.st2 = self.gb_[:, 0:1024]
        self.junk = self.att[:, 0:384]
        lat = []
        for tt in range(2):
            for i, g, w, c in ((0, "qg", 384, 64), (1, "kvg", 256, 72)):
                def one(tt=tt, i=i, g=g, w=w, c=c):
                    x = col(tt, i)
                    r, t = self.rms_rows(x, 1, w, 1e-6, [done, rows], col=c + 16 * tt)
                    lat.append((x, r, g, t))
                one()
        for x, r, g, t in lat:
            self.v(lambda e, x=x, r=r, g=g: e.scalar_tensor_tensor(x, x, r, R(g), ALU.mult, ALU.mult), t)
        ready = self.turn(lambda tt: proj[tt][:, 0:640], 5, P.own("vector"), free=used)
        if l == 0:
            self.rotated = self.rotations()
        turned_cs = self.rotated
        self.rt = [self.att[:, 1024:1536], self.att[:, 1536:2048]]
        rot = {}
        for tt in range(2):
            rot[tt] = (self.cos[:, tt * 20:tt * 20 + 16], self.sin[:, tt * 20:tt * 20 + 16],
                       self.cos[:, tt * 20 + 16:tt * 20 + 20], self.sin[:, tt * 20 + 16:tt * 20 + 20])

        def to_q(tt, n0, w, ps, tok):
            out = q[tt][:, n0:n0 + w]
            return self.a(lambda e: e.activation(out, ps, ACT.Copy), tok)
        self.moving(f"uq{l}", 384, 768, [(B[0], B[1]), (B[2], B[3])], to_q, ready)
        qdone = P.own("scalar")
        for tt in range(2):
            cm, sm, cd, sd = rot[tt]
            self.rope(col(tt, 2).unsqueeze(1), 1, 16, cm, sm, turned_cs)
            self.v(lambda e, tt=tt: e.tensor_copy(r3(kf[tt], 96)[:, :, 64:96], bc(col(tt, 2), 1, 8)))
            self.rope(r3(col(tt, 3), 32)[:, :, 0:8], 8, 4, cd, sd, None)
            self.rope(r3(col(tt, 4), 32)[:, :, 0:8], 8, 4, cd, sd, None)
        roped = P.own("vector")

        qT, kT = cut(8 * T), cut(8 * T)
        fqT, fkT = cut(4 * T), cut(4 * T)
        heads = self.heads_turned
        heads(lambda tt, i: col(tt, 3)[:, i * 32:(i + 1) * 32], 8, 32, qT, roped, B[4:8], p0=96)
        heads(lambda tt, i: col(tt, 4)[:, i * 32:(i + 1) * 32], 8, 32, kT, roped, B[4:8], p0=96)
        heads(lambda tt, i: col(tt, 6)[:, i * 64:(i + 1) * 64], 4, 64, fqT, done, B[4:8])
        heads(lambda tt, i: col(tt, 7)[:, i * 64:(i + 1) * 64], 4, 64, fkT, done, B[4:8])
        for tt in range(2):
            cm, sm, cd, sd = rot[tt]
            qroped = self.rope(r3(q[tt], 96)[:, :, 64:96], 8, 16, cm, sm, qdone)
        lf = [self.st[:, 0:4], self.st[:, 4:8]]
        cum = [self.st[:, 8:12], self.st[:, 12:16]]
        tmp = self.st[:, 16:24]
        lb = [proj[tt][:, 0:512] for tt in range(2)]
        for tt in range(2):
            self.v(lambda e, tt=tt: e.tensor_tensor(lf[tt], col(tt, 9), R("fb"), ALU.add))
        both = self.st[:, 0:8]
        t = self.v(lambda e: e.tensor_scalar(tmp, both, 0.0, None, ALU.min))
        t = self.a(lambda e: e.activation(both, both, ACT.Abs), t)
        t = self.a(lambda e: e.activation(both, both, ACT.Exp, scale=-1.0))
        t = self.a(lambda e: e.activation(both, both, ACT.Ln, bias=1.0))
        t = self.v(lambda e: e.tensor_tensor(both, tmp, both, ALU.subtract), t)
        for tt in range(2):
            t = self.v(lambda e, tt=tt: e.tensor_scalar(r3(lb[tt], 128), bc(lf[tt], 2, 128), -8.0, None, ALU.mult))
        bank = B[6]

        def cums(e):
            e.matmul(bank.t[:, 0:4], self.tri, lf[0], start=True, stop=True)
            e.matmul(bank.t[:, 4:8], self.ones, lf[0], start=True, stop=False)
            return e.matmul(bank.t[:, 4:8], self.tri, lf[1], start=False, stop=True)
        t = self.pe(cums, t, bank.free)
        t = self.v(lambda e: e.tensor_copy(self.st[:, 8:16], bank.t[:, 0:8]), t)
        bank.free = t
        forget = t
        def to_kv(tt, n0, w, ps, tok):
            h0 = n0 // 128
            p4 = r3(ps, 128)
            out_k = r3(kf[tt], 96)[:, h0:h0 + 4, 0:64]
            out_v = r3(vv[tt], 64)[:, h0:h0 + 4, :]
            t = self.a(lambda e: e.activation(out_k, p4[:, :, 0:64], ACT.Copy), tok)
            return self.v(lambda e: e.tensor_copy(out_v, p4[:, :, 64:128]), t)
        self.moving(f"ukv{l}", 256, 1024, [(B[0], B[1]), (B[2], B[3])], to_kv, ready, base=3)
        kvdone = [P.own("scalar"), P.own("vector")]
        heads(lambda tt, i: q[tt][:, i * 96:(i + 1) * 96], 8, 96, qT, [qroped, forget], B[0:4])
        heads(lambda tt, i: kf[tt][:, i * 96:(i + 1) * 96], 8, 96, kT, kvdone, B[0:4])
        ready = [P.own("scalar"), P.own("vector"), P.own("tensor")]
        o = [self.scr.t[:, q_at:q_at + D], self.scr.t[:, q_at + D:q_at + 2 * D]]

        def unit(tt, heads, off, m, kT_, qT_, p0, p1, **kw):
            nk = 128 * (tt + 1)
            mask = self.maskr[:, m + 256 - nk:m + 256]
            two = 2 if "lam" in kw else 1
            h0, ng = heads[0] // two, len(heads) // two

            def scores(e, out, h, last):
                fox = kw.get("fox")
                m = e.matmul(out, qT_[p0:p1, h * T + tt * 128:h * T + tt * 128 + 128], kT_[p0:p1, h * T:h * T + nk],
                             start=False, stop=last and not fox)
                if fox:
                    m = e.matmul(out, lb[0][:, h * 128:(h + 1) * 128], self.zto[:, 128:128 + nk], start=False,
                                 stop=last and tt == 0)
                    if tt:
                        m = e.matmul(out, lb[1][:, h * 128:(h + 1) * 128], self.zto[:, 0:256], start=False, stop=last)
                return m
            return dict(tt=tt, heads=heads, nk=nk, dv=64, scores=scores, mask=mask,
                        out=o[tt][:, off + h0 * 64:off + (h0 + ng) * 64], **kw)

        def vals(src, h0, two=1):
            return lambda j, k: src(k)[:, (h0 + j // two) * 64:(h0 + j // two + 1) * 64]
        units = []
        for tt, hs in ((0, range(8)), (1, range(4)), (1, range(4, 8))):
            units.append(unit(tt, list(hs), 512, 128, kT, qT, 96, 128, scale=32 ** -0.5, lam=lam[:, 2:3],
                              v=vals(lambda k: col(k, 5), hs[0] // 2, 2)))
        for tt in (0, 1):
            units.append(unit(tt, list(range(4)), 768, 384, fkT, fqT, 0, 64, scale=0.125, shift=cum[tt], fox=True,
                              v=vals(lambda k: col(k, 8), 0)))
        for tt, hs in ((0, range(8)), (1, range(4)), (1, range(4, 8))):
            units.append(unit(tt, list(hs), 0, 128, kT, qT, 0, 96, scale=96 ** -0.5, v=vals(lambda k: vv[k], hs[0])))
        done = self.attention(units, ready)
        ln = self.ln_load(f"row_ln1{l}", [P.own("vector"), P.own("scalar")])
        self.junk = self.att[:, 0:64]
        for tt in range(2):
            def one(tt=tt):
                x = o[tt][:, 512:768]
                r, t = self.rms_rows(x, 4, 64, 1e-6, done, col=64 + 8 * tt)
                t = self.v(lambda e: e.tensor_tensor(r3(x, 64), r3(x, 64), bc(r, 2, 64), ALU.mult), t)
                return self.v(lambda e: e.scalar_tensor_tensor(r3(x, 64), r3(x, 64), 1.0 - lam_init,
                                                               bc(R("subln"), 1, 4), ALU.mult, ALU.mult))
            one()
        self.P.meet()
        ready = self.turn(lambda tt: o[tt], 8, None)
        y = [kT[:, 0:D], kT[:, D:2 * D]]

        def to_y(tt, n0, w, ps, tok):
            return self.v(lambda e: e.scalar_tensor_tensor(y[tt][:, n0:n0 + w], self.x(tt)[:, n0:n0 + w], ALPHA, ps,
                                                           ALU.mult, ALU.add), tok)
        self.moving(f"w_out{l}", D, D, [(B[0], B[1]), (B[2], B[3])], to_y, ready)
        self.layer_norm(lambda tt: y[tt], P.own("vector"), ln)

    def moe(self, l):
        P, cut = self.P, self.scr.cut
        now = self.begin()
        rows = self.rows_load("moe", "row_moe", now)
        ln = self.ln_load(f"row_ln2{l}", now)
        B = self.bank
        rw = cut(128)
        rt = P.dma(self.d_x, lambda e: e.dma_start(rw, self.d["router"]), now)
        es = cut(16 * 128)
        late = P.dma(self.d_late, lambda e: e.dma_start(es[0:16, :], self.d["esel"]), now)
        xT = cut(8 * T)
        toks = []
        for n in range(4):
            bank = B[4 + n]

            def fn(e, n=n, bank=bank):
                for j in range(2):
                    for tt in range(2):
                        m = e.transpose(bank.t[:, j * T + tt * 128:j * T + tt * 128 + 128],
                                        self.x(tt)[:, (2 * n + j) * 128:(2 * n + j + 1) * 128], self.ident)
                return m
            t = self.pe(fn, bank.free)
            sl = slice(n * 512, (n + 1) * 512)
            if n % 2:
                t = self.v(lambda e, sl=sl, bank=bank: e.tensor_copy(xT[:, sl], bank.t[:, :]), t)
            else:
                t = self.a(lambda e, sl=sl, bank=bank: e.activation(xT[:, sl], bank.t[:, :], ACT.Copy), t)
            bank.free = t
            toks.append(t)
        bank = B[0]

        def route(e):
            for tt in range(2):
                for k in range(8):
                    m = e.matmul(bank.t[:, tt * 16:tt * 16 + 16], xT[:, k * T + tt * 128:k * T + tt * 128 + 128],
                                 rw[:, k * 16:(k + 1) * 16], start=(k == 0), stop=(k == 7))
            return m
        t = self.pe(route, toks, rt, bank.free)
        sc, bi, t1, t2, t3 = (cut(32) for _ in range(5))
        g1, g2, g3, g4 = (cut(16) for _ in range(4))
        oh = cut(32)
        t = self.a(lambda e: e.activation(sc, bank.t[:, 0:32], ACT.Sigmoid), t)
        bank.free = t
        V = self.v
        TT = lambda o_, a_, b_, op: V(lambda e: e.tensor_tensor(o_, a_, b_, op))
        V(lambda e: e.tensor_tensor(r3(bi, 16), r3(sc, 16), bc(self.row("moe", "rb"), 1, 2), ALU.add), t, rows)
        b4 = r3(bi, 2)
        TT(g1, b4[:, :, 0], b4[:, :, 1], ALU.max)
        TT(g2, b4[:, :, 0], b4[:, :, 1], ALU.min)
        h1, h2 = r3(g1, 2), r3(g2, 2)
        top, a1, a2 = g3[:, 0:8], g3[:, 8:16], g4[:, 0:8]
        TT(top, h1[:, :, 0], h1[:, :, 1], ALU.max)
        TT(a1, h1[:, :, 0], h1[:, :, 1], ALU.min)
        TT(a2, h2[:, :, 0], h2[:, :, 1], ALU.max)
        TT(a1, a1, a2, ALU.max)
        TT(top, top, a1, ALU.add)
        mx = g4[:, 8:10]

        def first_max(out, x, c, n):
            V(lambda e: e.tensor_reduce(mx, r3(x, n), AXX, ALU.max))
            V(lambda e: e.tensor_tensor(r3(out, n), r3(x, n), bc(mx, 2, n), ALU.is_equal))
            V(lambda e: e.tensor_tensor(r3(out, n), r3(out, n), bc(c, 1, 2), ALU.mult))
            V(lambda e: e.tensor_reduce(mx, r3(out, n), AXX, ALU.max))
            V(lambda e: e.tensor_tensor(r3(out, n), r3(out, n), bc(mx, 2, n), ALU.is_equal))
        grp = g1[:, 0:8]
        first_max(grp, top, self.c("c4"), 4)
        grouped = P.own("vector")
        t38 = g2[:, 0:8]
        V(lambda e: e.tensor_scalar(t38, grp, -NEG, NEG, ALU.mult, ALU.add))
        V(lambda e: e.tensor_tensor(r3(t1, 4), r3(bi, 4), bc(grp, 2, 4), ALU.mult))
        V(lambda e: e.tensor_tensor(r3(t1, 4), r3(t1, 4), bc(t38, 2, 4), ALU.add))
        first_max(t2, t1, self.c("c16"), 16)
        V(lambda e: e.scalar_tensor_tensor(t1, t2, 3 * NEG, t1, ALU.mult, ALU.add))
        first_max(t3, t1, self.c("c16"), 16)
        TT(t2, t2, t3, ALU.add)
        TT(t2, t2, sc, ALU.mult)
        V(lambda e: e.tensor_reduce(mx, r3(t2, 16), AXX, ALU.add))
        V(lambda e: e.reciprocal(mx, mx))
        t = V(lambda e: e.tensor_tensor(r3(oh, 16), r3(t2, 16), bc(mx, 2, 16), ALU.mult))
        gates_ready = t
        place, flag = self.st[:, 0:2], self.flag
        cnt = g3[:, 0:4]
        bk = B[1]

        def places(e):
            e.matmul(bk.t[:, 0:4], self.tri, grp[:, 0:4], start=True, stop=True)
            e.matmul(bk.t[:, 4:8], self.ones, grp[:, 0:4], start=True, stop=False)
            e.matmul(bk.t[:, 4:8], self.tri, grp[:, 4:8], start=False, stop=True)
            e.matmul(bk.t[:, 8:12], self.ones, grp[:, 0:4], start=True, stop=False)
            return e.matmul(bk.t[:, 8:12], self.ones, grp[:, 4:8], start=False, stop=True)
        t = self.pe(places, grouped, bk.free)
        V(lambda e: e.tensor_reduce(cnt[:, 0:1], bk.t[:, 8:12], AXX, ALU.max), t)
        V(lambda e: e.tensor_scalar(cnt[:, 0:1], cnt[:, 0:1], 128.0, None, ALU.is_le))
        known = V(lambda e: e.tensor_copy(flag, cnt[:, 0:1]))
        t = V(lambda e: e.tensor_tensor(g4[:, 0:8], bk.t[:, 0:8], grp, ALU.mult), t)
        bk.free = t
        V(lambda e: e.tensor_reduce(place, r3(g4[:, 0:8], 4), AXX, ALU.add))
        V(lambda e: e.tensor_scalar(place, place, -1.0, None, ALU.add))
        sel = cut(8 * 128)
        for g in range(4):
            for tt in range(2):
                i = tt * 4 + g
                placed = V(lambda e, i=i, tt=tt: e.tensor_scalar(
                    sel[:, i * 128:(i + 1) * 128], self.c("iota"), place[:, tt:tt + 1], grp[:, i:i + 1],
                    ALU.is_equal, ALU.mult))
        y = [xT[:, 0:D], xT[:, D:2 * D]]

        def dense():
            ready = []
            for n in range(4):
                sl = slice(n * 512, (n + 1) * 512)
                h = self.a(lambda e, sl=sl: e.activation(self.thi[:, sl], xT[:, sl], ACT.Copy), toks)
                ready.append(self.v(lambda e, sl=sl: e.tensor_tensor(self.tlo[:, sl], xT[:, sl],
                                                                     self.thi[:, sl].bitcast(F32), ALU.subtract), h))
            gt = cut(T)
            gb = cut(NE * T)

            def tg(e):
                for tt in range(2):
                    m = e.transpose(bank.t[0:16, tt * 128:(tt + 1) * 128], oh[:, tt * 16:(tt + 1) * 16], self.ident)
                return m
            t = self.pe(tg, gates_ready, bank.free)
            t = V(lambda e: e.tensor_copy(gt[0:16, :], bank.t[0:16, 0:T]), t)
            bank.free = t
            for n in range(8):
                bk = B[n % 4]

                def fn(e, n=n, bk=bk):
                    for j in range(2):
                        i = 2 * n + j
                        m = e.matmul(bk.t[:, j * T:(j + 1) * T], es[0:16, i * 128:(i + 1) * 128], gt[0:16, :],
                                     start=True, stop=True)
                    return m
                t2_ = self.pe(fn, t, late, bk.free)
                out = gb[:, n * 512:(n + 1) * 512]
                bk.free = V(lambda e, out=out, bk=bk: e.tensor_copy(out, bk.t[:, :]), t2_)
            last = self.gated(f"exp{l}", plan_experts(), ready + [P.own("vector")],
                              gate=lambda f: gb[:, (f // 4) * T:(f // 4 + 1) * T])
            for tt in range(2):
                for half in range(2):
                    bk = B[tt * 2 + half]
                    sl = slice(half * 512, half * 512 + 512)
                    bk.free = V(lambda e, tt=tt, sl=sl, bk=bk: e.scalar_tensor_tensor(
                        y[tt][:, sl], self.x(tt)[:, sl], ALPHA, bk.t[:, :], ALU.mult, ALU.add), last)

        def compact():
            name = f"exp{l}"
            C = 128
            gc, yg = cut(NE), cut(D)
            back = cut(4 * T)
            sil = [cut(C) for _ in range(4)]
            val = [cut(C) for _ in range(4)]
            hi3 = self.thi[:, :].rearrange("p (k t) -> p k t", t=T)
            lo3 = self.tlo[:, :].rearrange("p (k t) -> p k t", t=T)
            fetched, products = {}, {}

            def fetch(g):
                hf = g % 2
                banks = B[2 * hf:2 * hf + 2]
                ready = []
                for b, bk in enumerate(banks):
                    def fn(e, b=b, bk=bk):
                        for k in range(4):
                            kk = 4 * b + k
                            for tt in range(2):
                                i = tt * 4 + g
                                m = e.matmul(bk.t[:, k * C:(k + 1) * C], self.x(tt)[:, kk * 128:(kk + 1) * 128],
                                             sel[:, i * 128:(i + 1) * 128], start=(tt == 0), stop=(tt == 1))
                        return m
                    t = self.pe(fn, placed, bk.free)
                    h_, l_ = (x[:, 4 * b:4 * b + 4, hf * C:(hf + 1) * C] for x in (hi3, lo3))
                    ps = r3(bk.t[:, :], C)
                    t = self.a(lambda e, h_=h_, ps=ps: e.activation(h_, ps, ACT.Copy), t, products.get(g - 2))
                    t = self.v(lambda e, h_=h_, l_=l_, ps=ps: e.tensor_tensor(l_, ps, h_.bitcast(F32), ALU.subtract), t)
                    bk.free = t
                    ready.append(t)
                fetched[g] = ready

            fetch(0)
            b4_ = B[4]

            def fn(e):
                for g in range(4):
                    for tt in range(2):
                        i = tt * 4 + g
                        m = e.matmul(b4_.t[:, g * 4:g * 4 + 4], sel[:, i * 128:(i + 1) * 128],
                                     oh[:, tt * 16 + g * 4:tt * 16 + g * 4 + 4], start=(tt == 0), stop=(tt == 1))
                return m
            t = self.pe(fn, placed, gates_ready, b4_.free)
            b4_.free = V(lambda e: e.tensor_copy(gc, b4_.t[:, 0:16]), t)
            fetch(1)
            for n in range(2):
                bk = B[4 + n]

                def fn(e, n=n, bk=bk):
                    for j in range(4):
                        g, tt = 2 * n + j // 2, j % 2
                        i = tt * 4 + g
                        m = e.transpose(bk.t[:, j * 128:(j + 1) * 128], sel[:, i * 128:(i + 1) * 128], self.ident)
                    return m
                t = self.pe(fn, placed, bk.free)
                bk.free = V(lambda e, n=n, bk=bk: e.tensor_copy(back[:, n * 512:(n + 1) * 512], bk.t[:, :]), t)
            backed = P.own("vector")
            sums = {}
            state = {"yg": None}

            def collect(g):
                hf = g % 2
                out = []
                for half in range(2):
                    bk = B[2 * hf + half]
                    out.append(self.a(lambda e, half=half, bk=bk: e.activation(
                        yg[:, half * 512:half * 512 + 512], bk.t[:, :], ACT.Copy), sums[g], state["yg"]))
                    bk.free = out[-1]
                sums[g] = out

            def send(g, tt):
                hf = g % 2
                for half in range(2):
                    bk = B[2 * hf + half]
                    sl = slice(half * 512, half * 512 + 512)
                    t = self.pe(lambda e, bk=bk, sl=sl: e.matmul(
                        bk.t[:, :], back[:, g * T + tt * 128:g * T + tt * 128 + 128], yg[:, sl], start=True, stop=True),
                        sums[g], backed, bk.free)
                    state["yg"] = t
                    if g == 0:
                        t = V(lambda e, bk=bk, sl=sl: e.scalar_tensor_tensor(
                            y[tt][:, sl], self.x(tt)[:, sl], ALPHA, bk.t[:, :], ALU.mult, ALU.add), t)
                    else:
                        t = V(lambda e, bk=bk, sl=sl: e.tensor_tensor(y[tt][:, sl], y[tt][:, sl], bk.t[:, :], ALU.add), t)
                    bk.free = t

            nf = FE // 128 * 4
            act, parts, used, vtok, ttok = {}, {}, {}, {}, {}

            def product(f):
                g = f // nf
                bk = B[4 + f % 4]

                def fn(e, hi, lo):
                    hk, lk = (x[:, :].rearrange("p (s k c) -> p k s c", s=2, k=8) for x in (hi, lo))
                    out = bk.t[:, 0:2 * C]
                    for k in range(8):
                        xs = slice(k * T + (g % 2) * C, k * T + (g % 2) * C + C)
                        e.matmul(out, self.thi[:, xs], hk[:, k], start=(k == 0), stop=False)
                        e.matmul(out, self.thi[:, xs], lk[:, k], start=False, stop=False)
                        m = e.matmul(out, self.tlo[:, xs], hk[:, k], start=False, stop=(k == 7))
                    return m

                def between(tok):
                    s_, o_ = sil[f % 4], val[f % 4]
                    t = self.a(lambda e: e.activation(s_, bk.t[:, 0:C], ACT.Silu), tok, vtok.get(f - 4))
                    vtok[f] = self.v(lambda e: e.scalar_tensor_tensor(
                        o_, s_, gc[:, f // 4:f // 4 + 1], bk.t[:, C:2 * C], ALU.mult, ALU.mult), t, ttok.get(f - 4))
                    if f:
                        turn_act(f - 1)
                products[g] = self.chunk(name, fn, fetched[g], bk.free, between=between)

            def turn_act(f):
                bk = B[4 + f % 4]
                ps = bk.t[:, 2 * C:3 * C]
                t = ttok[f] = self.pe(lambda e: e.transpose(ps, val[f % 4], self.ident), vtok[f])
                hi, lo = (x[:, (f % 4) * T:(f % 4) * T + C] for x in (self.ahi, self.alo))
                down_ = used.get((f - 4) - (f - 4) % 2)
                act[f] = self.a(lambda e: e.activation(hi, ps, ACT.Copy), t, down_, parts.get(f - 4))
                parts[f] = self.v(lambda e: e.tensor_tensor(lo, ps, hi.bitcast(F32), ALU.subtract), act[f], down_)
                bk.free = parts[f]

            def down(f):
                g = f // nf
                ys = B[2 * (g % 2):2 * (g % 2) + 2]

                def fn(e, hi, lo):
                    for j in range(2):
                        xs = slice(((f + j) % 4) * T, ((f + j) % 4) * T + C)
                        for half in range(2):
                            ws = slice(j * D + half * 512, j * D + half * 512 + 512)
                            out = ys[half].t[:, :]
                            e.matmul(out, self.ahi[:, xs], hi[:, ws], start=((f + j) % nf == 0), stop=False)
                            e.matmul(out, self.ahi[:, xs], lo[:, ws], start=False, stop=False)
                            m = e.matmul(out, self.alo[:, xs], hi[:, ws], start=False, stop=((f + j) % nf == nf - 1))
                    return m
                first = [b.free for b in ys] if f % nf == 0 else []
                used[f] = sums[g] = self.chunk(name, fn, first, act[f], parts[f], act[f + 1], parts[f + 1])

            for kind, f in plan_experts():
                if kind == "d":
                    if f == NE * nf // 4 - 2:
                        turn_act(f + 1)
                    down(f)
                    continue
                product(f)
                g, at = f // nf, f % nf
                if g and at == 4:
                    collect(g - 1)
                    send(g - 1, 0)
                if g and at == 6:
                    send(g - 1, 1)
                if g and at == 8 and g + 1 < 4:
                    fetch(g + 1)
            collect(3)
            send(3, 0)
            send(3, 1)

        P.branch(flag[0:1, 0:1], known, compact, dense, self.held, self.hold)
        self.joined()
        self.layer_norm(lambda tt: y[tt], P.own("vector"), ln)

    def ffn(self, name, gain):
        self.begin()
        ready = self.rms_turn(gain, None)
        last = self.gated(name, plan_gated(F // 128), ready)
        for tt in range(2):
            for half in range(2):
                bk = self.bank[tt * 2 + half]
                x = self.x(tt)[:, half * 512:half * 512 + 512]
                bk.free = self.v(lambda e, x=x, bk=bk: e.scalar_tensor_tensor(x, bk.t[:, :], 0.5, x, ALU.mult, ALU.add),
                                 last)

    def add_moving(self, name, ready, bias=None):
        B = self.bank

        def evac(tt, n0, w, ps, tok):
            x = self.x(tt)[:, n0:n0 + w]
            t = self.v(lambda e: e.tensor_tensor(x, x, ps, ALU.add), tok)
            if bias is not None:
                t = self.v(lambda e: e.tensor_tensor(x, x, bias[:, n0:n0 + w], ALU.add))
            return t
        return self.moving(name, D, D, [(B[0], B[1]), (B[2], B[3])], evac, ready)

    def memory(self):
        P, cut = self.P, self.scr.cut
        now = self.begin()
        rows = self.rows_load("mem", "row_mem", now)
        mm = [cut(D) for _ in range(2)]
        t = None
        for tt in range(2):
            t = P.dma(self.d_x, lambda e, tt=tt: e.dma_start(mm[tt], self.d["mem"][tt * 128:(tt + 1) * 128, :]), now)
        self.junk = cut(D)
        done = []
        for tt in range(2):
            def one(tt=tt):
                r, t2 = self.rms_rows(mm[tt], 1, D, 1e-6, t, col=64 + 8 * tt)
                return self.v(lambda e: e.tensor_scalar(mm[tt], mm[tt], r, None, ALU.mult), t2)
            done.append(one())
        ready = self.turn(lambda tt: mm[tt], 8, done, scale=lambda k: self.vec("mem_norm", k))
        mk = [cut(D) for _ in range(2)]
        B = self.bank

        def evac(tt, n0, w, ps, tok):
            if n0 < D:
                return self.a(lambda e: e.activation(mk[tt][:, n0:n0 + w], ps, ACT.Copy), tok)
            return self.v(lambda e: e.tensor_copy(self.memv[tt][:, n0 - D:n0 - D + w], ps), tok)
        self.moving("mem_wkv", D, 2 * D, [(B[0], B[1]), (B[2], B[3])], evac, ready)
        done = [P.own("scalar"), P.own("vector")]
        self.head_norm(mk, 4, 256, self.row("mem", "kn"), [done, rows])
        self.heads_turned(lambda tt, i: mk[tt][:, i * 128:(i + 1) * 128], 8, 128, self.memk, P.own("vector"), B[4:8])

    def head_norm(self, x, H, w, gain, ready, base=96):
        for tt in range(2):
            def one(tt=tt):
                a = x[tt]
                r, t = self.rms_rows(a, H, w, 1e-6, ready, col=base + 32 * tt)
                self.v(lambda e: e.tensor_tensor(r3(a, w), r3(a, w), bc(r, 2, w), ALU.mult), t)
                return self.v(lambda e: e.tensor_tensor(r3(a, w), r3(a, w), bc(gain, 1, H), ALU.mult))
            one()

    def cross(self, l):
        P, cut = self.P, self.scr.cut
        now = self.begin()
        rows = self.rows_load("xat", f"row_xat{l}", now)
        ready = self.rms_turn(f"xattn_norm{l}", None)
        B = self.bank
        q = [cut(D) for _ in range(2)]

        def evac(tt, n0, w, ps, tok):
            return self.a(lambda e: e.activation(q[tt][:, n0:n0 + w], ps, ACT.Copy), tok)
        self.moving(f"xwq{l}", D, D, [(B[0], B[1]), (B[2], B[3])], evac, ready)
        self.head_norm(q, 4, 256, self.row("xat", "qn"), [P.own("scalar"), rows])
        qT = cut(8 * T)
        self.heads_turned(lambda tt, i: q[tt][:, i * 128:(i + 1) * 128], 8, 128, qT, P.own("vector"), B[4:8])
        ready = [P.own("scalar"), P.own("vector")]

        def scores(tt):
            def f(e, out, h, last):
                for c in range(2):
                    i = 2 * h + c
                    m = e.matmul(out, qT[:, i * T + tt * 128:i * T + tt * 128 + 128], self.memk[:, i * T:(i + 1) * T],
                                 start=(c == 0), stop=(c == 1))
                return m
            return f
        o = [cut(D) for _ in range(2)]
        self.att = cut(4096)
        units = [dict(tt=tt, heads=[0, 1, 2, 3], nk=256, dv=256, scale=1 / 16.0,
                      scores=scores(tt), out=o[tt], v=lambda j, k: self.memv[k][:, j * 256:(j + 1) * 256])
                 for tt in range(2)]
        done = self.attention(units, ready)
        ready = self.turn(lambda tt: o[tt], 8, done)
        self.add_moving(f"xwo{l}", ready)

    def swa(self):
        P, cut = self.P, self.scr.cut
        now = self.begin()
        rows = self.rows_load("swa", "row_swa", now)
        ali = cut(16 * T)
        late = P.dma(self.d_late, lambda e: e.dma_start(ali, self.d["alibi"]), now)
        R = lambda n: self.row("swa", n)
        mark = self.scr.at
        ready = self.rms_turn("mix_norm1", None)
        self.P.meet()
        self.scr.at = mark
        self.junk = cut(64)
        B = self.bank
        qkv = [cut(1536) for _ in range(2)]

        def evac(tt, n0, w, ps, tok):
            return self.v(lambda e: e.tensor_tensor(qkv[tt][:, n0:n0 + w], ps, R("bqkv")[:, n0:n0 + w], ALU.add), tok, rows)
        self.moving("wqkv", D, 1536, [(B[0], B[1]), (B[2], B[3])], evac, ready)
        done = P.own("vector")
        self.head_norm([x[:, 0:1024] for x in qkv], 16, 64, R("qn"), [done], base=96)
        self.head_norm([x[:, 1024:1280] for x in qkv], 4, 64, R("kn"), [done], base=160)
        qT, kT = cut(8 * T), cut(2 * T)
        t = P.own("vector")
        for up in range(2):
            self.heads_turned(lambda tt, i, up=up: qkv[tt][:, (8 * up + i) * 64:(8 * up + i + 1) * 64], 8, 64, qT, t,
                              B[4:8], p0=64 * up)
            self.heads_turned(lambda tt, i, up=up: qkv[tt][:, 1024 + (2 * up + i) * 64:1024 + (2 * up + i + 1) * 64],
                              2, 64, kT, t, B[4:8], p0=64 * up)
        ready = [P.own("scalar"), P.own("vector"), late]
        o = [self.gb_[:, 0:D], self.gb_[:, D:2 * D]]

        def scores(tt):
            def f(e, out, h, last):
                nk = 128 * (tt + 1)
                e.matmul(out, self.ident, ali3[:, h, 256 - nk:], start=True, stop=False)
                p0, i, k = h // 8 * 64, h % 8, h // 4 % 2
                return e.matmul(out, qT[p0:p0 + 64, i * T + tt * 128:i * T + tt * 128 + 128],
                                kT[p0:p0 + 64, k * T:k * T + nk], start=False, stop=True)
            return f
        ali3 = r3(ali, T)
        self.att = cut(4096)
        units = []
        for tt, n in ((0, 8), (1, 4)):
            for h0 in range(0, 16, n):
                units.append(dict(
                    tt=tt, heads=list(range(h0, h0 + n)), nk=128 * (tt + 1), dv=64, scale=0.125, scores=scores(tt),
                    sink=R("sink")[:, h0:h0 + n], out=o[tt][:, h0 * 64:(h0 + n) * 64],
                    v=lambda j, k, h0=h0: qkv[k][:, 1280 + (h0 + j) // 4 * 64:1280 + (h0 + j) // 4 * 64 + 64]))
        done = self.attention(units, ready)
        ready = self.turn(lambda tt: o[tt], 8, done)
        self.add_moving("wo", ready, bias=R("bo"))

    def ssd(self):
        P, cut = self.P, self.scr.cut
        now = self.begin()
        rows = self.rows_load("ssd", "row_ssd", now)
        R = lambda n: self.row("ssd", n)
        B = self.bank
        V, A, G = self.v, self.a, self.g
        h32 = cut(8 * T)
        mark = self.scr.at
        xn = [cut(D) for _ in range(2)]
        self.junk = cut(D)
        done = []
        for tt in range(2):
            r, t = self.rms_rows(self.x(tt), 1, D, 1e-6, None, col=64 + 8 * tt)
            done.append(V(lambda e, tt=tt, r=r: e.tensor_scalar(xn[tt], self.x(tt), r, None, ALU.mult), t))
        for n in range(4):
            bank = B[4 + n]

            def fn(e, n=n, bank=bank):
                for j in range(2):
                    for tt in range(2):
                        m = e.transpose(bank.t[:, j * T + tt * 128:j * T + tt * 128 + 128],
                                        xn[tt][:, (2 * n + j) * 128:(2 * n + j + 1) * 128], self.ident)
                return m
            t = self.pe(fn, done, bank.free)
            for j in range(2):
                k = 2 * n + j
                t = V(lambda e, k=k, j=j, bank=bank: e.tensor_scalar(
                    h32[:, k * T:(k + 1) * T], bank.t[:, j * T:(j + 1) * T], self.vec("mix_norm0", k), None, ALU.mult), t)
            bank.free = t

        def parts(after):
            t = A(lambda e: e.activation(self.thi[:, :], h32, ACT.Copy), after)
            return V(lambda e: e.tensor_tensor(self.tlo[:, :], h32, self.thi[:, :].bitcast(F32), ALU.subtract), t, after)
        ready = parts(P.own("vector"))
        self.P.meet()
        self.scr.at = mark
        u = [cut(D) for _ in range(2)]
        bands = cut(8 * T)
        late = P.dma(self.d_late, lambda e: e.dma_start(bands, self.d["bands"]), now, P.own("vector"), P.own("scalar"))

        def to_u(tt, n0, w, ps, tok):
            if tt == 0:
                return A(lambda e: e.activation(u[tt][:, n0:n0 + w], ps, ACT.Copy), tok)
            return V(lambda e: e.tensor_copy(u[tt][:, n0:n0 + w], ps), tok)
        self.moving("pool_in", D, D, [(B[0], B[1]), (B[2], B[3])], to_u, ready)
        used = P.own("tensor")
        done = [P.own("scalar"), P.own("vector"), late]
        bnd = bands.rearrange("p (s w t) -> p s w t", s=2, w=4)
        toks = []
        for w in range(4):
            bank = B[4 + w]

            def fn(e, w=w, bank=bank):
                for c in range(2):
                    for s in range(2):
                        m = e.matmul(bank.t[:, c * T:(c + 1) * T], u[s][:, w * 256 + c * 128:w * 256 + (c + 1) * 128],
                                     bnd[:, s, w, :], start=(s == 0), stop=(s == 1))
                return m
            t = self.pe(fn, done, bank.free)
            sl = slice(w * 512, (w + 1) * 512)
            t = A(lambda e, sl=sl, bank=bank: e.activation(self.thi[:, sl], bank.t[:, :], ACT.Copy), t, used)
            t = V(lambda e, sl=sl, bank=bank: e.tensor_tensor(self.tlo[:, sl], bank.t[:, :],
                                                              self.thi[:, sl].bitcast(F32), ALU.subtract), t)
            bank.free = t
            toks.append(t)

        def pools(e, hi, lo):
            for w in range(4):
                for o_ in range(2):
                    out = B[w].t[:, o_ * T:(o_ + 1) * T]
                    for k in range(2):
                        ws = slice(((w * 2 + o_) * 2 + k) * 128, ((w * 2 + o_) * 2 + k + 1) * 128)
                        xs = slice((w * 2 + k) * T, (w * 2 + k + 1) * T)
                        e.matmul(out, hi[:, ws], self.thi[:, xs], start=(k == 0), stop=False)
                        e.matmul(out, hi[:, ws], self.tlo[:, xs], start=False, stop=False)
                        m = e.matmul(out, lo[:, ws], self.thi[:, xs], start=False, stop=(k == 1))
            return m
        tok = self.chunk("pool_w", pools, toks, [b.free for b in B[0:4]])
        done = []
        for w in range(4):
            for o_ in range(2):
                k = 2 * w + o_
                ps, sl = B[w].t[:, o_ * T:(o_ + 1) * T], slice(k * T, (k + 1) * T)
                sc = self.vec("pool_scale", k)
                t = A(lambda e, ps=ps, sl=sl, sc=sc: e.activation(self.thi[:, sl], ps, ACT.Copy, scale=sc), tok)
            for o_ in range(2):
                k = 2 * w + o_
                ps, sl = B[w].t[:, o_ * T:(o_ + 1) * T], slice(k * T, (k + 1) * T)
                sc = self.vec("pool_scale", k)
                t = V(lambda e, ps=ps, sl=sl, sc=sc: e.scalar_tensor_tensor(
                    self.tlo[:, sl], ps, sc, self.thi[:, sl].bitcast(F32), ALU.mult, ALU.subtract), t)
            B[w].free = t
            done.append(t)
        self.add_moving("out_pool", done)
        ready = parts([P.own("tensor")])
        self.P.meet()
        self.scr.at = mark
        U = cut(12 * 260).rearrange("p (c t) -> p c t", t=260)
        cv = cut(12 * T)
        z0 = V(lambda e: e.memset(U[:, :, 0:4], 0.0))
        conv = {}
        for f in range(6):
            bank = B[f % 4]
            tok = self.pair_product("ssd_xbc", bank, ready)
            t = A(lambda e, f=f, bank=bank: e.activation(U[:, 2 * f:2 * f + 2, 4:260], r3(bank.t[:, :], T), ACT.Copy), tok)
            bank.free = t
            for c in (2 * f, 2 * f + 1):
                out = cv[:, c * T:(c + 1) * T]
                V(lambda e, c=c, out=out: e.tensor_scalar(out, U[:, c, 4:260], self.vec("conv_w", 36 + c), None, ALU.mult),
                  t, z0)
                for k in (2, 1, 0):
                    t2 = V(lambda e, c=c, out=out, k=k: e.scalar_tensor_tensor(
                        out, U[:, c, 1 + k:257 + k], self.vec("conv_w", 12 * k + c), out, ALU.mult, ALU.add))
                conv[c] = A(lambda e, c=c, out=out: e.activation(out, out, ACT.Silu, bias=self.vec("conv_b", c)), t2)
        z = [h32[:, 0:D], h32[:, D:2 * D]]
        dtr = [self.st[:, 0:16], self.st[:, 16:32]]

        def to_z(tt, n0, w, ps, tok):
            if n0 < D:
                return A(lambda e: e.activation(z[tt][:, n0:n0 + w], ps, ACT.Silu), tok)
            return V(lambda e: e.tensor_copy(dtr[tt], ps), tok)
        self.moving("ssd_z", D, D + 16, [(B[0], B[1]), (B[2], B[3])], to_z, ready)
        self.P.meet()
        self.scr.at = mark
        xs = [cut(D) for _ in range(2)]
        Bt, cb = cut(256), cut(512)
        self.scr.at = mark + 12 * 260 + 12 * T
        both, tmp, ea = self.st[:, 0:32], self.st[:, 32:64], self.st[:, 64:80]
        dt = dtr
        V(lambda e: e.tensor_tensor(r3(both, 16), r3(both, 16), bc(R("dtb"), 1, 2), ALU.add), rows)
        t = V(lambda e: e.tensor_scalar(tmp, both, 0.0, None, ALU.max))
        A(lambda e: e.activation(both, both, ACT.Abs), t)
        A(lambda e: e.activation(both, both, ACT.Exp, scale=-1.0))
        A(lambda e: e.activation(both, both, ACT.Ln, bias=1.0))
        t = A(lambda e: e.activation(ea, R("alog"), ACT.Exp))
        V(lambda e: e.tensor_tensor(both, both, tmp, ALU.add), t)
        V(lambda e: e.tensor_scalar(ea, ea, -1.0, None, ALU.mult))
        adt = self.st[:, 80:112]
        t = V(lambda e: e.tensor_tensor(r3(adt, 16), r3(both, 16), bc(ea, 1, 2), ALU.mult))
        bank = B[4]
        acs, dfs, dte = self.st[:, 112:144], self.st[:, 144:160], self.st[:, 160:176]

        def cums(e):
            e.matmul(bank.t[:, 0:16], self.tri, adt[:, 0:16], start=True, stop=True)
            e.matmul(bank.t[:, 16:32], self.tri, adt[:, 16:32], start=True, stop=True)
            return e.matmul(bank.t[:, 32:48], self.ones, adt[:, 0:16], start=True, stop=True)
        t = self.pe(cums, t, bank.free)
        V(lambda e: e.tensor_copy(acs, bank.t[:, 0:32]), t)
        bank.free = V(lambda e: e.tensor_tensor(dte, bank.t[:, 32:48], acs[:, 0:16], ALU.subtract))
        t = P.own("vector")
        A(lambda e: e.activation(dte, dte, ACT.Exp), t)
        t_exp = A(lambda e: e.activation(dfs, acs[:, 16:32], ACT.Exp))
        for n in range(4):
            bk = B[5 + n % 3]
            tt, half = n // 2, n % 2

            def fn(e, tt=tt, half=half, bk=bk):
                for j in range(4):
                    c = half * 4 + j
                    m = e.transpose(bk.t[:, j * 128:(j + 1) * 128], cv[:, c * T + tt * 128:c * T + tt * 128 + 128],
                                    self.ident)
                return m
            t = self.pe(fn, bk.free)
            bk.free = A(lambda e, tt=tt, half=half, bk=bk: e.activation(
                xs[tt][:, half * 512:half * 512 + 512], bk.t[:, :], ACT.Copy), t)
        bk = B[5]

        def fn(e):
            for g in range(2):
                m = e.transpose(bk.t[:, g * 128:(g + 1) * 128], cv[:, (8 + g) * T:(8 + g) * T + 128], self.ident)
            return m
        t = self.pe(fn, bk.free)
        bk.free = A(lambda e: e.activation(Bt, bk.t[:, 0:256], ACT.Copy), t)
        t = P.own("scalar")
        xr = [cut(D) for _ in range(2)]
        xd = cut(D)
        for tt in range(2):
            V(lambda e, tt=tt: e.tensor_tensor(r3(xr[tt], 64), r3(xs[tt], 64), bc(dt[tt], 2, 64), ALU.mult), t)
        xready = V(lambda e: e.tensor_tensor(r3(xd, 64), r3(xr[0], 64), bc(dte, 2, 64), ALU.mult), t_exp)
        sts = cut(D)
        for g in range(2):
            bk = B[6 + g]
            t = self.pe(lambda e, g=g, bk=bk: e.matmul(bk.t[:, :], Bt[:, g * 128:(g + 1) * 128],
                                                      xd[:, g * 512:(g + 1) * 512], start=True, stop=True),
                        xready, P.own("scalar"), bk.free)
            bk.free = A(lambda e, g=g, bk=bk: e.activation(sts[:, g * 512:(g + 1) * 512], bk.t[:, :], ACT.Copy), t)
        st_ready = P.own("scalar")
        bk5 = B[5]

        def fcb(e):
            for tt in range(2):
                for g in range(2):
                    m = e.matmul(bk5.t[:, (2 * tt + g) * 128:(2 * tt + g + 1) * 128],
                                 cv[:, (8 + g) * T + tt * 128:(8 + g) * T + tt * 128 + 128],
                                 cv[:, (10 + g) * T + tt * 128:(10 + g) * T + tt * 128 + 128], start=True, stop=True)
            return m
        t = self.pe(fcb, bk5.free)
        bk5.free = A(lambda e: e.activation(cb, bk5.t[:, :], ACT.Copy), t)
        cbt = P.own("scalar")
        ab = self.gb_
        M = cut(16 * 128)
        y = [cv[:, 0:D], cv[:, D:2 * D]]
        mseg = self.c("mseg")
        mt, spent = {}, {}
        qbanks = [B[0], B[1], B[4], B[5]]
        for tt in range(2):
            def quarter(tt, hb):
                a = ab[:, hb * 512:(hb + 1) * 512]
                t = V(lambda e: e.tensor_copy(r3(a, 128), bc(adt[:, tt * 16 + hb * 4:tt * 16 + hb * 4 + 4], 2, 128)),
                      self.abused.get(hb))
                yield
                bk = qbanks[hb]

                def fn(e):
                    for j in range(4):
                        m = e.matmul(bk.t[:, j * 128:(j + 1) * 128], a[:, j * 128:(j + 1) * 128], self.tri,
                                     start=True, stop=True)
                    return m
                t = self.pe(fn, t, bk.free)
                self.abused[hb] = t
                yield
                m4 = M[:, hb * 512:(hb + 1) * 512]
                m3 = r3(m4, 128)
                t = V(lambda e: e.tensor_tensor(m3, r3(bk.t[:, :], 128),
                                                bc(acs[:, tt * 16 + hb * 4:tt * 16 + hb * 4 + 4], 2, 128),
                                                ALU.subtract), t, spent.get((tt - 1, hb // 2)))
                bk.free = t
                yield
                t = G(lambda e: e.tensor_tensor(m3, m3, bc(mseg, 1, 4), ALU.add), t)
                yield
                t = A(lambda e: e.activation(m4, m4, ACT.Exp), t)
                yield
                g = hb // 2
                mt[tt, hb] = V(lambda e: e.tensor_tensor(
                    m3, m3, bc(cb[:, (2 * tt + g) * 128:(2 * tt + g + 1) * 128], 1, 4), ALU.mult), t, cbt)
            interleave([quarter(tt, hb) for hb in range(4)], 4)
            for g in range(2):
                def half(tt=tt, g=g):
                    bk = B[2 + g]

                    def fn(e):
                        for j in range(8):
                            h = g * 8 + j
                            m = e.matmul(bk.t[:, j * 64:(j + 1) * 64], M[:, h * 128:(h + 1) * 128],
                                         xr[tt][:, h * 64:(h + 1) * 64], start=True, stop=True)
                        return m
                    t = self.pe(fn, mt[tt, 2 * g], mt[tt, 2 * g + 1], xready, bk.free)
                    spent[tt, g] = t
                    yy = y[tt][:, g * 512:(g + 1) * 512]
                    x_ = xs[tt][:, g * 512:(g + 1) * 512]
                    V(lambda e: e.tensor_tensor(r3(yy, 64), r3(x_, 64), bc(R("dskip")[:, g * 8:g * 8 + 8], 2, 64), ALU.mult))
                    bk.free = V(lambda e: e.tensor_tensor(yy, yy, bk.t[:, :], ALU.add), t)
                    if tt == 1:
                        b2 = B[6 + g]
                        t = self.pe(lambda e: e.matmul(b2.t[:, :], cv[:, (10 + g) * T + 128:(10 + g) * T + 256],
                                                       sts[:, g * 512:(g + 1) * 512], start=True, stop=True),
                                    st_ready, b2.free)
                        t = V(lambda e: e.tensor_tensor(r3(x_, 64), r3(b2.t[:, :], 64),
                                                        bc(dfs[:, g * 8:g * 8 + 8], 2, 64), ALU.mult), t)
                        b2.free = t
                        V(lambda e: e.tensor_tensor(yy, yy, x_, ALU.add))
                    return V(lambda e: e.tensor_tensor(yy, yy, z[tt][:, g * 512:(g + 1) * 512], ALU.mult))
                half()
        self.junk = M[:, 0:512]
        t = [P.own("vector"), P.own("tensor")]
        done = []
        for tt in range(2):
            def one(tt=tt):
                r, t2 = self.rms_rows(y[tt], 2, 512, 1e-6, t, col=176 + 8 * tt)
                return V(lambda e: e.tensor_tensor(r3(y[tt], 512), r3(y[tt], 512), bc(r, 2, 512), ALU.mult), t2)
            done.append(one())
        ready = self.turn(lambda tt: y[tt], 8, done, scale=lambda k: self.vec("ssd_norm", k))
        self.add_moving("out_ssd", ready)


def program(nc, d, out, upto=99):
    with ExitStack() as ctx:
        K = Kernel(nc, ctx, d)
        P = K.P
        K.small = ctx.enter_context(nc.sbuf_tensor("small", [128, 100], F32))
        K.abused, K.mused = {}, None
        K.flag = K.small[:, 96:97].bitcast(I32)
        K.begin_program()
        steps = []
        for l in range(DEPTH):
            steps += [lambda l=l: K.mixer(l), lambda l=l: K.moe(l)]

        def late():
            K.memk = K.scr.t[:, K.scr.size - 2048:K.scr.size]
            K.memv = [K.scr.t[:, K.scr.size - 4096:K.scr.size - 3072], K.scr.t[:, K.scr.size - 3072:K.scr.size - 2048]]
            K.scr.size -= 4096
            K.memory()
        steps += [late, lambda: K.ffn("ffn10", "ffn1_norm0"), K.ssd, lambda: K.cross(0),
                  lambda: K.ffn("ffn20", "ffn2_norm0"), lambda: K.ffn("ffn11", "ffn1_norm1"), K.swa,
                  lambda: K.cross(1), lambda: K.ffn("ffn21", "ffn2_norm1")]
        for step in steps[:upto]:
            step()
        now = P.meet()
        for tt in range(2):
            last = P.dma(K.d_out, lambda e, tt=tt: e.dma_start(out[tt * 128:(tt + 1) * 128, :], K.x(tt)), now)
        P.gate["sync"] = []
        with nc.Block() as block:
            P.emit(block, last)




def kernel(**inputs):
    from concourse import bacc
    from concourse.bass_utils import run_bass_kernel_spmd

    i = {k: np.asarray(v) for k, v in inputs.items()}
    arrays = {**pack_weights(i), **pack_small(i)}
    nc = bacc.Bacc("TRN2", target_bir_lowering=False, num_devices=1)
    d = {n: nc.dram_tensor("in_" + n, a.shape, mybir.dt.from_np(a.dtype), kind="ExternalInput").ap()
         for n, a in arrays.items()}
    out = nc.dram_tensor("out_x", (T, D), F32, kind="ExternalOutput").ap()
    program(nc, d, out)
    r = run_bass_kernel_spmd(nc, [{"in_" + n: a for n, a in arrays.items()}], core_ids=[0])
    return r.results[0]["out_x"].reshape(1, T, D)
```

```python
from contextlib import ExitStack
import math

import numpy as np
import concourse.bass as bass
from concourse import mybir

F32 = mybir.dt.float32
F32R = mybir.dt.float32r
I32 = mybir.dt.int32
ACT = mybir.ActivationFunctionType
ALU = mybir.AluOpType
AXX = mybir.AxisListType.X

D, T, DEPTH, HD = 1024, 256, 2, 64
F, NE, FE = 2816, 16, 512
CW = 2048
NS, NR = 3, 3
ALPHA = (2 * DEPTH) ** 0.25
NEG = -1e30
MAGIC = 12582912.0
SPLITS = (384, 256, 32, 256, 256, 256, 256, 256, 256, 4)
IN_COLS = sum(SPLITS)
OFF = [sum(SPLITS[:i]) for i in range(len(SPLITS))]



def constants():
    p = np.arange(128)
    out = {}
    out["ident"] = np.eye(128)
    out["zto"] = np.concatenate([np.zeros((128, 128)), (p[:, None] <= p[None, :]) * 1.0, np.ones((128, 128))], axis=1)
    k = np.arange(256)
    q1 = 128 + p
    out["mchunk"] = np.where(k[None, :] // 64 <= q1[:, None] // 64, 0.0, NEG)
    out["mframe"] = np.where(k[None, :] <= q1[:, None], 0.0, NEG)
    out["mseg"] = np.where(p[:, None] <= p[None, :], 0.0, NEG)
    fm = [500000.0 ** (-i / 32) for i in range(0, 32, 2)]
    fd = [500000.0 ** (-i / 8) for i in range(0, 8, 2)]
    out["invf"] = np.tile(np.array(fm + fd), (128, 1))
    out["iota"] = np.tile(np.arange(128), (128, 1))
    out["c4"] = np.tile(np.arange(4, 0, -1), (128, 1))
    out["c16"] = np.tile(np.arange(16, 0, -1), (128, 1))
    out["half"] = np.full((128, 8), -0.5)
    return out


def mask_constants():
    c = constants()
    return np.concatenate([c["ident"], c["mchunk"], c["mframe"]], axis=1)


def late_constants():
    p = np.arange(128)
    k = np.arange(256)
    t = np.arange(256)
    bands = np.zeros((128, 2, 4, 256))
    for w in range(4):
        n = 2 << w
        for s in range(2):
            si = s * 128 + p
            d = t[None, :] - si[:, None]
            cnt = np.minimum(t + 1, n)
            bands[:, s, w, :] = ((d >= 0) & (d < n)) / cnt[None, :] - (d == 0)
    dist = (128 + p)[:, None] - k[None, :]
    slopes = 2.0 ** (-8.0 * (np.arange(16) + 1) / 16)
    ali = np.where((dist >= 0) & (dist < 128), 0.0, NEG)[:, None, :] - slopes[None, :, None] * dist[:, None, :]
    ali = np.where(ali > 0.5 * NEG, 8.0 * ali, NEG)
    e = np.zeros((128, 16, 128))
    for i in range(16):
        e[i, i, :] = 1.0
    return {"esel": e.reshape(128, -1)[:16], "bands": bands.reshape(128, -1), "alibi": ali.reshape(128, -1)}


def layout(parts):
    at, out = 0, {}
    for name, a in parts.items():
        out[name] = (at, a.shape[1])
        at += a.shape[1]
    return out, at


CONST, NCONST = layout(constants())

VECS = [("mem_norm", 8), ("ffn1_norm0", 8), ("ffn1_norm1", 8), ("mix_norm0", 8), ("mix_norm1", 8),
        ("xattn_norm0", 8), ("xattn_norm1", 8), ("ffn2_norm0", 8), ("ffn2_norm1", 8), ("ssd_norm", 8),
        ("pool_scale", 8), ("conv_b", 12), ("conv_w", 48)]
VAT, NV = {}, 0
for _n, _c in VECS:
    VAT[_n] = NV
    NV += _c

ROWS = {
    "mla": [("qg", 384), ("kvg", 256), ("subln", 64), ("fb", 4), ("lq1", 32), ("lq2", 32), ("lk1", 32), ("lk2", 32)],
    "moe": [("rb", 16)],
    "ssd": [("dtb", 16), ("alog", 16), ("dskip", 16)],
    "swa": [("bqkv", 1536), ("qn", 64), ("kn", 64), ("sink", 16), ("bo", 1024)],
    "mem": [("kn", 256)],
    "xat": [("qn", 256)],
}


def row_at(stage, name):
    at = 0
    for n, c in ROWS[stage]:
        if n == name:
            return at, at + c
        at += c
    raise KeyError(name)


def row_len(stage):
    return sum(c for _, c in ROWS[stage])




def plan_moving(K, N):
    out = []
    for n0 in range(0, N, 512):
        w = min(512, N - n0)
        per = CW // w
        kt = K // 128
        for k0 in range(0, kt, per):
            out.append((n0, w, k0, min(per, kt - k0)))
    return out


def pack_moving(W):
    K, N = W.shape
    return [W[k0 * 128:(k0 + n) * 128, n0:n0 + w].reshape(n, 128, w).transpose(1, 0, 2).reshape(-1)
            for n0, w, k0, n in plan_moving(K, N)]


def pack_pair(G, U, f):
    g = G[:, f * 128:(f + 1) * 128].reshape(-1, 128, 128).transpose(1, 0, 2)
    u = U[:, f * 128:(f + 1) * 128].reshape(-1, 128, 128).transpose(1, 0, 2)
    return np.stack([g, u], axis=1).reshape(-1)


def pack_down(W, f):
    return W[f * 128:(f + 2) * 128].reshape(2, 128, -1).transpose(1, 0, 2).reshape(-1)


def plan_gated(nf):
    out = []
    for f in range(0, nf, 2):
        out += [("gu", f), ("gu", f + 1)]
        if f >= 2:
            out.append(("d", f - 2))
    return out + [("d", nf - 2)]


def pack_gated(G, U, W):
    return [pack_pair(G, U, f) if kind == "gu" else pack_down(W, f) for kind, f in plan_gated(G.shape[1] // 128)]


def plan_experts():
    return plan_gated(NE * FE // 128)


def pack_experts(G, U, W):
    nf = FE // 128
    return [pack_pair(G[f // nf], U[f // nf], f % nf) if kind == "gu" else pack_down(W[f // nf], f % nf)
            for kind, f in plan_experts()]


def sizes_moving(K, N):
    return [w * n for _, w, _, n in plan_moving(K, N)]


STREAM = []
for _l in range(DEPTH):
    STREAM += [(f"w_in{_l}", sizes_moving(D, IN_COLS)), (f"uq{_l}", sizes_moving(384, 768)),
               (f"ukv{_l}", sizes_moving(256, 1024)), (f"w_out{_l}", sizes_moving(D, D)),
               (f"exp{_l}", [CW] * len(plan_experts()))]
STREAM += [("mem_wkv", sizes_moving(D, 2 * D)), ("ffn10", [CW] * len(plan_gated(F // 128))),
           ("ssd_xbc", [CW] * 6), ("ssd_z", sizes_moving(D, D + 16)), ("pool_in", sizes_moving(D, D)),
           ("pool_w", [CW]), ("out_pool", sizes_moving(D, D)), ("out_ssd", sizes_moving(D, D)),
           ("xwq0", sizes_moving(D, D)), ("xwo0", sizes_moving(D, D)), ("ffn20", [CW] * len(plan_gated(F // 128))),
           ("ffn11", [CW] * len(plan_gated(F // 128))), ("wqkv", sizes_moving(D, 1536)), ("wo", sizes_moving(D, D)),
           ("xwq1", sizes_moving(D, D)), ("xwo1", sizes_moving(D, D)), ("ffn21", [CW] * len(plan_gated(F // 128)))]


def pack_weights(i):
    out = {}
    for l in range(DEPTH):
        out[f"w_in{l}"] = pack_moving(i["w_in"][l])
        out[f"uq{l}"] = pack_moving(i["mla_w_uq"][l])
        out[f"ukv{l}"] = pack_moving(i["mla_w_ukv"][l])
        out[f"w_out{l}"] = pack_moving(i["w_out"][l])
        out[f"exp{l}"] = pack_experts(i["exp_w_gate"][l], i["exp_w_up"][l], i["exp_w_down"][l])
        for n in ("ffn1", "ffn2"):
            wi = i[n + "_wi_2"][l]
            out[f"{n}{l}"] = pack_gated(wi[:, :F], wi[:, F:], i[n + "_wo_2"][l])
        out[f"xwq{l}"] = pack_moving(i["xattn_wq_2"][l])
        out[f"xwo{l}"] = pack_moving(i["xattn_wo_2"][l])
    out["mem_wkv"] = pack_moving(i["mem_wkv_2"])
    w = i["ssd_in_proj_2"][0]
    out["ssd_z"] = pack_moving(np.concatenate([w[:, :1024], w[:, 2560:2576]], axis=1))
    out["pool_in"] = pack_moving(w[:, 2576:3600])
    x = w[:, 1024:2560].reshape(D, 12, 128)
    even, odd = x[:, 0::2].reshape(D, 768), x[:, 1::2].reshape(D, 768)
    out["ssd_xbc"] = [pack_pair(even, odd, f) for f in range(6)]
    pw = i["pool_w_2"][0].reshape(4, 2, 128, 2, 128)
    out["pool_w"] = [pw.transpose(2, 0, 3, 1, 4).reshape(-1)]
    out["out_ssd"] = pack_moving(i["even_out_proj_2"][0][:1024])
    out["out_pool"] = pack_moving(i["even_out_proj_2"][0][1024:])
    out["wqkv"] = pack_moving(i["attn_wqkv_2"][0])
    out["wo"] = pack_moving(i["attn_wo_2"][0])
    return {n: np.concatenate(out[n]) for n, _ in STREAM}


def pack_small(i):
    f = np.float32
    out = {"const": np.concatenate(list(constants().values()), axis=1).astype(f)}
    for n, a in late_constants().items():
        out[n] = a.astype(f)
    out["masks"] = mask_constants().astype(f)
    v = {"mem_norm": i["mem_norm_2"], "ssd_norm": i["ssd_norm_2"][0], "pool_scale": i["pool_scale_2"][0],
         "conv_b": i["ssd_conv_b_2"][0], "conv_w": i["ssd_conv_w_2"][0].reshape(-1)}
    for l in range(DEPTH):
        for n in ("ffn1_norm", "mix_norm", "xattn_norm", "ffn2_norm"):
            v[f"{n}{l}"] = i[n + "_2"][l]
    out["vecs"] = np.ascontiguousarray(np.concatenate([v[n].reshape(-1, 128) for n, _ in VECS], axis=0).T)
    for l in range(DEPTH):
        out[f"row_mla{l}"] = np.concatenate([i["mla_q_norm_g"][l], i["mla_kv_norm_g"][l], i["diff_subln_g"][l],
                                             i["fox_f_bias"][l], i["diff_lam_q1"][l], i["diff_lam_q2"][l],
                                             i["diff_lam_k1"][l], i["diff_lam_k2"][l]])
        out[f"row_ln1{l}"] = np.concatenate([i["ln1_g"][l], i["ln1_b"][l]])
        out[f"row_ln2{l}"] = np.concatenate([i["ln2_g"][l], i["ln2_b"][l]])
        out[f"row_xat{l}"] = i["xattn_qnorm_2"][l]
    out["row_moe"] = i["router_bias"]
    out["row_lnin"] = np.concatenate([i["ln_in_g"], i["ln_in_b"]])
    out["row_ssd"] = np.concatenate([i["ssd_dt_bias_2"][0], i["ssd_a_log_2"][0], i["ssd_d_2"][0]])
    out["row_swa"] = np.concatenate([i["attn_bqkv_2"][0], i["attn_qnorm_2"][0], i["attn_knorm_2"][0],
                                     i["attn_sinks_2"][0], i["attn_bo_2"][0]])
    out["row_mem"] = i["mem_knorm_2"]
    out["x"] = i["x"][0]
    out["mem"] = i["mem_2"][0]
    out["pos"] = np.ascontiguousarray(i["positions"].reshape(2, 128).T)
    out["router"] = np.ascontiguousarray(i["router_w"].reshape(8, 128, 16).transpose(1, 0, 2).reshape(128, 128))
    return out



class Program:

    ENGINES = ("sync", "tensor", "vector", "scalar", "gpsimd")

    def __init__(self, nc, ctx):
        self.nc, self.ctx = nc, ctx
        self.todo = {e: [] for e in self.ENGINES}
        self.done = {e: 0 for e in self.ENGINES}
        self.sems = {e: ctx.enter_context(nc.semaphore("s_" + e)) for e in self.ENGINES}
        self.gate = {e: [] for e in self.ENGINES}

    def sem(self, name):
        self.sems[name] = self.ctx.enter_context(self.nc.semaphore(name))
        self.done[name] = 0
        return name

    def op(self, engine, fn, *after):
        waits = list(after) + self.gate[engine]
        self.gate[engine] = []
        self.done[engine] += 1
        self.todo[engine].append((waits, fn, engine, 1))
        return (engine, self.done[engine])

    def dma(self, sem, fn, *after, engine="sync"):
        self.done[sem] += 16
        self.todo[engine].append((list(after), fn, sem, 16))
        return (sem, self.done[sem])

    def own(self, engine):
        return (engine, self.done[engine])

    def meet(self):
        now = [self.own(e) for e in ("tensor", "vector", "scalar", "gpsimd")]
        for e in ("tensor", "vector", "scalar", "gpsimd"):
            self.gate[e] = list(now)
        return now

    def branch(self, flag, known, yes, no, held, hold):
        outer, start, gates = self.todo, dict(self.done), {e: list(g) for e, g in self.gate.items()}
        kept = held()
        ways = []
        for way in (yes, no):
            self.todo = {e: [] for e in self.ENGINES}
            self.done = dict(start)
            self.gate = {e: list(g) for e, g in gates.items()}
            hold(kept)
            way()
            ways.append((self.todo, dict(self.done)))
        self.todo = outer
        self.done = {s: max(w[1][s] for w in ways) for s in start}
        for e in self.ENGINES:
            both = []
            for todo, done in ways:
                short = self.done[e] - done[e]
                pad = [([(e, done[e])], lambda eng: eng.nop(), e, short)] if short else []
                both.append(todo[e] + pad)
            if both[0] or both[1]:
                self.todo[e].append(("branch", (flag, known), *both))
        assert all(self.done[s] == w[1][s] for w in ways for s in start if s not in self.ENGINES)
        self.meet()

    def emit(self, block, last):
        def flat(x):
            for t in x:
                if isinstance(t, list):
                    yield from flat(t)
                elif t is not None:
                    yield t

        def play(eng, todo, seen):
            for waits, fn, sem, n in todo:
                if waits == "branch":
                    flag, known = fn
                    eng.wait_ge(self.sems[known[0]], known[1])
                    seen[known[0]] = max(seen.get(known[0], 0), known[1])
                    taken = eng.value_load(flag, min_val=0, max_val=1)
                    with eng.If(taken == 1):
                        play(eng, sem, dict(seen))
                    with eng.Else():
                        play(eng, n, dict(seen))
                    continue
                for s, v in flat(waits):
                    if v > seen.get(s, 0):
                        eng.wait_ge(self.sems[s], v)
                        seen[s] = v
                fn(eng).then_inc(self.sems[sem], n)

        def run(engine):
            def body(eng):
                play(eng, self.todo[engine], {})
                if engine == "sync":
                    eng.wait_ge(self.sems[last[0]], last[1])
            return body

        block.sync(run("sync"))
        block.tensor(run("tensor"))
        block.vector(run("vector"))
        block.scalar(run("scalar"))
        block.gpsimd(run("gpsimd"))


def woven(steps, width):
    going, left = [], list(steps)
    while going or left:
        if len(going) < width and left:
            going.append(left.pop(0))
        for gen in list(going):
            try:
                next(gen)
            except StopIteration:
                going.remove(gen)
        yield


def interleave(steps, width):
    for _ in woven(steps, width):
        pass


class Bank:

    def __init__(self, tensor):
        self.t = tensor
        self.free = None


class Scratch:

    def __init__(self, tensor, size):
        self.t, self.size, self.at = tensor, size, 0

    def cut(self, n):
        a = self.at
        self.at += n
        assert self.at <= self.size, self.at
        return self.t[:, a:a + n]


def bc(ap, axis, n):
    ap = ap.unsqueeze(axis)
    shape = list(ap.shape)
    shape[axis] = n
    return ap.broadcast_to(shape)


def r3(ap, b):
    return ap.rearrange("p (a b) -> p a b", b=b)


class Turned(list):
    pass


class Kernel:

    def __init__(self, nc, ctx, d):
        self.nc, self.d = nc, d
        self.P = Program(nc, ctx)

        def sb(name, n, dt=F32, p=128):
            return ctx.enter_context(nc.sbuf_tensor(name, [p, n], dt))

        self.stage = [sb(f"stage{i}", CW) for i in range(NS)]
        self.hi = [sb(f"hi{i}", CW, F32R) for i in range(NR)]
        self.lo = [sb(f"lo{i}", CW, F32R) for i in range(NR)]
        self.thi = sb("thi", 8 * T, F32R)
        self.tlo = sb("tlo", 8 * T, F32R)
        self.ahi = sb("ahi", 4 * T, F32R)
        self.alo = sb("alo", 4 * T, F32R)
        self.X = sb("X", 2 * D)
        self.gb_ = sb("gb_", 2 * D)
        self.rows = sb("rows", max(row_len(s) for s in ROWS))
        self.const = sb("const_sb", NCONST)
        self.vecs = sb("vecs_sb", NV)
        self.maskr = sb("maskr", 640, F32R)
        self.identr = self.maskr[:, 0:128]
        self.st = sb("st", 288)
        self.rw = self.rows[:, row_len("swa") - 128:row_len("swa")]
        n = 19240
        self.scr = Scratch(sb("scr", n), n)
        self.bank = [Bank(ctx.enter_context(nc.psum_tensor(f"bank{i}", [128, 512], F32))) for i in range(8)]
        self.d_stage = [self.P.sem(f"d_stage{i}") for i in range(NS)]
        self.d_const = self.P.sem("d_const")
        self.d_x = self.P.sem("d_x")
        self.d_rw = self.P.sem("d_rw")
        self.d_row = self.P.sem("d_row")
        self.d_ln = self.P.sem("d_ln")
        self.d_late = self.P.sem("d_late")
        self.d_out = self.P.sem("d_out")
        self.ident = self.c("ident")
        self.zto = self.c("zto")
        self.tri, self.ones = self.zto[:, 128:256], self.zto[:, 256:384]
        self.chunks = []
        for name, sizes in STREAM:
            at = 0
            for n in sizes:
                self.chunks.append((name, at, n))
                at += 128 * n
        self.at = 0
        self.loaded, self.rounded, self.parted, self.used = {}, {}, {}, {}

    def start(self):
        for i in range(NS):
            self.load(i)
        for i in range(NR - 1):
            self.split(i)
            self.load(i + NS)

    def c(self, name):
        a, n = CONST[name]
        return self.const[:, a:a + n]

    def vec(self, name, k):
        a = VAT[name] + k
        return self.vecs[:, a:a + 1]

    def row(self, stage, name):
        a, b = row_at(stage, name)
        return self.rows[:, a:b]

    def v(self, fn, *after):
        return self.P.op("vector", fn, self.P.own("vector"), *after)

    def a(self, fn, *after):
        return self.P.op("scalar", fn, self.P.own("scalar"), *after)

    def g(self, fn, *after):
        return self.P.op("gpsimd", fn, self.P.own("gpsimd"), *after)

    def pe(self, fn, *after):
        return self.P.op("tensor", fn, *after)

    def load(self, i):
        if i >= len(self.chunks):
            return
        name, at, n = self.chunks[i]
        src = self.d[name][at:at + 128 * n].rearrange("(p c) -> p c", p=128)
        dst = self.stage[i % NS][:, :n]
        before = [self.rounded[i - NS], self.parted[i - NS]] if i >= NS else []
        self.loaded[i] = self.P.dma(self.d_stage[i % NS], lambda e: e.dma_start(dst, src), *before)

    def split(self, i):
        if i >= len(self.chunks):
            return
        n = self.chunks[i][2]
        src = self.stage[i % NS][:, :n]
        hi, lo = self.hi[i % NR][:, :n], self.lo[i % NR][:, :n]
        last = self.used.get(i - NR)
        old = self.parted.get(i - NR)
        m = n // 2

        def part(a, b, *after):
            s_, h_, l_ = src[:, a:b], hi[:, a:b], lo[:, a:b]
            r = self.P.op("scalar", lambda e: e.activation(h_, s_, ACT.Copy), self.loaded[i], last, old)
            return r, (l_, s_, h_)
        both = [part(0, m), part(m, n)]
        for r, (l_, s_, h_) in both:
            self.parted[i] = self.P.op("vector", lambda e, l_=l_, s_=s_, h_=h_: e.tensor_tensor(
                l_, s_, h_.bitcast(F32), ALU.subtract), self.loaded[i], r, last)
        self.rounded[i] = both[1][0]

    def chunk(self, name, fn, *after, between=None):
        i = self.at
        assert self.chunks[i][0] == name, (self.chunks[i], name)
        self.at += 1
        hi, lo = self.hi[i % NR], self.lo[i % NR]
        parts = fn if isinstance(fn, list) else [(fn, None)]
        before = [self.rounded[i], self.parted[i], *after]
        self.pieces = []
        for f, need in parts:
            tok = self.P.op("tensor", lambda e, f=f: f(e, hi, lo), before, need)
            self.pieces.append(tok)
        self.used[i] = tok
        self.split(i + NR - 1)
        self.load(i + NR - 1 + NS)
        if between is not None:
            between(tok)
        return tok

    def moving(self, *args, **kw):
        interleave([self.moving_steps(*args, **kw)], 1)

    def moving_steps(self, name, K, N, banks, evac, ready, src=None):
        plan = plan_moving(K, N)
        thi, tlo = src or (self.thi, self.tlo)
        kt = K // 128
        turn = 0
        for n0, w, k0, n in plan:
            pair = banks[turn % len(banks)]

            def fn(e, hi, lo, js, tts=range(2), n0=n0, w=w, k0=k0, n=n, pair=pair):
                for j in js:
                    for tt in tts:
                        xs = slice((k0 + j) * T + tt * 128, (k0 + j) * T + tt * 128 + 128)
                        ws = slice(j * w, (j + 1) * w)
                        out = pair[tt].t[:, :w]
                        e.matmul(out, thi[:, xs], hi[:, ws], start=(k0 + j == 0), stop=False)
                        e.matmul(out, thi[:, xs], lo[:, ws], start=False, stop=False)
                        m = e.matmul(out, tlo[:, xs], hi[:, ws], start=False, stop=(k0 + j == kt - 1))
                return m
            if isinstance(ready, Turned) and n0 == 0:
                parts = [(lambda e, hi, lo, j=j, fn=fn: fn(e, hi, lo, [j]), ready[(k0 + j) // 2]) for j in range(n)]
            elif k0 + n == kt:
                parts = [(lambda e, hi, lo, n=n, fn=fn, tt=tt: fn(e, hi, lo, range(n), [tt]), ready) for tt in range(2)]
            else:
                parts = [(lambda e, hi, lo, n=n, fn=fn: fn(e, hi, lo, range(n)), ready)]
            tok = self.chunk(name, parts, pair[0].free, pair[1].free)
            if k0 + n == kt:
                toks = self.pieces if not isinstance(ready, Turned) or n0 else [tok, tok]
                for tt, tok in enumerate(toks):
                    pair[tt].free = evac(tt, n0, w, pair[tt].t[:, :w], tok)
                turn += 1
            yield

    def pair_product(self, name, bank, ready):
        def fn(e, hi, lo, ss=range(2), ks=range(8)):
            for s in ss:
                out = bank.t[:, s * T:(s + 1) * T]
                for k in ks:
                    ws = slice((s * 8 + k) * 128, (s * 8 + k + 1) * 128)
                    xs = slice(k * T, (k + 1) * T)
                    e.matmul(out, hi[:, ws], self.thi[:, xs], start=(k == 0), stop=False)
                    e.matmul(out, hi[:, ws], self.tlo[:, xs], start=False, stop=False)
                    m = e.matmul(out, lo[:, ws], self.thi[:, xs], start=False, stop=(k == 7))
            return m
        if isinstance(ready, Turned):
            parts = [(lambda e, hi, lo, k=k: fn(e, hi, lo, [0], [k, k + 1]), ready[k // 2]) for k in range(0, 8, 2)]
            return self.chunk(name, parts + [(lambda e, hi, lo: fn(e, hi, lo, [1]), None)], bank.free)
        return self.chunk(name, fn, ready, bank.free)

    def gated(self, name, plan, ready, gate=None, aside={}):
        nf = max(f for k, f in plan if k == "gu") + 1
        act, used = {}, {}
        ys = self.bank[0:4]
        sil = [self.scr.cut(T) for _ in range(4)]
        val = [self.scr.cut(T) for _ in range(4)]
        last = None
        vfree, parts = {}, {}
        for kind, f in plan:
            if kind == "gu":
                bank = self.bank[4 + f % 4]
                tok = self.pair_product(name, bank, ready if f == 0 else None)
                s, o = sil[f % 4], val[f % 4]
                g_ps, u_ps = bank.t[:, :T], bank.t[:, T:]
                sl = slice((f % 4) * T, (f % 4 + 1) * T)
                hi, lo = self.ahi[:, sl], self.alo[:, sl]
                t = self.a(lambda e, s=s, x=g_ps: e.activation(s, x, ACT.Silu), tok, parts.get(f - 4), vfree.get(f - 4))
                if gate is not None:
                    gt = gate(f)
                    t = self.g(lambda e, s=s, gt=gt: e.tensor_tensor(s, s, gt, ALU.mult), t)
                t = self.v(lambda e, s=s, o=o, x=u_ps: e.tensor_tensor(o, s, x, ALU.mult), t, act.get(f - 4))
                bank.free = t
                vfree[f] = t
                down = used.get((f - 4) - (f - 4) % 2) if f >= 4 else None
                h = self.a(lambda e, o=o, hi=hi: e.activation(hi, o, ACT.Copy), t, down, parts.get(f - 4))
                p = self.v(lambda e, o=o, hi=hi, lo=lo: e.tensor_tensor(lo, o, hi.bitcast(F32), ALU.subtract), h, down)
                act[f], parts[f] = h, p
                if f in aside:
                    aside[f]()
            else:
                def fn(e, hi, lo, tts=range(2), f=f):
                    for tt in tts:
                        for j in range(2):
                            at = ((f + j) % 4) * T + tt * 128
                            xs = slice(at, at + 128)
                            for half in range(2):
                                ws = slice(j * D + half * 512, j * D + half * 512 + 512)
                                out = ys[tt * 2 + half].t[:, :]
                                e.matmul(out, self.ahi[:, xs], hi[:, ws], start=(f + j == 0), stop=False)
                                e.matmul(out, self.ahi[:, xs], lo[:, ws], start=False, stop=False)
                                m = e.matmul(out, self.alo[:, xs], hi[:, ws], start=False, stop=(f + j == nf - 1))
                    return m
                first = [b.free for b in ys] if f == 0 else []
                if f + 2 == nf:
                    fn = [(lambda e, hi, lo, fn=fn, tt=tt: fn(e, hi, lo, [tt]), None) for tt in range(2)]
                used[f] = self.chunk(name, fn, first, act[f], parts[f], act[f + 1], parts[f + 1])
        return self.pieces

    def held(self):
        return (self.at, dict(self.loaded), dict(self.rounded), dict(self.parted), dict(self.used),
                self.scr.at, [b.free for b in self.bank])

    def hold(self, kept):
        self.at, self.scr.at = kept[0], kept[5]
        self.loaded, self.rounded, self.parted, self.used = (dict(x) for x in kept[1:5])
        for b, t in zip(self.bank, kept[6]):
            b.free = t

    def joined(self):
        for i in range(self.at - NS - NR, self.at + NS + NR):
            if i in self.rounded:
                self.rounded[i], self.parted[i] = self.P.own("scalar"), self.P.own("vector")
            if i in self.used:
                self.used[i] = self.P.own("tensor")
        for b in self.bank:
            b.free = [self.P.own(e) for e in ("tensor", "vector", "scalar")]

    def turn(self, src, kts, ready, scale=None, free=None, hi=None, lo=None):
        hi = hi or self.thi
        lo = lo or self.tlo
        toks = Turned()
        for n, k0 in enumerate(range(0, kts, 2)):
            bank = self.bank[4 + n % 4]
            kk = min(2, kts - k0)

            def fn(e, k0=k0, kk=kk, bank=bank):
                for j in range(kk):
                    for tt in range(2):
                        m = e.transpose(bank.t[:, j * T + tt * 128:j * T + tt * 128 + 128],
                                        src(tt)[:, (k0 + j) * 128:(k0 + j + 1) * 128], self.ident)
                return m
            tok = self.pe(fn, ready, bank.free)
            if scale is None:
                h_, l_ = hi[:, k0 * T:(k0 + kk) * T], lo[:, k0 * T:(k0 + kk) * T]
                ps = bank.t[:, :kk * T]
                t = self.a(lambda e, h_=h_, ps=ps: e.activation(h_, ps, ACT.Copy), tok, free)
                t = self.v(lambda e, h_=h_, l_=l_, ps=ps: e.tensor_tensor(l_, ps, h_.bitcast(F32), ALU.subtract), t, free)
            else:
                t = tok
                for j in range(kk):
                    sl = slice((k0 + j) * T, (k0 + j + 1) * T)
                    h_, l_, ps = hi[:, sl], lo[:, sl], bank.t[:, j * T:(j + 1) * T]
                    sc = scale(k0 + j)
                    t = self.a(lambda e, h_=h_, ps=ps, sc=sc: e.activation(h_, ps, ACT.Copy, scale=sc), t, free)
                for j in range(kk):
                    sl = slice((k0 + j) * T, (k0 + j + 1) * T)
                    h_, l_, ps = hi[:, sl], lo[:, sl], bank.t[:, j * T:(j + 1) * T]
                    sc = scale(k0 + j)
                    t = self.v(lambda e, h_=h_, l_=l_, ps=ps, sc=sc: e.scalar_tensor_tensor(
                        l_, ps, sc, h_.bitcast(F32), ALU.mult, ALU.subtract), t, free)
            bank.free = t
            toks.append(t)
        return toks

    def power(self, out, x, n, after):
        return self.g(lambda e: e.tensor_tensor(out, x, self.c("half")[:, :1].broadcast_to([128, n]), ALU.pow), after)

    def x(self, tt):
        return self.X[:, tt * D:(tt + 1) * D]

    def layer_norm(self, src, ready, ln):
        s, st = [src(tt) for tt in range(2)], [self.st[:, tt * 32:(tt + 1) * 32] for tt in range(2)]
        v, t = self.v, {}
        for tt in range(2):
            for c in range(2):
                v(lambda e, tt=tt, c=c: e.bn_stats(st[tt][:, c * 6:(c + 1) * 6], s[tt][:, c * 512:(c + 1) * 512]), ready)
            v(lambda e, tt=tt: e.bn_aggr(st[tt][:, 12:14], st[tt][:, 0:12]))
            t[tt] = v(lambda e, tt=tt: e.tensor_scalar(st[tt][:, 14:15], st[tt][:, 13:14], 1e-5, None, ALU.add))
            t[tt] = self.power(st[tt][:, 15:16], st[tt][:, 14:15], 1, t[tt])
        v(lambda e: e.tensor_scalar(s[0], s[0], st[0][:, 12:13], st[0][:, 15:16], ALU.subtract, ALU.mult), t[0])
        t0 = v(lambda e: e.tensor_tensor(s[0], s[0], self.gb_[:, :D], ALU.mult), ln)
        t0 = self.g(lambda e: e.tensor_tensor(self.x(0), s[0], self.gb_[:, D:], ALU.add), t0)
        v(lambda e: e.tensor_scalar(s[1], s[1], st[1][:, 12:13], st[1][:, 15:16], ALU.subtract, ALU.mult), t[1])
        v(lambda e: e.tensor_tensor(s[1], s[1], self.gb_[:, :D], ALU.mult))
        t1 = v(lambda e: e.tensor_tensor(self.x(1), s[1], self.gb_[:, D:], ALU.add))
        return [t0, t1]

    def rms_rows(self, src, groups, width, eps, ready, col=64):
        junk = self.junk[:, :width]
        ss, r = self.st[:, col:col + groups], self.st[:, col + groups:col + 2 * groups]
        for i in range(groups):
            t = self.a(lambda e, i=i: e.activation(junk, src[:, i * width:(i + 1) * width], ACT.Square,
                                                   accum_out=ss[:, i:i + 1]), ready)
        t = self.v(lambda e: e.tensor_scalar(ss, ss, 1.0 / width, eps, ALU.mult, ALU.add), t)
        return r, self.power(r, ss, groups, t)

    def rms_scaled(self, src, out, ready):
        done = []
        for tt in range(2):
            r, t = self.rms_rows(src(tt), 1, D, 1e-6, ready and ready[tt], col=64 + 8 * tt)
            done.append(self.v(lambda e, tt=tt, r=r: e.tensor_scalar(out(tt), src(tt), r, None, ALU.mult), t))
        return done

    def rms_turn(self, gain):
        xn = [self.scr.cut(D) for _ in range(2)]
        self.junk = self.scr.cut(D)
        done = self.rms_scaled(self.x, lambda tt: xn[tt], self.xdone)
        return self.turn(lambda tt: xn[tt], 8, done, scale=lambda k: self.vec(gain, k))

    def rows_load(self, stage, name, after):
        n = row_len(stage)
        src = self.d[name].partition_broadcast(128)
        return self.P.dma(self.d_row, lambda e: e.dma_start(self.rows[:, :n], src), after)

    def ln_load(self, name, after):
        src = self.d[name].partition_broadcast(128)
        return self.P.dma(self.d_ln, lambda e: e.dma_start(self.gb_[:, :], src), after)

    def begin(self):
        self.scr.at = 0
        return self.P.meet()

    def follow(self):
        self.scr.at = 0
        return [self.P.own(e) for e in ("tensor", "vector", "scalar", "gpsimd")]

    def heads_turned(self, src, n, width, dst, ready, banks, p0=0):
        todo = [(i, tt) for i in range(n) for tt in range(2)]
        toks = []
        for m, at in enumerate(range(0, len(todo), 4)):
            part = todo[at:at + 4]
            bank = banks[m % len(banks)]

            def fn(e, part=part, bank=bank):
                for j, (i, tt) in enumerate(part):
                    ins = e.transpose(bank.t[0:width, j * 128:(j + 1) * 128], src(tt, i), self.ident)
                return ins
            tok = self.pe(fn, ready, bank.free)
            i0 = part[0][0] * T
            out, ps = dst[p0:p0 + width, i0:i0 + len(part) * 128], bank.t[0:width, :len(part) * 128]
            if m % 2 == 0:
                bank.free = self.a(lambda e, out=out, ps=ps: e.activation(out, ps, ACT.Copy), tok)
            else:
                bank.free = self.v(lambda e, out=out, ps=ps: e.tensor_copy(out, ps), tok)
            toks.append(bank.free)
        return toks

    def attention(self, units, ready):
        sc = [self.att[:, i * 1024:(i + 1) * 1024] for i in range(2)]
        pt = [self.att[:, (2 + i) * 1024:(3 + i) * 1024] for i in range(2)]
        turned, summed = {}, {}

        def one(u):
            unit = units[u]
            H, nk = len(unit["heads"]), unit["nk"]
            per = 512 // nk
            banks = self.bank[0:2] if u % 2 == 0 else self.bank[2:4]
            S, PT = sc[u % 2], pt[u % 2]
            scale = unit["scale"]

            def fn(e):
                for j in range(H):
                    bank = banks[j // per].t
                    if "mask" in unit and j % per == 0:
                        hb = min(per, H - j)
                        e.matmul(bank[:, :hb * nk], self.identr, bc(unit["mask"], 1, hb), start=True, stop=False)
                    last = j % per == per - 1 or j == H - 1
                    m = unit["scores"](e, bank[:, (j % per) * nk:(j % per + 1) * nk], unit["heads"][j], last)
                return m
            tok = self.pe(fn, ready, banks[0].free, banks[1].free)
            yield
            c0 = 96 + 80 * (u % 2)
            m, s, x, b = (self.st[:, c0 + 16 * i:c0 + 16 * i + H] for i in range(4))
            for i in range((H + per - 1) // per):
                hb = min(per, H - i * per)
                t = self.v(lambda e, i=i, hb=hb: e.tensor_reduce(
                    m[:, i * per:i * per + hb], r3(banks[i].t[:, :hb * nk], nk), AXX, ALU.max), tok, summed.get(u - 2))
            if "shift" in unit:
                self.v(lambda e: e.scalar_tensor_tensor(m, m, scale, unit["shift"], ALU.mult, ALU.add))
                t = self.v(lambda e: e.tensor_tensor(b, unit["shift"], m, ALU.subtract))
            elif "sink" in unit:
                self.v(lambda e: e.scalar_tensor_tensor(m, m, scale, unit["sink"], ALU.mult, ALU.max))
                self.v(lambda e: e.tensor_tensor(x, unit["sink"], m, ALU.subtract))
                t = self.v(lambda e: e.tensor_scalar(b, m, -1.0, None, ALU.mult))
            else:
                t = self.v(lambda e: e.tensor_scalar(b, m, -scale, None, ALU.mult))
            yield
            for j in range(H):
                bank = banks[j // per]
                ps = bank.t[:, (j % per) * nk:(j % per + 1) * nk]
                t2 = self.P.op("scalar", lambda e, j=j, ps=ps: e.activation(
                    S[:, j * nk:(j + 1) * nk], ps, ACT.Exp, bias=b[:, j:j + 1], scale=scale, accum_out=s[:, j:j + 1]),
                    t, turned.get(u - 2))
                bank.free = t2
            if "sink" in unit:
                t2 = self.a(lambda e: e.activation(x, x, ACT.Exp), t)
            yield
            if "sink" in unit:
                self.v(lambda e: e.tensor_tensor(s, s, x, ALU.add), t2)
            self.v(lambda e: e.reciprocal(s, s), t2)
            if "lam" in unit:
                self.v(lambda e: e.tensor_scalar(s[:, 1:H:2], s[:, 1:H:2], unit["lam"], None, ALU.mult))
            nt = nk // 128
            nb = H * nt // 4
            toks = []
            for n in range(nb):
                bank = self.bank[4 + n]

                def fn(e, n=n, bank=bank):
                    for q in range(4):
                        at = (4 * n + q) * 128
                        ins = e.transpose(bank.t[:, q * 128:(q + 1) * 128], S[:, at:at + 128], self.ident)
                    return ins
                toks.append(self.pe(fn, t2, bank.free))
            turned[u] = toks[-1]
            pts = []
            for n in range(nb):
                bank = self.bank[4 + n]
                out, ps = PT[:, n * 512:(n + 1) * 512], bank.t[:, :]
                if n == 0:
                    bank.free = self.a(lambda e, out=out, ps=ps: e.activation(out, ps, ACT.Copy), toks[n], summed.get(u - 2))
                else:
                    bank.free = self.v(lambda e, out=out, ps=ps: e.tensor_copy(out, ps), toks[n], summed.get(u - 2))
                pts.append(bank.free)
            yield
            dv = unit["dv"]
            hp = 512 // dv
            vtok = []
            for i in range((H + hp - 1) // hp):
                hb = min(hp, H - i * hp)
                bank = self.bank[6 + (u + i) % 2]

                def fn(e, i=i, hb=hb, bank=bank):
                    for j in range(i * hp, i * hp + hb):
                        for k in range(nt):
                            ins = e.matmul(bank.t[:, (j - i * hp) * dv:(j - i * hp + 1) * dv],
                                           PT[:, (j * nt + k) * 128:(j * nt + k + 1) * 128],
                                           unit["v"](j, k), start=(k == 0), stop=(k == nt - 1))
                    return ins
                tok = self.pe(fn, pts, bank.free)
                vtok.append(tok)
                ps = r3(bank.t[:, :hb * dv], dv)
                rr = bc(s[:, i * hp:i * hp + hb], 2, dv)
                if "lam" in unit:
                    o8 = r3(self.st2[:, (u % 2) * 512:(u % 2) * 512 + hb * dv], dv)
                    out = r3(unit["out"], dv)
                    bank.free = self.v(lambda e, ps=ps, rr=rr, o8=o8: e.tensor_tensor(o8, ps, rr, ALU.mult), tok)
                    self.v(lambda e, o8=o8, out=out, hb=hb: e.tensor_tensor(
                        out, o8[:, 0:hb:2, :], o8[:, 1:hb:2, :], ALU.subtract))
                else:
                    out = r3(unit["out"], dv)[:, i * hp:i * hp + hb, :]
                    bank.free = self.v(lambda e, out=out, ps=ps, rr=rr: e.tensor_tensor(out, ps, rr, ALU.mult), tok)
            summed[u] = vtok + [self.P.own("vector")]
            if "then" in unit:
                unit["then"](summed[u][-1])

        interleave([one(u) for u in range(len(units))], 2)
        return self.P.own("vector")

    def rope(self, x, H, half, cos, sin, after):
        n = H * 2 * half
        t1, t2 = self.rt[0][:, :n], self.rt[1][:, :n]
        v4 = lambda a: a.rearrange("p (h s f) -> p h s f", s=2, f=half)
        c = bc(bc(cos, 1, 2), 1, H)
        s = bc(bc(sin, 1, 2), 1, H)
        x4 = x.rearrange("p h (s f) -> p h s f", s=2)
        self.v(lambda e: e.tensor_tensor(v4(t1), x4, c, ALU.mult), after)
        self.v(lambda e: e.tensor_tensor(v4(t2), x4, s, ALU.mult))
        self.v(lambda e: e.tensor_tensor(x4[:, :, 0, :], v4(t1)[:, :, 0, :], v4(t2)[:, :, 1, :], ALU.subtract))
        return self.v(lambda e: e.tensor_tensor(x4[:, :, 1, :], v4(t1)[:, :, 1, :], v4(t2)[:, :, 0, :], ALU.add))

    def rotations(self):
        P = self.P
        n = 40
        pos = self.keep(2, I32)
        ang, k, r, b = (self.att[:, 2048 + 64 * i:2048 + 64 * i + n] for i in range(4))
        self.cos, self.sin = self.keep(n), self.keep(n)
        posf = self.keep(2)
        t = P.dma(self.d_late, lambda e: e.dma_start(pos, self.d["pos"]))
        t = self.v(lambda e: e.tensor_copy(posf, pos), t)
        for tt in range(2):
            t = self.v(lambda e, tt=tt: e.tensor_scalar(ang[:, tt * 20:(tt + 1) * 20], self.c("invf"), posf[:, tt:tt + 1],
                                                        None, ALU.mult), t, self.const_ready)
        self.v(lambda e: e.tensor_scalar(k, ang, 1.0 / (2 * math.pi), None, ALU.mult))
        self.v(lambda e: e.tensor_scalar(k, k, MAGIC, None, ALU.add))
        self.v(lambda e: e.tensor_scalar(k, k, -MAGIC, None, ALU.add))
        c1 = 6.28125
        c2 = float(np.float32(2 * math.pi - c1))
        c3 = 2 * math.pi - c1 - c2
        for c in (c1, c2, c3):
            self.v(lambda e, c=c: e.scalar_tensor_tensor(ang, k, -c, ang, ALU.mult, ALU.add))
        pi = float(np.nextafter(np.float32(math.pi), np.float32(0)))
        t = self.v(lambda e: e.tensor_scalar(r, ang, pi, -pi, ALU.min, ALU.max))
        self.a(lambda e: e.activation(self.sin, r, ACT.Sin), t)
        self.v(lambda e: e.tensor_scalar(ang, ang, math.pi / 2, None, ALU.add))
        self.v(lambda e: e.tensor_scalar(b, ang, math.pi, -2 * math.pi, ALU.is_gt, ALU.mult))
        self.v(lambda e: e.tensor_tensor(ang, ang, b, ALU.add))
        t = self.v(lambda e: e.tensor_scalar(ang, ang, pi, -pi, ALU.min, ALU.max))
        return self.a(lambda e: e.activation(self.cos, ang, ACT.Sin), t)

    def keep(self, n, dt=F32):
        a = self.kept_at
        self.kept_at += n
        ap = self.small[:, a:a + n]
        return ap.bitcast(dt) if dt != F32 else ap

    def begin_program(self):
        P = self.P
        self.kept_at = 0
        xs = [self.scr.cut(D) for _ in range(2)]
        t = None
        for tt in range(2):
            t = P.dma(self.d_x, lambda e, tt=tt: e.dma_start(xs[tt], self.d["x"][tt * 128:(tt + 1) * 128, :]))
        P.dma(self.d_const, lambda e: e.dma_start(self.const[:, :], self.d["const"]))
        ln = self.ln_load("row_lnin", None)
        raw = self.scr.cut(640)
        P.dma(self.d_const, lambda e: e.dma_start(raw, self.d["masks"]))
        self.const_ready = P.dma(self.d_const, lambda e: e.dma_start(self.vecs[:, :], self.d["vecs"]))
        self.start()
        self.routed = P.dma(self.d_rw, lambda e: e.dma_start(self.rw[:, :], self.d["router"]))
        self.layer_norm(lambda tt: xs[tt], [t, self.const_ready], ln)
        self.a(lambda e: e.activation(self.maskr[:, :], raw, ACT.Copy), self.const_ready)

    def mixer(self, l):
        P, cut = self.P, self.scr.cut
        now = self.begin()
        rows = self.rows_load("mla", f"row_mla{l}", now)
        R = lambda n: self.row("mla", n)
        proj = [cut(IN_COLS) for _ in range(2)]
        B = self.bank
        lam_init = 0.8 - 0.6 * math.exp(-0.3 * l)
        ready = self.turn(self.x, 8, None)
        col = lambda tt, i, j=None: proj[tt][:, OFF[i]:OFF[(j or i) + 1] if (j or i) + 1 < 10 else IN_COLS]
        q_at = self.scr.at
        q = [cut(768) for _ in range(2)]
        kf = [cut(768) for _ in range(2)]
        vv = [cut(512) for _ in range(2)]
        self.att = cut(4096)
        self.st2 = self.gb_[:, 0:1024]
        self.junk = self.att[:, 0:384]
        self.rt = [self.att[:, 1024:1536], self.att[:, 1536:2048]]
        qT, kT = cut(8 * T), cut(8 * T)
        fqT, fkT = cut(4 * T), cut(4 * T)
        heads = self.heads_turned
        lam = self.keep(8) if l == 0 else self.lam
        self.lam = lam
        prod = self.gb_[:, 1024:1088]
        a, b = row_at("mla", "lq1")[0], row_at("mla", "lk1")[0]
        self.v(lambda e: e.tensor_tensor(prod, self.rows[:, a:a + 64], self.rows[:, b:b + 64], ALU.mult), rows)
        t = self.v(lambda e: e.tensor_reduce(lam[:, 0:2], r3(prod, 32), AXX, ALU.add))
        t = self.a(lambda e: e.activation(lam[:, 0:2], lam[:, 0:2], ACT.Exp), t)
        t = self.v(lambda e: e.tensor_tensor(lam[:, 2:3], lam[:, 0:1], lam[:, 1:2], ALU.subtract), t)
        self.v(lambda e: e.tensor_scalar(lam[:, 2:3], lam[:, 2:3], lam_init, None, ALU.add))
        if l == 0:
            self.rotated = self.rotations()
        turned_cs = self.rotated
        rot = {}
        for tt in range(2):
            rot[tt] = (self.cos[:, tt * 20:tt * 20 + 16], self.sin[:, tt * 20:tt * 20 + 16],
                       self.cos[:, tt * 20 + 16:tt * 20 + 20], self.sin[:, tt * 20 + 16:tt * 20 + 20])

        def to_proj(tt, n0, w, ps, tok):
            out = proj[tt][:, n0:n0 + w]
            if tt == 0:
                return self.a(lambda e: e.activation(out, ps, ACT.Copy), tok)
            return self.v(lambda e: e.tensor_copy(out, ps), tok)
        got, lat = {}, []

        def latents():
            done = [P.own("scalar"), P.own("vector")]
            for tt in range(2):
                for i, w, c in ((0, 384, 64), (1, 256, 72)):
                    r, t = self.rms_rows(col(tt, i), 1, w, 1e-6, [done, rows], col=c + 16 * tt)
                    lat.append((col(tt, i), r, ("qg", "kvg")[i], t))

        def latents_turned():
            for x, r, g, t in lat:
                self.v(lambda e, x=x, r=r, g=g: e.scalar_tensor_tensor(x, x, r, R(g), ALU.mult, ALU.mult), t)
            got["lat"] = t = P.own("vector")
            got["q"] = self.turn(lambda tt: proj[tt][:, 0:384], 3, t, hi=self.ahi, lo=self.alo)

        def diff_roped():
            done = [P.own("scalar"), P.own("vector")]
            for tt in range(2):
                cm, sm, cd, sd = rot[tt]
                self.rope(col(tt, 2).unsqueeze(1), 1, 16, cm, sm, [turned_cs, done])
                self.v(lambda e, tt=tt: e.tensor_copy(r3(kf[tt], 96)[:, :, 64:96], bc(col(tt, 2), 1, 8)))
                self.rope(r3(col(tt, 3), 32)[:, :, 0:8], 8, 4, cd, sd, None)
                self.rope(r3(col(tt, 4), 32)[:, :, 0:8], 8, 4, cd, sd, None)
            got["roped"] = P.own("vector")

        def diff_turned():
            heads(lambda tt, i: col(tt, 3)[:, i * 32:(i + 1) * 32], 8, 32, qT, got["roped"], B[4:8], p0=96)
            heads(lambda tt, i: col(tt, 4)[:, i * 32:(i + 1) * 32], 8, 32, kT, got["roped"], B[4:8], p0=96)

        aside = {3: latents, 4: latents_turned, 5: diff_roped, 7: diff_turned}
        for i, _ in enumerate(self.moving_steps(f"w_in{l}", D, IN_COLS, [(B[0], B[1]), (B[2], B[3])], to_proj, ready)):
            if i in aside:
                aside[i]()
        used = P.own("tensor")
        done = [P.own("scalar"), P.own("vector")]
        kv_ready = self.turn(lambda tt: proj[tt][:, 384:640], 2, got["lat"], free=used)

        def to_q(tt, n0, w, ps, tok):
            out = q[tt][:, n0:n0 + w]
            return self.a(lambda e: e.activation(out, ps, ACT.Copy), tok)
        self.moving(f"uq{l}", 384, 768, [(B[0], B[1]), (B[2], B[3])], to_q, got["q"], src=(self.ahi, self.alo))
        qdone = P.own("scalar")
        heads(lambda tt, i: col(tt, 6)[:, i * 64:(i + 1) * 64], 4, 64, fqT, done, B[4:8])
        heads(lambda tt, i: col(tt, 7)[:, i * 64:(i + 1) * 64], 4, 64, fkT, done, B[4:8])
        for tt in range(2):
            cm, sm, cd, sd = rot[tt]
            qroped = self.rope(r3(q[tt], 96)[:, :, 64:96], 8, 16, cm, sm, qdone)
        lf = [self.st[:, 0:4], self.st[:, 4:8]]
        cum = [self.st[:, 8:12], self.st[:, 12:16]]
        tmp = self.st[:, 16:24]
        lb = [proj[tt][:, 0:512] for tt in range(2)]
        for tt in range(2):
            self.v(lambda e, tt=tt: e.tensor_tensor(lf[tt], col(tt, 9), R("fb"), ALU.add))
        both = self.st[:, 0:8]
        t = self.v(lambda e: e.tensor_scalar(tmp, both, 0.0, None, ALU.min))
        t = self.a(lambda e: e.activation(both, both, ACT.Abs), t)
        t = self.a(lambda e: e.activation(both, both, ACT.Exp, scale=-1.0))
        t = self.a(lambda e: e.activation(both, both, ACT.Ln, bias=1.0))
        t = self.v(lambda e: e.tensor_tensor(both, tmp, both, ALU.subtract), t)
        for tt in range(2):
            t = self.v(lambda e, tt=tt: e.tensor_scalar(r3(lb[tt], 128), bc(lf[tt], 2, 128), -8.0, None, ALU.mult))
        bank = B[6]

        def cums(e):
            e.matmul(bank.t[:, 0:4], self.tri, lf[0], start=True, stop=True)
            e.matmul(bank.t[:, 4:8], self.ones, lf[0], start=True, stop=False)
            return e.matmul(bank.t[:, 4:8], self.tri, lf[1], start=False, stop=True)
        gates = t

        def to_kv(tt, n0, w, ps, tok):
            h0 = n0 // 128
            p4 = r3(ps, 128)
            out_k = r3(kf[tt], 96)[:, h0:h0 + 4, 0:64]
            out_v = r3(vv[tt], 64)[:, h0:h0 + 4, :]
            t = self.a(lambda e: e.activation(out_k, p4[:, :, 0:64], ACT.Copy), tok)
            return self.v(lambda e: e.tensor_copy(out_v, p4[:, :, 64:128]), t)
        self.moving(f"ukv{l}", 256, 1024, [(B[0], B[1]), (B[2], B[3])], to_kv, kv_ready)
        t = self.pe(cums, gates, bank.free)
        t = self.v(lambda e: e.tensor_copy(self.st[:, 8:16], bank.t[:, 0:8]), t)
        bank.free = t
        kvdone = [P.own("scalar"), P.own("vector")]
        heads(lambda tt, i: q[tt][:, i * 96:(i + 1) * 96], 8, 96, qT, qroped, B[0:4])
        heads(lambda tt, i: kf[tt][:, i * 96:(i + 1) * 96], 8, 96, kT, kvdone, B[0:4])
        ready = [P.own("scalar"), P.own("vector"), P.own("tensor")]
        o = [self.scr.t[:, q_at:q_at + D], self.scr.t[:, q_at + D:q_at + 2 * D]]

        def unit(tt, heads, off, m, kT_, qT_, p0, p1, **kw):
            nk = 128 * (tt + 1)
            mask = self.maskr[:, m + 256 - nk:m + 256]
            two = 2 if "lam" in kw else 1
            h0, ng = heads[0] // two, len(heads) // two

            def scores(e, out, h, last):
                fox = kw.get("fox")
                m = e.matmul(out, qT_[p0:p1, h * T + tt * 128:h * T + tt * 128 + 128], kT_[p0:p1, h * T:h * T + nk],
                             start=False, stop=last and not fox)
                if fox:
                    m = e.matmul(out, lb[0][:, h * 128:(h + 1) * 128], self.zto[:, 128:128 + nk], start=False,
                                 stop=last and tt == 0)
                    if tt:
                        m = e.matmul(out, lb[1][:, h * 128:(h + 1) * 128], self.zto[:, 0:256], start=False, stop=last)
                return m
            return dict(tt=tt, heads=heads, nk=nk, dv=64, scores=scores, mask=mask,
                        out=o[tt][:, off + h0 * 64:off + (h0 + ng) * 64], **kw)

        def vals(src, h0, two=1):
            return lambda j, k: src(k)[:, (h0 + j // two) * 64:(h0 + j // two + 1) * 64]
        def diff_normed(after):
            self.junk = self.gb_[:, 1088:1152]
            for tt in range(2):
                def one(tt=tt):
                    x = o[tt][:, 512:768]
                    r, t = self.rms_rows(x, 4, 64, 1e-6, after, col=64 + 8 * tt)
                    t = self.v(lambda e: e.tensor_tensor(r3(x, 64), r3(x, 64), bc(r, 2, 64), ALU.mult), t)
                    return self.v(lambda e: e.scalar_tensor_tensor(r3(x, 64), r3(x, 64), 1.0 - lam_init,
                                                                   bc(R("subln"), 1, 4), ALU.mult, ALU.mult))
                one()
        units = []
        for tt, hs in ((0, range(8)), (1, range(4)), (1, range(4, 8))):
            units.append(unit(tt, list(hs), 512, 128, kT, qT, 96, 128, scale=32 ** -0.5, lam=lam[:, 2:3],
                              v=vals(lambda k: col(k, 5), hs[0] // 2, 2)))
        units[-1]["then"] = diff_normed
        for tt in (0, 1):
            units.append(unit(tt, list(range(4)), 768, 384, fkT, fqT, 0, 64, scale=0.125, shift=cum[tt], fox=True,
                              v=vals(lambda k: col(k, 8), 0)))
        for tt, hs in ((0, range(8)), (1, range(4)), (1, range(4, 8))):
            units.append(unit(tt, list(hs), 0, 128, kT, qT, 0, 96, scale=96 ** -0.5, v=vals(lambda k: vv[k], hs[0])))
        done = self.attention(units, ready)
        ln = self.ln_load(f"row_ln1{l}", [P.own("vector"), P.own("scalar")])
        self.P.meet()
        ready = self.turn(lambda tt: o[tt], 8, None)
        y = [kT[:, 0:D], kT[:, D:2 * D]]

        def to_y(tt, n0, w, ps, tok):
            return self.v(lambda e: e.scalar_tensor_tensor(y[tt][:, n0:n0 + w], self.x(tt)[:, n0:n0 + w], ALPHA, ps,
                                                           ALU.mult, ALU.add), tok)
        self.moving(f"w_out{l}", D, D, [(B[0], B[1]), (B[2], B[3])], to_y, ready)
        self.layer_norm(lambda tt: y[tt], P.own("vector"), ln)

    def moe(self, l):
        P, cut = self.P, self.scr.cut
        now = self.begin()
        rows = self.rows_load("moe", "row_moe", now)
        ln = self.ln_load(f"row_ln2{l}", now)
        B = self.bank
        rw = self.rw[:, :]
        es = cut(16 * 128)
        late = P.dma(self.d_late, lambda e: e.dma_start(es[0:16, :], self.d["esel"]), now)
        xT = cut(8 * T)
        if l == DEPTH - 1:
            mm = self.memory_load(now)
        toks = []
        for n in range(4):
            bank = B[4 + n]

            def fn(e, n=n, bank=bank):
                for j in range(2):
                    for tt in range(2):
                        m = e.transpose(bank.t[:, j * T + tt * 128:j * T + tt * 128 + 128],
                                        self.x(tt)[:, (2 * n + j) * 128:(2 * n + j + 1) * 128], self.ident)
                return m
            t = self.pe(fn, bank.free)
            sl = slice(n * 512, (n + 1) * 512)
            if n % 2:
                t = self.v(lambda e, sl=sl, bank=bank: e.tensor_copy(xT[:, sl], bank.t[:, :]), t)
            else:
                t = self.a(lambda e, sl=sl, bank=bank: e.activation(xT[:, sl], bank.t[:, :], ACT.Copy), t)
            bank.free = t
            toks.append(t)
        bank = B[0]

        def route(e):
            for tt in range(2):
                for k in range(8):
                    m = e.matmul(bank.t[:, tt * 16:tt * 16 + 16], xT[:, k * T + tt * 128:k * T + tt * 128 + 128],
                                 rw[:, k * 16:(k + 1) * 16], start=(k == 0), stop=(k == 7))
            return m
        t = self.pe(route, toks, self.routed, bank.free)
        sc, bi, t1, t2, t3 = (cut(32) for _ in range(5))
        g1, g2, g3, g4 = (cut(16) for _ in range(4))
        oh = cut(32)
        t = self.a(lambda e: e.activation(sc, bank.t[:, 0:32], ACT.Sigmoid), t)
        bank.free = t
        V = self.v
        TT = lambda o_, a_, b_, op: V(lambda e: e.tensor_tensor(o_, a_, b_, op))
        V(lambda e: e.tensor_tensor(r3(bi, 16), r3(sc, 16), bc(self.row("moe", "rb"), 1, 2), ALU.add), t, rows)
        b4 = r3(bi, 2)
        TT(g1, b4[:, :, 0], b4[:, :, 1], ALU.max)
        TT(g2, b4[:, :, 0], b4[:, :, 1], ALU.min)
        h1, h2 = r3(g1, 2), r3(g2, 2)
        top, a1, a2 = g3[:, 0:8], g3[:, 8:16], g4[:, 0:8]
        TT(top, h1[:, :, 0], h1[:, :, 1], ALU.max)
        TT(a1, h1[:, :, 0], h1[:, :, 1], ALU.min)
        TT(a2, h2[:, :, 0], h2[:, :, 1], ALU.max)
        TT(a1, a1, a2, ALU.max)
        TT(top, top, a1, ALU.add)
        mx = g4[:, 8:10]

        def first_max(out, x, c, n):
            V(lambda e: e.tensor_reduce(mx, r3(x, n), AXX, ALU.max))
            V(lambda e: e.tensor_tensor(r3(out, n), r3(x, n), bc(mx, 2, n), ALU.is_equal))
            V(lambda e: e.tensor_tensor(r3(out, n), r3(out, n), bc(c, 1, 2), ALU.mult))
            V(lambda e: e.tensor_reduce(mx, r3(out, n), AXX, ALU.max))
            V(lambda e: e.tensor_tensor(r3(out, n), r3(out, n), bc(mx, 2, n), ALU.is_equal))
        grp = g1[:, 0:8]
        first_max(grp, top, self.c("c4"), 4)
        grouped = P.own("vector")
        t38 = g2[:, 0:8]
        V(lambda e: e.tensor_scalar(t38, grp, -NEG, NEG, ALU.mult, ALU.add))
        V(lambda e: e.tensor_tensor(r3(t1, 4), r3(bi, 4), bc(grp, 2, 4), ALU.mult))
        V(lambda e: e.tensor_tensor(r3(t1, 4), r3(t1, 4), bc(t38, 2, 4), ALU.add))
        first_max(t2, t1, self.c("c16"), 16)
        V(lambda e: e.scalar_tensor_tensor(t1, t2, 3 * NEG, t1, ALU.mult, ALU.add))
        first_max(t3, t1, self.c("c16"), 16)
        TT(t2, t2, t3, ALU.add)
        TT(t2, t2, sc, ALU.mult)
        V(lambda e: e.tensor_reduce(mx, r3(t2, 16), AXX, ALU.add))
        V(lambda e: e.reciprocal(mx, mx))
        t = V(lambda e: e.tensor_tensor(r3(oh, 16), r3(t2, 16), bc(mx, 2, 16), ALU.mult))
        gates_ready = t
        place, flag = self.st[:, 0:2], self.flag
        cnt = g3[:, 0:4]
        bk = B[1]

        def places(e):
            e.matmul(bk.t[:, 0:4], self.tri, grp[:, 0:4], start=True, stop=True)
            e.matmul(bk.t[:, 4:8], self.ones, grp[:, 0:4], start=True, stop=False)
            e.matmul(bk.t[:, 4:8], self.tri, grp[:, 4:8], start=False, stop=True)
            e.matmul(bk.t[:, 8:12], self.ones, grp[:, 0:4], start=True, stop=False)
            return e.matmul(bk.t[:, 8:12], self.ones, grp[:, 4:8], start=False, stop=True)
        t = self.pe(places, grouped, bk.free)
        V(lambda e: e.tensor_reduce(cnt[:, 0:1], bk.t[:, 8:12], AXX, ALU.max), t)
        V(lambda e: e.tensor_scalar(cnt[:, 0:1], cnt[:, 0:1], 128.0, None, ALU.is_le))
        known = V(lambda e: e.tensor_copy(flag, cnt[:, 0:1]))
        t = V(lambda e: e.tensor_tensor(g4[:, 0:8], bk.t[:, 0:8], grp, ALU.mult), t)
        bk.free = t
        V(lambda e: e.tensor_reduce(place, r3(g4[:, 0:8], 4), AXX, ALU.add))
        V(lambda e: e.tensor_scalar(place, place, -1.0, None, ALU.add))
        sel = cut(8 * 128)
        for g in range(4):
            for tt in range(2):
                i = tt * 4 + g
                placed = V(lambda e, i=i, tt=tt: e.tensor_scalar(
                    sel[:, i * 128:(i + 1) * 128], self.c("iota"), place[:, tt:tt + 1], grp[:, i:i + 1],
                    ALU.is_equal, ALU.mult))
        if l == DEPTH - 1:
            scaled = self.rms_scaled(lambda tt: mm[tt], lambda tt: mm[tt], [self.mem_loaded] * 2)
        y = [xT[:, 0:D], xT[:, D:2 * D]]
        mark = self.scr.at

        def dense():
            ready = []
            for n in range(4):
                sl = slice(n * 512, (n + 1) * 512)
                h = self.a(lambda e, sl=sl: e.activation(self.thi[:, sl], xT[:, sl], ACT.Copy), toks)
                ready.append(self.v(lambda e, sl=sl: e.tensor_tensor(self.tlo[:, sl], xT[:, sl],
                                                                     self.thi[:, sl].bitcast(F32), ALU.subtract), h))
            gt = cut(T)
            gb = cut(NE * T)

            def tg(e):
                for tt in range(2):
                    m = e.transpose(bank.t[0:16, tt * 128:(tt + 1) * 128], oh[:, tt * 16:(tt + 1) * 16], self.ident)
                return m
            t = self.pe(tg, gates_ready, bank.free)
            t = V(lambda e: e.tensor_copy(gt[0:16, :], bank.t[0:16, 0:T]), t)
            bank.free = t
            for n in range(8):
                bk = B[n % 4]

                def fn(e, n=n, bk=bk):
                    for j in range(2):
                        i = 2 * n + j
                        m = e.matmul(bk.t[:, j * T:(j + 1) * T], es[0:16, i * 128:(i + 1) * 128], gt[0:16, :],
                                     start=True, stop=True)
                    return m
                t2_ = self.pe(fn, t, late, bk.free)
                out = gb[:, n * 512:(n + 1) * 512]
                bk.free = V(lambda e, out=out, bk=bk: e.tensor_copy(out, bk.t[:, :]), t2_)
            lasts = self.gated(f"exp{l}", plan_experts(), ready + [P.own("vector")],
                              gate=lambda f: gb[:, (f // 4) * T:(f // 4 + 1) * T])
            for tt in range(2):
                for half in range(2):
                    bk = B[tt * 2 + half]
                    sl = slice(half * 512, half * 512 + 512)
                    bk.free = V(lambda e, tt=tt, sl=sl, bk=bk: e.scalar_tensor_tensor(
                        y[tt][:, sl], self.x(tt)[:, sl], ALPHA, bk.t[:, :], ALU.mult, ALU.add), lasts[tt])

        def compact():
            name = f"exp{l}"
            C = 128
            gc, yg = cut(NE), cut(D)
            back = cut(4 * T)
            sil = [cut(C) for _ in range(4)]
            val = [cut(C) for _ in range(4)]
            hi3 = self.thi[:, :].rearrange("p (k t) -> p k t", t=T)
            lo3 = self.tlo[:, :].rearrange("p (k t) -> p k t", t=T)
            fetched, products = {}, {}

            def fetch(g):
                hf = g % 2
                banks = B[2 * hf:2 * hf + 2]
                ready = []
                for b, bk in enumerate(banks):
                    def fn(e, b=b, bk=bk):
                        for k in range(4):
                            kk = 4 * b + k
                            for tt in range(2):
                                i = tt * 4 + g
                                m = e.matmul(bk.t[:, k * C:(k + 1) * C], self.x(tt)[:, kk * 128:(kk + 1) * 128],
                                             sel[:, i * 128:(i + 1) * 128], start=(tt == 0), stop=(tt == 1))
                        return m
                    t = self.pe(fn, placed, bk.free)
                    h_, l_ = (x[:, 4 * b:4 * b + 4, hf * C:(hf + 1) * C] for x in (hi3, lo3))
                    ps = r3(bk.t[:, :], C)
                    t = self.a(lambda e, h_=h_, ps=ps: e.activation(h_, ps, ACT.Copy), t, products.get(g - 2))
                    t = self.v(lambda e, h_=h_, l_=l_, ps=ps: e.tensor_tensor(l_, ps, h_.bitcast(F32), ALU.subtract), t)
                    bk.free = t
                    ready.append(t)
                fetched[g] = ready

            fetch(0)
            b4_ = B[4]

            def fn(e):
                for g in range(4):
                    for tt in range(2):
                        i = tt * 4 + g
                        m = e.matmul(b4_.t[:, g * 4:g * 4 + 4], sel[:, i * 128:(i + 1) * 128],
                                     oh[:, tt * 16 + g * 4:tt * 16 + g * 4 + 4], start=(tt == 0), stop=(tt == 1))
                return m
            t = self.pe(fn, placed, gates_ready, b4_.free)
            b4_.free = V(lambda e: e.tensor_copy(gc, b4_.t[:, 0:16]), t)
            fetch(1)
            for n in range(2):
                bk = B[4 + n]

                def fn(e, n=n, bk=bk):
                    for j in range(4):
                        g, tt = 2 * n + j // 2, j % 2
                        i = tt * 4 + g
                        m = e.transpose(bk.t[:, j * 128:(j + 1) * 128], sel[:, i * 128:(i + 1) * 128], self.ident)
                    return m
                t = self.pe(fn, placed, bk.free)
                bk.free = V(lambda e, n=n, bk=bk: e.tensor_copy(back[:, n * 512:(n + 1) * 512], bk.t[:, :]), t)
            backed = P.own("vector")
            sums = {}
            state = {"yg": None}

            def collect(g):
                hf = g % 2
                out = []
                for half in range(2):
                    bk = B[2 * hf + half]
                    out.append(self.a(lambda e, half=half, bk=bk: e.activation(
                        yg[:, half * 512:half * 512 + 512], bk.t[:, :], ACT.Copy), sums[g], state["yg"]))
                    bk.free = out[-1]
                sums[g] = out

            def send(g, tt):
                hf = g % 2
                for half in range(2):
                    bk = B[2 * hf + half]
                    sl = slice(half * 512, half * 512 + 512)
                    t = self.pe(lambda e, bk=bk, sl=sl: e.matmul(
                        bk.t[:, :], back[:, g * T + tt * 128:g * T + tt * 128 + 128], yg[:, sl], start=True, stop=True),
                        sums[g], backed, bk.free)
                    state["yg"] = t
                    if g == 0:
                        t = V(lambda e, bk=bk, sl=sl: e.scalar_tensor_tensor(
                            y[tt][:, sl], self.x(tt)[:, sl], ALPHA, bk.t[:, :], ALU.mult, ALU.add), t)
                    else:
                        t = V(lambda e, bk=bk, sl=sl: e.tensor_tensor(y[tt][:, sl], y[tt][:, sl], bk.t[:, :], ALU.add), t)
                    bk.free = t

            nf = FE // 128 * 4
            act, parts, used, vtok, ttok = {}, {}, {}, {}, {}

            def product(f):
                g = f // nf
                bk = B[4 + f % 4]

                def fn(e, hi, lo):
                    hk, lk = (x[:, :].rearrange("p (s k c) -> p k s c", s=2, k=8) for x in (hi, lo))
                    out = bk.t[:, 0:2 * C]
                    for k in range(8):
                        xs = slice(k * T + (g % 2) * C, k * T + (g % 2) * C + C)
                        e.matmul(out, self.thi[:, xs], hk[:, k], start=(k == 0), stop=False)
                        e.matmul(out, self.thi[:, xs], lk[:, k], start=False, stop=False)
                        m = e.matmul(out, self.tlo[:, xs], hk[:, k], start=False, stop=(k == 7))
                    return m

                def between(tok):
                    s_, o_ = sil[f % 4], val[f % 4]
                    t = self.a(lambda e: e.activation(s_, bk.t[:, 0:C], ACT.Silu), tok, vtok.get(f - 4))
                    vtok[f] = self.v(lambda e: e.scalar_tensor_tensor(
                        o_, s_, gc[:, f // 4:f // 4 + 1], bk.t[:, C:2 * C], ALU.mult, ALU.mult), t, ttok.get(f - 4))
                    if f:
                        turn_act(f - 1)
                products[g] = self.chunk(name, fn, fetched[g], bk.free, between=between)

            def turn_act(f):
                bk = B[4 + f % 4]
                ps = bk.t[:, 2 * C:3 * C]
                t = ttok[f] = self.pe(lambda e: e.transpose(ps, val[f % 4], self.ident), vtok[f])
                hi, lo = (x[:, (f % 4) * T:(f % 4) * T + C] for x in (self.ahi, self.alo))
                down_ = used.get((f - 4) - (f - 4) % 2)
                act[f] = self.a(lambda e: e.activation(hi, ps, ACT.Copy), t, down_, parts.get(f - 4))
                parts[f] = self.v(lambda e: e.tensor_tensor(lo, ps, hi.bitcast(F32), ALU.subtract), act[f], down_)
                bk.free = parts[f]

            def down(f):
                g = f // nf
                ys = B[2 * (g % 2):2 * (g % 2) + 2]

                def fn(e, hi, lo):
                    for j in range(2):
                        xs = slice(((f + j) % 4) * T, ((f + j) % 4) * T + C)
                        for half in range(2):
                            ws = slice(j * D + half * 512, j * D + half * 512 + 512)
                            out = ys[half].t[:, :]
                            e.matmul(out, self.ahi[:, xs], hi[:, ws], start=((f + j) % nf == 0), stop=False)
                            e.matmul(out, self.ahi[:, xs], lo[:, ws], start=False, stop=False)
                            m = e.matmul(out, self.alo[:, xs], hi[:, ws], start=False, stop=((f + j) % nf == nf - 1))
                    return m
                first = [b.free for b in ys] if f % nf == 0 else []
                used[f] = sums[g] = self.chunk(name, fn, first, act[f], parts[f], act[f + 1], parts[f + 1])

            for kind, f in plan_experts():
                if kind == "d":
                    if f == NE * nf // 4 - 2:
                        turn_act(f + 1)
                    down(f)
                    continue
                product(f)
                g, at = f // nf, f % nf
                if g and at == 4:
                    collect(g - 1)
                    send(g - 1, 0)
                if g and at == 6:
                    send(g - 1, 1)
                if g and at == 8 and g + 1 < 4:
                    fetch(g + 1)
            collect(3)
            send(3, 0)
            send(3, 1)

        P.branch(flag[0:1, 0:1], known, compact, dense, self.held, self.hold)
        self.joined()
        summed = P.own("vector")
        if l < DEPTH - 1:
            self.layer_norm(lambda tt: y[tt], summed, ln)
            return
        ready = self.turn(lambda tt: mm[tt], 8, scaled, scale=lambda k: self.vec("mem_norm", k))
        self.scr.at = mark
        xn = [cut(D) for _ in range(2)]
        done = self.layer_norm(lambda tt: y[tt], summed, ln)
        heads, done = self.memory(ready, [summed, scaled], lambda: self.rms_scaled(self.x, lambda tt: xn[tt], done))
        used = P.own("tensor")
        ready = self.turn(lambda tt: xn[tt], 8, done, scale=lambda k: self.vec("ffn1_norm0", k), free=used)
        self.ffn("ffn10", None, ready, heads)

    def ffn(self, name, gain, ready=None, aside={}):
        if ready is None:
            self.follow()
            ready = self.rms_turn(gain)
        lasts = self.gated(name, plan_gated(F // 128), ready, aside=aside)
        for tt in range(2):
            for half in range(2):
                bk = self.bank[tt * 2 + half]
                x = self.x(tt)[:, half * 512:half * 512 + 512]
                bk.free = self.v(lambda e, x=x, bk=bk: e.scalar_tensor_tensor(x, bk.t[:, :], 0.5, x, ALU.mult, ALU.add),
                                 lasts[tt])
                self.xdone[tt] = bk.free

    def add_moving(self, *args, **kw):
        interleave([self.add_steps(*args, **kw)], 1)

    def add_steps(self, name, ready, bias=None):
        B = self.bank

        def evac(tt, n0, w, ps, tok):
            x = self.x(tt)[:, n0:n0 + w]
            t = self.v(lambda e: e.tensor_tensor(x, x, ps, ALU.add), tok)
            if bias is not None:
                t = self.v(lambda e: e.tensor_tensor(x, x, bias[:, n0:n0 + w], ALU.add))
            self.xdone[tt] = t
            return t
        return self.moving_steps(name, D, D, [(B[0], B[1]), (B[2], B[3])], evac, ready)

    def memory_load(self, now):
        size = self.scr.size
        self.memk = self.scr.t[:, size - 2048:size]
        self.memv = [self.scr.t[:, size - 4096:size - 3072], self.scr.t[:, size - 3072:size - 2048]]
        self.scr.size -= 4096
        self.junk = self.memk[:, 0:D]
        mm = [self.scr.cut(D) for _ in range(2)]
        for tt in range(2):
            self.mem_loaded = self.P.dma(self.d_x, lambda e, tt=tt: e.dma_start(
                mm[tt], self.d["mem"][tt * 128:(tt + 1) * 128, :]), now)
        return mm

    def memory(self, ready, free, aside):
        P, cut = self.P, self.scr.cut
        rows = self.rows_load("mem", "row_mem", free)
        other = []
        mk = [cut(D) for _ in range(2)]
        B = self.bank

        def evac(tt, n0, w, ps, tok):
            if n0 == D and tt == 0:
                other.append(aside())
            if n0 < D:
                return self.a(lambda e: e.activation(mk[tt][:, n0:n0 + w], ps, ACT.Copy), tok)
            return self.v(lambda e: e.tensor_copy(self.memv[tt][:, n0 - D:n0 - D + w], ps), tok)
        self.moving("mem_wkv", D, 2 * D, [(B[0], B[1]), (B[2], B[3])], evac, ready)
        done = [P.own("scalar"), P.own("vector")]

        def norm():
            self.head_norm(mk, 4, 256, self.row("mem", "kn"), [done, rows])

        def turn():
            self.heads_turned(lambda tt, i: mk[tt][:, i * 128:(i + 1) * 128], 8, 128, self.memk, P.own("vector"), B[4:8])
        return {0: norm, 3: turn}, other[0]

    def head_norm(self, x, H, w, gain, ready, base=96):
        self.head_scaled(x, H, w, gain, self.head_rms(x, H, w, ready, base))

    def head_rms(self, x, H, w, ready, base):
        return [self.rms_rows(x[tt], H, w, 1e-6, ready, col=base + 32 * tt) for tt in range(2)]

    def head_scaled(self, x, H, w, gain, rms):
        for a, (r, t) in zip(x, rms):
            self.v(lambda e, a=a, r=r: e.tensor_tensor(r3(a, w), r3(a, w), bc(r, 2, w), ALU.mult), t)
            self.v(lambda e, a=a: e.tensor_tensor(r3(a, w), r3(a, w), bc(gain, 1, H), ALU.mult))
        return self.P.own("vector")

    def cross(self, l):
        P, cut = self.P, self.scr.cut
        now = self.follow()
        rows = self.rows_load("xat", f"row_xat{l}", now)
        ready = self.rms_turn(f"xattn_norm{l}")
        B = self.bank
        q = [cut(D) for _ in range(2)]

        def evac(tt, n0, w, ps, tok):
            return self.a(lambda e: e.activation(q[tt][:, n0:n0 + w], ps, ACT.Copy), tok)
        qT = cut(8 * T)
        rms, normed = {}, {}

        def half(n):
            return [x[:, n * 512:(n + 1) * 512] for x in q]

        def norm(n):
            rms[n] = self.head_rms(half(n), 2, 256, P.own("scalar"), 96 + 8 * n)

        def scaled(n):
            rms[n][0] = (rms[n][0][0], [rms[n][0][1], rows])
            normed[n] = self.head_scaled(half(n), 2, 256, self.row("xat", "qn"), rms[n])

        def turn(n):
            self.heads_turned(lambda tt, i: q[tt][:, (4 * n + i) * 128:(4 * n + i + 1) * 128], 4, 128,
                              qT[:, n * 4 * T:(n + 1) * 4 * T], normed[n], B[4:8])
        for i, _ in enumerate(self.moving_steps(f"xwq{l}", D, D, [(B[0], B[1]), (B[2], B[3])], evac, ready)):
            if i == 1:
                norm(0)
            if i == 2:
                scaled(0)
        norm(1)
        turn(0)
        scaled(1)
        turn(1)
        ready = [P.own("scalar"), P.own("vector")]

        def scores(tt):
            def f(e, out, h, last):
                for c in range(2):
                    i = 2 * h + c
                    m = e.matmul(out, qT[:, i * T + tt * 128:i * T + tt * 128 + 128], self.memk[:, i * T:(i + 1) * T],
                                 start=(c == 0), stop=(c == 1))
                return m
            return f
        o = [cut(D) for _ in range(2)]
        self.att = cut(4096)
        units = [dict(tt=tt, heads=[0, 1, 2, 3], nk=256, dv=256, scale=1 / 16.0,
                      scores=scores(tt), out=o[tt], v=lambda j, k: self.memv[k][:, j * 256:(j + 1) * 256])
                 for tt in range(2)]
        done = self.attention(units, ready)
        ready = self.turn(lambda tt: o[tt], 8, done)
        self.add_moving(f"xwo{l}", ready)

    def swa(self):
        P, cut = self.P, self.scr.cut
        now = self.follow()
        rows = self.rows_load("swa", "row_swa", now)
        ali = cut(16 * T)
        late = P.dma(self.d_late, lambda e: e.dma_start(ali, self.d["alibi"]), now)
        R = lambda n: self.row("swa", n)
        mark = self.scr.at
        ready = self.rms_turn("mix_norm1")
        self.P.meet()
        self.scr.at = mark
        self.junk = cut(64)
        B = self.bank
        qkv = [cut(1536) for _ in range(2)]

        def evac(tt, n0, w, ps, tok):
            return self.v(lambda e: e.tensor_tensor(qkv[tt][:, n0:n0 + w], ps, R("bqkv")[:, n0:n0 + w], ALU.add), tok, rows)
        qT, kT = cut(8 * T), cut(2 * T)
        rms, normed = {}, {}

        def strip(n):
            return [x[:, n * 512:n * 512 + (512 if n < 2 else 256)] for x in qkv], 8 if n < 2 else 4, 64

        def norm(n):
            rms[n] = self.head_rms(*strip(n), P.own("vector"), 96 + 16 * n if n < 2 else 160)

        def scaled(n):
            normed[n] = self.head_scaled(*strip(n), R("qn" if n < 2 else "kn"), rms[n])

        def turn(up):
            self.heads_turned(lambda tt, i: qkv[tt][:, (8 * up + i) * 64:(8 * up + i + 1) * 64], 8, 64, qT,
                              normed[up], B[4:8], p0=64 * up)
        for i, _ in enumerate(self.moving_steps("wqkv", D, 1536, [(B[0], B[1]), (B[2], B[3])], evac, ready)):
            if i in (1, 3):
                norm(i // 2)
            if i in (2, 4):
                scaled(i // 2 - 1)
            if i == 3:
                turn(0)
        norm(2)
        turn(1)
        scaled(2)
        t = normed[2]
        for up in range(2):
            self.heads_turned(lambda tt, i, up=up: qkv[tt][:, 1024 + (2 * up + i) * 64:1024 + (2 * up + i + 1) * 64],
                              2, 64, kT, t, B[4:8], p0=64 * up)
        ready = [P.own("scalar"), P.own("vector"), late]
        o = [self.gb_[:, 0:D], self.gb_[:, D:2 * D]]

        def scores(tt):
            def f(e, out, h, last):
                nk = 128 * (tt + 1)
                e.matmul(out, self.ident, ali3[:, h, 256 - nk:], start=True, stop=False)
                p0, i, k = h // 8 * 64, h % 8, h // 4 % 2
                return e.matmul(out, qT[p0:p0 + 64, i * T + tt * 128:i * T + tt * 128 + 128],
                                kT[p0:p0 + 64, k * T:k * T + nk], start=False, stop=True)
            return f
        ali3 = r3(ali, T)
        self.att = cut(4096)
        units = []
        for tt, n in ((0, 8), (1, 4)):
            for h0 in range(0, 16, n):
                units.append(dict(
                    tt=tt, heads=list(range(h0, h0 + n)), nk=128 * (tt + 1), dv=64, scale=0.125, scores=scores(tt),
                    sink=R("sink")[:, h0:h0 + n], out=o[tt][:, h0 * 64:(h0 + n) * 64],
                    v=lambda j, k, h0=h0: qkv[k][:, 1280 + (h0 + j) // 4 * 64:1280 + (h0 + j) // 4 * 64 + 64]))
        done = self.attention(units, ready)
        ready = self.turn(lambda tt: o[tt], 8, done)
        self.add_moving("wo", ready, bias=R("bo"))

    def ssd(self):
        P, cut = self.P, self.scr.cut
        now = self.follow()
        rows = self.rows_load("ssd", "row_ssd", now)
        R = lambda n: self.row("ssd", n)
        B = self.bank
        V, A, G = self.v, self.a, self.g
        bands = self.rows[:, 640:640 + 8 * T]
        late = P.dma(self.d_late, lambda e: e.dma_start(bands, self.d["bands"]), now)
        h_at = self.scr.at
        ready = self.rms_turn("mix_norm0")
        turned = P.own("tensor")
        room = self.scr.t[:, h_at:h_at + 3 * D]
        xr, xd = [room[:, 0:D], room[:, D:2 * D]], room[:, 2 * D:3 * D]
        z = [cut(D) for _ in range(2)]
        cv = cut(12 * T)
        u_at = self.scr.at
        U = cut(12 * 260).rearrange("p (c t) -> p c t", t=260)
        u = cut(2 * D)
        sts = cut(D)
        z0 = V(lambda e: e.memset(U[:, :, 0:4], 0.0))
        conv = {}
        for f in range(6):
            bank = B[f % 4]
            tok = self.pair_product("ssd_xbc", bank, ready if f == 0 else None)
            t = A(lambda e, f=f, bank=bank: e.activation(U[:, 2 * f:2 * f + 2, 4:260], r3(bank.t[:, :], T), ACT.Copy), tok)
            bank.free = t
            for c in (2 * f, 2 * f + 1):
                out = cv[:, c * T:(c + 1) * T]
                V(lambda e, c=c, out=out: e.tensor_scalar(out, U[:, c, 4:260], self.vec("conv_w", 36 + c), None, ALU.mult),
                  t, z0)
                for k in (2, 1, 0):
                    t2 = V(lambda e, c=c, out=out, k=k: e.scalar_tensor_tensor(
                        out, U[:, c, 1 + k:257 + k], self.vec("conv_w", 12 * k + c), out, ALU.mult, ALU.add))
                conv[c] = A(lambda e, c=c, out=out: e.activation(out, out, ACT.Silu, bias=self.vec("conv_b", c)), t2)
        convolved = P.own("vector")
        dtr = [self.st[:, 0:16], self.st[:, 16:32]]

        def to_z(tt, n0, w, ps, tok):
            if n0 < D:
                return A(lambda e: e.activation(z[tt][:, n0:n0 + w], ps, ACT.Silu), tok)
            return V(lambda e: e.tensor_copy(dtr[tt], ps), tok)
        self.moving("ssd_z", D, D + 16, [(B[0], B[1]), (B[2], B[3])], to_z, None)
        xs = [self.scr.t[:, u_at + tt * D:u_at + (tt + 1) * D] for tt in range(2)]
        Bt, cb = (self.scr.t[:, u_at + 2 * D:u_at + 2 * D + 256], self.scr.t[:, u_at + 2 * D + 256:u_at + 2 * D + 768])
        us = [u[:, 0:D], u[:, D:2 * D]]
        banded = {}

        def pool():
            def to_u(tt, n0, w, ps, tok):
                if tt == 0:
                    return A(lambda e: e.activation(us[tt][:, n0:n0 + w], ps, ACT.Copy), tok)
                return V(lambda e: e.tensor_copy(us[tt][:, n0:n0 + w], ps), tok)
            yield from self.moving_steps("pool_in", D, D, [(B[0], B[1]), (B[2], B[3])], to_u, None)
            used = P.own("tensor")
            done = [B[i].free for i in range(4)]
            bnd = bands.rearrange("p (s w t) -> p s w t", s=2, w=4)
            toks = []
            for w in range(4):
                bank = B[w]

                def fn(e, w=w, bank=bank):
                    for c in range(2):
                        for s in range(2):
                            m = e.matmul(bank.t[:, c * T:(c + 1) * T],
                                         us[s][:, w * 256 + c * 128:w * 256 + (c + 1) * 128],
                                         bnd[:, s, w, :], start=(s == 0), stop=(s == 1))
                    return m
                t = banded["read"] = self.pe(fn, done, late, bank.free)
                sl = slice(w * 512, (w + 1) * 512)
                t = A(lambda e, sl=sl, bank=bank: e.activation(self.thi[:, sl], bank.t[:, :], ACT.Copy), t, used)
                t = V(lambda e, sl=sl, bank=bank: e.tensor_tensor(self.tlo[:, sl], bank.t[:, :],
                                                                  self.thi[:, sl].bitcast(F32), ALU.subtract), t)
                bank.free = t
                toks.append(t)
                yield

            def pools(e, hi, lo):
                for w in range(4):
                    for o_ in range(2):
                        out = B[w].t[:, o_ * T:(o_ + 1) * T]
                        for k in range(2):
                            ws = slice(((w * 2 + o_) * 2 + k) * 128, ((w * 2 + o_) * 2 + k + 1) * 128)
                            xs_ = slice((w * 2 + k) * T, (w * 2 + k + 1) * T)
                            e.matmul(out, hi[:, ws], self.thi[:, xs_], start=(k == 0), stop=False)
                            e.matmul(out, hi[:, ws], self.tlo[:, xs_], start=False, stop=False)
                            m = e.matmul(out, lo[:, ws], self.thi[:, xs_], start=False, stop=(k == 1))
                return m
            tok = self.chunk("pool_w", pools, toks, [b.free for b in B[0:4]])
            yield
            done = Turned()
            for w in range(4):
                for o_ in range(2):
                    k = 2 * w + o_
                    ps, sl = B[w].t[:, o_ * T:(o_ + 1) * T], slice(k * T, (k + 1) * T)
                    sc = self.vec("pool_scale", k)
                    t = A(lambda e, ps=ps, sl=sl, sc=sc: e.activation(self.thi[:, sl], ps, ACT.Copy, scale=sc), tok)
                for o_ in range(2):
                    k = 2 * w + o_
                    ps, sl = B[w].t[:, o_ * T:(o_ + 1) * T], slice(k * T, (k + 1) * T)
                    sc = self.vec("pool_scale", k)
                    t = V(lambda e, ps=ps, sl=sl, sc=sc: e.scalar_tensor_tensor(
                        self.tlo[:, sl], ps, sc, self.thi[:, sl].bitcast(F32), ALU.mult, ALU.subtract), t)
                B[w].free = t
                done.append(t)
                if w % 2:
                    yield
            yield from self.add_steps("out_pool", done)

        y = [cv[:, 0:D], cv[:, D:2 * D]]
        M = u

        def core():
            for n in range(4):
                bk = B[4 + n]
                tt, half = n // 2, n % 2

                def fn(e, tt=tt, half=half, bk=bk):
                    for j in range(4):
                        c = half * 4 + j
                        m = e.transpose(bk.t[:, j * 128:(j + 1) * 128], cv[:, c * T + tt * 128:c * T + tt * 128 + 128],
                                        self.ident)
                    return m
                t = self.pe(fn, bk.free, [conv[half * 4 + j] for j in range(4)])
                bk.free = A(lambda e, tt=tt, half=half, bk=bk: e.activation(
                    xs[tt][:, half * 512:half * 512 + 512], bk.t[:, :], ACT.Copy), t, convolved)
                if n % 2:
                    yield
            bk4 = B[4]

            def fb(e):
                for g in range(2):
                    m = e.transpose(bk4.t[:, g * 128:(g + 1) * 128], cv[:, (8 + g) * T:(8 + g) * T + 128], self.ident)
                return m
            t = self.pe(fb, bk4.free, conv[8], conv[9])
            bk4.free = A(lambda e: e.activation(Bt, bk4.t[:, 0:256], ACT.Copy), t)
            bk5 = B[5]

            def fcb(e):
                for tt in range(2):
                    for g in range(2):
                        m = e.matmul(bk5.t[:, (2 * tt + g) * 128:(2 * tt + g + 1) * 128],
                                     cv[:, (8 + g) * T + tt * 128:(8 + g) * T + tt * 128 + 128],
                                     cv[:, (10 + g) * T + tt * 128:(10 + g) * T + tt * 128 + 128], start=True, stop=True)
                return m
            t = self.pe(fcb, bk5.free, conv[10], conv[11])
            bk5.free = A(lambda e: e.activation(cb, bk5.t[:, :], ACT.Copy), t)
            byt = P.own("scalar")
            yield
            both, tmp, ea = self.st[:, 0:32], self.st[:, 32:64], self.st[:, 64:80]
            dt = dtr
            V(lambda e: e.tensor_tensor(r3(both, 16), r3(both, 16), bc(R("dtb"), 1, 2), ALU.add), rows)
            t = V(lambda e: e.tensor_scalar(tmp, both, 0.0, None, ALU.max))
            A(lambda e: e.activation(both, both, ACT.Abs), t)
            A(lambda e: e.activation(both, both, ACT.Exp, scale=-1.0))
            A(lambda e: e.activation(ea, R("alog"), ACT.Exp))
            t = A(lambda e: e.activation(both, both, ACT.Ln, bias=1.0))
            V(lambda e: e.tensor_tensor(both, both, tmp, ALU.add), t)
            V(lambda e: e.tensor_scalar(ea, ea, -1.0, None, ALU.mult))
            adt = self.st[:, 80:112]
            t = V(lambda e: e.tensor_tensor(r3(adt, 16), r3(both, 16), bc(ea, 1, 2), ALU.mult))
            yield
            bank = B[6]
            acs, dfs, dte = self.st[:, 112:144], self.st[:, 144:160], self.st[:, 160:176]

            def cums(e):
                e.matmul(bank.t[:, 0:16], self.tri, adt[:, 0:16], start=True, stop=True)
                e.matmul(bank.t[:, 16:32], self.tri, adt[:, 16:32], start=True, stop=True)
                return e.matmul(bank.t[:, 32:48], self.ones, adt[:, 0:16], start=True, stop=True)
            t = self.pe(cums, t, bank.free)
            V(lambda e: e.tensor_copy(acs, bank.t[:, 0:32]), t)
            bank.free = t = V(lambda e: e.tensor_tensor(dte, bank.t[:, 32:48], acs[:, 0:16], ALU.subtract))
            A(lambda e: e.activation(dte, dte, ACT.Exp), t)
            t_exp = A(lambda e: e.activation(dfs, acs[:, 16:32], ACT.Exp))
            for tt in range(2):
                V(lambda e, tt=tt: e.tensor_tensor(r3(xr[tt], 64), r3(xs[tt], 64), bc(dt[tt], 2, 64), ALU.mult),
                  byt, turned)
            xready = V(lambda e: e.tensor_tensor(r3(xd, 64), r3(xr[0], 64), bc(dte, 2, 64), ALU.mult), t_exp)
            yield
            for g in range(2):
                bk = B[6 + g]
                t = self.pe(lambda e, g=g, bk=bk: e.matmul(bk.t[:, :], Bt[:, g * 128:(g + 1) * 128],
                                                          xd[:, g * 512:(g + 1) * 512], start=True, stop=True),
                            xready, byt, bk.free)
                bk.free = A(lambda e, g=g, bk=bk: e.activation(sts[:, g * 512:(g + 1) * 512], bk.t[:, :], ACT.Copy), t)
            st_ready = P.own("scalar")
            yield
            ab = self.gb_
            mseg = self.c("mseg")
            mt, spent = {}, {}
            for tt in range(2):
                def quarter(tt, hb):
                    a = ab[:, hb * 512:(hb + 1) * 512]
                    t = V(lambda e: e.tensor_copy(r3(a, 128), bc(adt[:, tt * 16 + hb * 4:tt * 16 + hb * 4 + 4], 2, 128)),
                          self.abused.get(hb))
                    yield
                    bk = B[4 + hb]

                    def fn(e):
                        for j in range(4):
                            m = e.matmul(bk.t[:, j * 128:(j + 1) * 128], a[:, j * 128:(j + 1) * 128], self.tri,
                                         start=True, stop=True)
                        return m
                    t = self.pe(fn, t, bk.free)
                    self.abused[hb] = t
                    yield
                    m4 = M[:, hb * 512:(hb + 1) * 512]
                    m3 = r3(m4, 128)
                    t = V(lambda e: e.tensor_tensor(m3, r3(bk.t[:, :], 128),
                                                    bc(acs[:, tt * 16 + hb * 4:tt * 16 + hb * 4 + 4], 2, 128),
                                                    ALU.subtract), t, spent.get((tt - 1, hb // 2)), banded["read"])
                    bk.free = t
                    yield
                    t = G(lambda e: e.tensor_tensor(m3, m3, bc(mseg, 1, 4), ALU.add), t)
                    yield
                    t = A(lambda e: e.activation(m4, m4, ACT.Exp), t)
                    yield
                    g = hb // 2
                    mt[tt, hb] = V(lambda e: e.tensor_tensor(
                        m3, m3, bc(cb[:, (2 * tt + g) * 128:(2 * tt + g + 1) * 128], 1, 4), ALU.mult), t, byt)
                for i, _ in enumerate(woven([quarter(tt, hb) for hb in range(4)], 4)):
                    if i % 2:
                        yield
                for g in range(2):
                    def half(tt=tt, g=g):
                        bk = B[4 + g]

                        def fn(e):
                            for j in range(8):
                                h = g * 8 + j
                                m = e.matmul(bk.t[:, j * 64:(j + 1) * 64], M[:, h * 128:(h + 1) * 128],
                                             xr[tt][:, h * 64:(h + 1) * 64], start=True, stop=True)
                            return m
                        t = self.pe(fn, mt[tt, 2 * g], mt[tt, 2 * g + 1], xready, bk.free)
                        spent[tt, g] = t
                        yy = y[tt][:, g * 512:(g + 1) * 512]
                        x_ = xs[tt][:, g * 512:(g + 1) * 512]
                        V(lambda e: e.tensor_tensor(r3(yy, 64), r3(x_, 64), bc(R("dskip")[:, g * 8:g * 8 + 8], 2, 64),
                                                    ALU.mult))
                        bk.free = V(lambda e: e.tensor_tensor(yy, yy, bk.t[:, :], ALU.add), t)
                        if tt == 1:
                            b2 = B[6 + g]
                            t = self.pe(lambda e: e.matmul(b2.t[:, :], cv[:, (10 + g) * T + 128:(10 + g) * T + 256],
                                                           sts[:, g * 512:(g + 1) * 512], start=True, stop=True),
                                        st_ready, b2.free)
                            t = V(lambda e: e.tensor_tensor(r3(x_, 64), r3(b2.t[:, :], 64),
                                                            bc(dfs[:, g * 8:g * 8 + 8], 2, 64), ALU.mult), t)
                            b2.free = t
                            V(lambda e: e.tensor_tensor(yy, yy, x_, ALU.add))
                        return V(lambda e: e.tensor_tensor(yy, yy, z[tt][:, g * 512:(g + 1) * 512], ALU.mult))
                    half()
                    yield
        interleave([pool(), core()], 2)
        self.junk = M[:, 0:512]
        t = [P.own("vector"), P.own("tensor")]
        done = []
        for tt in range(2):
            def one(tt=tt):
                r, t2 = self.rms_rows(y[tt], 2, 512, 1e-6, t, col=176 + 8 * tt)
                return V(lambda e: e.tensor_tensor(r3(y[tt], 512), r3(y[tt], 512), bc(r, 2, 512), ALU.mult), t2)
            done.append(one())
        ready = self.turn(lambda tt: y[tt], 8, done, scale=lambda k: self.vec("ssd_norm", k))
        self.add_moving("out_ssd", ready)


def program(nc, d, out, upto=99):
    with ExitStack() as ctx:
        K = Kernel(nc, ctx, d)
        P = K.P
        K.small = ctx.enter_context(nc.sbuf_tensor("small", [128, 100], F32))
        K.abused, K.xdone = {}, [None, None]
        K.flag = K.small[:, 96:97].bitcast(I32)
        K.begin_program()
        steps = []
        for l in range(DEPTH):
            steps += [lambda l=l: K.mixer(l), lambda l=l: K.moe(l)]
        steps += [K.ssd, lambda: K.cross(0),
                  lambda: K.ffn("ffn20", "ffn2_norm0"), lambda: K.ffn("ffn11", "ffn1_norm1"), K.swa,
                  lambda: K.cross(1), lambda: K.ffn("ffn21", "ffn2_norm1")]
        for step in steps[:upto]:
            step()
        now = P.meet()
        for tt in range(2):
            last = P.dma(K.d_out, lambda e, tt=tt: e.dma_start(out[tt * 128:(tt + 1) * 128, :], K.x(tt)), now)
        P.gate["sync"] = []
        with nc.Block() as block:
            P.emit(block, last)




def kernel(**inputs):
    from concourse import bacc
    from concourse.bass_utils import run_bass_kernel_spmd

    i = {k: np.asarray(v) for k, v in inputs.items()}
    arrays = {**pack_weights(i), **pack_small(i)}
    nc = bacc.Bacc("TRN2", target_bir_lowering=False, num_devices=1)
    d = {n: nc.dram_tensor("in_" + n, a.shape, mybir.dt.from_np(a.dtype), kind="ExternalInput").ap()
         for n, a in arrays.items()}
    out = nc.dram_tensor("out_x", (T, D), F32, kind="ExternalOutput").ap()
    program(nc, d, out)
    r = run_bass_kernel_spmd(nc, [{"in_" + n: a for n, a in arrays.items()}], core_ids=[0])
    return r.results[0]["out_x"].reshape(1, T, D)
```
